# Optimizing a Trainium2 kernel written in Bass

```python
import jax
import jax.numpy as jnp
from jax import lax
import numpy as np

D_MODEL = 1024
BATCH = 1
SEQ = 256
DEPTH = 2

D_FF = 2816
NORM_EPS = 1e-6
N_BRANCH = 3

RW_HEADS = 8
RW_HEAD_DIM = 64
RW_WIDTH = RW_HEADS * RW_HEAD_DIM
RW_DECAY_RANK = 64
RW_ICL_RANK = 64
RW_VRES_RANK = 32
RW_GATE_RANK = 128
RW_GN_EPS = 64e-5

CV_CHANNELS = 512
CONV_TAPS = 31
CV_LN_EPS = 1e-5

MLA_HEADS = 8
MLA_Q_RANK = 384
MLA_KV_RANK = 256
MLA_NOPE = 64
MLA_ROPE = 32
MLA_QK = MLA_NOPE + MLA_ROPE
MLA_V = 64
ROPE_THETA = 10000.0
Q_BLOCK = 128

RW_COLS = 3 * RW_WIDTH + 2 * RW_DECAY_RANK + 2 * RW_ICL_RANK + RW_GATE_RANK
CV_COLS = 2 * CV_CHANNELS
MLA_COLS = MLA_Q_RANK + MLA_KV_RANK + MLA_ROPE
GATE_COLS = N_BRANCH * D_MODEL
N_IN = RW_COLS + CV_COLS + MLA_COLS + GATE_COLS

kernel_name = 'hybrid_rwkv7_conformer_mla_encoder'

def rms_norm(x, g, eps=NORM_EPS):
    xf = x.astype(jnp.float32)
    y = xf * lax.rsqrt(jnp.mean(xf * xf, axis=-1, keepdims=True) + eps)
    return (y * g.astype(jnp.float32)).astype(x.dtype)

def layer_norm(x, g, b, eps):
    xf = x.astype(jnp.float32)
    mu = jnp.mean(xf, axis=-1, keepdims=True)
    xc = xf - mu
    var = jnp.mean(xc * xc, axis=-1, keepdims=True)
    y = xc * lax.rsqrt(var + eps) * g.astype(jnp.float32) + b.astype(jnp.float32)
    return y.astype(x.dtype)

def swiglu(x, w1, w3, w2):
    return (jax.nn.silu(x @ w1) * (x @ w3)) @ w2

def centred_shift_mix(p, mu):
    prev = jnp.pad(p[:, :-1], ((0, 0), (1, 0), (0, 0)))
    nxt = jnp.pad(p[:, 1:], ((0, 0), (0, 1), (0, 0)))
    return p + (0.5 * (prev + nxt) - p) * mu

def rwkv7_bidir_scan(r, w, k, v, a, b):
    def to_time_major(t):
        t = jnp.concatenate([t[:1], jnp.flip(t[1:], axis=2)], axis=0)
        return jnp.moveaxis(t, 2, 0)

    def step(state, inp):
        r_t, w_t, k_t, v_t, a_t, b_t = inp
        sa = jnp.einsum('dbhvk,dbhk->dbhv', state, a_t)
        state = (state * w_t[..., None, :] + sa[..., :, None] * b_t[..., None, :]
                 + v_t[..., :, None] * k_t[..., None, :])
        return state, jnp.einsum('dbhvk,dbhk->dbhv', state, r_t)

    xs = tuple(to_time_major(t) for t in (r, w, k, v, a, b))
    s0 = jnp.zeros(xs[0].shape[1:] + (RW_HEAD_DIM,), jnp.float32)
    _, out = lax.scan(step, s0, xs)
    out = jnp.moveaxis(out, 0, 2)
    return out[0] + jnp.flip(out[1], axis=1)

def rwkv7_branch(p, h, v_first, vres, mu, w0, w_up, a0, a_up, g_up, k_k, k_a, r_k,
                 gn_g, gn_b, w_branch):
    B, S, _ = p.shape
    H, N, C = RW_HEADS, RW_HEAD_DIM, RW_WIDTH
    p = centred_shift_mix(p, mu)
    o1 = 3 * C + 2 * RW_DECAY_RANK
    r, k, v, wd, ad, gd = jnp.split(p, [C, 2 * C, 3 * C, o1, o1 + 2 * RW_ICL_RANK], axis=-1)
    wd = jnp.tanh(wd.reshape(B, S, 2, RW_DECAY_RANK))
    ad = ad.reshape(B, S, 2, RW_ICL_RANK)
    w_log = -jax.nn.softplus(-(w0 + jnp.einsum('bsdr,drc->bsdc', wd, w_up)).astype(jnp.float32)) - 0.5
    decay = jnp.exp(-jnp.exp(w_log))
    icl = jax.nn.sigmoid((a0 + jnp.einsum('bsdr,drc->bsdc', ad, a_up)).astype(jnp.float32))
    g = jax.nn.sigmoid(gd) @ g_up
    if vres is None:
        v_first = v
    else:
        v0, v_down, v_up = vres
        nu = jax.nn.sigmoid(v0 + (h @ v_down) @ v_up)
        v = v + (v_first - v) * nu
    rf, kf, vf = (t.astype(jnp.float32) for t in (r, k, v))
    kk = (kf * k_k).reshape(B, S, H, N)
    kk = kk / jnp.maximum(jnp.linalg.norm(kk, axis=-1, keepdims=True), 1e-12)
    kk = kk.reshape(B, S, 1, C)
    k_dir = kf[:, :, None] * (1.0 + (icl - 1.0) * k_a)

    def heads(t):
        t = jnp.broadcast_to(t, (B, S, 2, C)).reshape(B, S, 2, H, N)
        return jnp.moveaxis(t, 2, 0)

    o = rwkv7_bidir_scan(heads(rf[:, :, None]), heads(decay), heads(k_dir),
                         heads(vf[:, :, None]), heads(-kk), heads(kk * icl))
    o = layer_norm(o, gn_g.reshape(H, N), gn_b.reshape(H, N), RW_GN_EPS)
    k_bonus = jnp.mean(k_dir, axis=2).reshape(B, S, H, N)
    bonus = jnp.sum(rf.reshape(B, S, H, N) * k_bonus * r_k, axis=-1, keepdims=True) * vf.reshape(B, S, H, N)
    o = (o + bonus).reshape(B, S, C).astype(h.dtype)
    return (o * g) @ w_branch, v_first

def conformer_conv_branch(p, dw_w, dw_b, ln_g, ln_b, w_branch):
    val, gate = jnp.split(p, 2, axis=-1)
    u = val * jax.nn.sigmoid(gate)
    half = CONV_TAPS // 2
    u = lax.conv_general_dilated(u, dw_w[:, None, :].astype(u.dtype), window_strides=(1,),
                                 padding=[(half, half)], dimension_numbers=('NWC', 'WIO', 'NWC'),
                                 feature_group_count=CV_CHANNELS) + dw_b
    u = jax.nn.silu(layer_norm(u, ln_g, ln_b, CV_LN_EPS))
    return u @ w_branch

def rope_angles(positions):
    inv = ROPE_THETA ** (-jnp.arange(0, MLA_ROPE, 2, dtype=jnp.float32) / MLA_ROPE)
    ang = positions.astype(jnp.float32)[..., None] * inv
    return jnp.cos(ang)[:, :, None, :], jnp.sin(ang)[:, :, None, :]

def apply_rope_tail(t, cos, sin):
    nope = t[..., :MLA_NOPE]
    rot = t[..., MLA_NOPE:].astype(jnp.float32)
    half = MLA_ROPE // 2
    x1, x2 = rot[..., :half], rot[..., half:]
    rot = jnp.concatenate([x1 * cos - x2 * sin, x2 * cos + x1 * sin], axis=-1)
    return jnp.concatenate([nope, rot.astype(t.dtype)], axis=-1)

def blocked_attention(q, k, v):
    B, S, H, Dq = q.shape
    nb = S // Q_BLOCK
    scale = Dq ** -0.5
    qb = jnp.moveaxis(q.reshape(B, nb, Q_BLOCK, H, Dq), 1, 0)

    def attend(q_blk):
        s = jnp.einsum('bqhd,bkhd->bhqk', q_blk, k).astype(jnp.float32) * scale
        pr = jax.nn.softmax(s, axis=-1).astype(v.dtype)
        return jnp.einsum('bhqk,bkhd->bqhd', pr, v)

    o = lax.map(attend, qb)
    return jnp.moveaxis(o, 0, 1).reshape(B, S, H, v.shape[-1])

def mla_branch(p, cos, sin, q_norm, w_uq, kv_norm, w_ukv, qk_q_g, qk_k_g, w_branch):
    B, S, _ = p.shape
    H = MLA_HEADS
    cq, ckv, k_rope = jnp.split(p, [MLA_Q_RANK, MLA_Q_RANK + MLA_KV_RANK], axis=-1)
    q = (rms_norm(cq, q_norm) @ w_uq).reshape(B, S, H, MLA_QK)
    kv = (rms_norm(ckv, kv_norm) @ w_ukv).reshape(B, S, H, MLA_NOPE + MLA_V)
    k_nope, v = kv[..., :MLA_NOPE], kv[..., MLA_NOPE:]
    k = jnp.concatenate([k_nope, jnp.broadcast_to(k_rope[:, :, None], (B, S, H, MLA_ROPE))], axis=-1)
    q = apply_rope_tail(rms_norm(q, qk_q_g), cos, sin)
    k = apply_rope_tail(rms_norm(k, qk_k_g), cos, sin)
    o = blocked_attention(q, k, v)
    return o.reshape(B, S, H * MLA_V) @ w_branch

def setup_inputs(seed: int = 0) -> dict:
    key = jax.random.key(seed)
    ks = iter(jax.random.split(key, 64))
    L = DEPTH

    def nrm(shape, scale):
        return jax.random.normal(next(ks), shape, jnp.float32) * scale

    def gain(shape):
        return 1.0 + nrm(shape, 0.02)

    D, F = D_MODEL, D_FF
    x = jax.random.normal(next(ks), (BATCH, SEQ, D), jnp.float32)
    positions = (jnp.arange(SEQ, dtype=jnp.int32)[None, :]
                 + jax.random.randint(next(ks), (BATCH, 1), 0, 1024, dtype=jnp.int32))
    return {
        'x': x,
        'positions': positions,
        'norm_ffn1': gain((L, D)),
        'ffn1_w1': nrm((L, D, F), D ** -0.5),
        'ffn1_w3': nrm((L, D, F), D ** -0.5),
        'ffn1_w2': nrm((L, F, D), F ** -0.5),
        'norm_mix': gain((L, D)),
        'w_in': nrm((L, D, N_IN), D ** -0.5),
        'rw_mu': jax.random.uniform(next(ks), (L, RW_COLS), jnp.float32),
        'rw_w0': jax.random.uniform(next(ks), (L, 2, RW_WIDTH), jnp.float32, -4.0, 0.0),
        'rw_w_up': nrm((L, 2, RW_DECAY_RANK, RW_WIDTH), 0.1),
        'rw_a0': nrm((L, 2, RW_WIDTH), 0.1),
        'rw_a_up': nrm((L, 2, RW_ICL_RANK, RW_WIDTH), 0.1),
        'rw_g_up': nrm((L, RW_GATE_RANK, RW_WIDTH), RW_GATE_RANK ** -0.5),
        'rw_k_k': 0.85 + nrm((L, RW_WIDTH), 0.05),
        'rw_k_a': 1.0 + nrm((L, RW_WIDTH), 0.05),
        'rw_r_k': nrm((L, RW_HEADS, RW_HEAD_DIM), 0.1),
        'rw_v0': nrm((L - 1, RW_WIDTH), 0.1),
        'rw_v_down': nrm((L - 1, D, RW_VRES_RANK), D ** -0.5),
        'rw_v_up': nrm((L - 1, RW_VRES_RANK, RW_WIDTH), RW_VRES_RANK ** -0.5),
        'rw_gn_g': gain((L, RW_WIDTH)),
        'rw_gn_b': nrm((L, RW_WIDTH), 0.02),
        'rw_w_branch': nrm((L, RW_WIDTH, D), RW_WIDTH ** -0.5),
        'cv_dw_w': nrm((L, CONV_TAPS, CV_CHANNELS), CONV_TAPS ** -0.5),
        'cv_dw_b': nrm((L, CV_CHANNELS), 0.02),
        'cv_ln_g': gain((L, CV_CHANNELS)),
        'cv_ln_b': nrm((L, CV_CHANNELS), 0.02),
        'cv_w_branch': nrm((L, CV_CHANNELS, D), CV_CHANNELS ** -0.5),
        'mla_q_norm': gain((L, MLA_Q_RANK)),
        'mla_w_uq': nrm((L, MLA_Q_RANK, MLA_HEADS * MLA_QK), MLA_Q_RANK ** -0.5),
        'mla_kv_norm': gain((L, MLA_KV_RANK)),
        'mla_w_ukv': nrm((L, MLA_KV_RANK, MLA_HEADS * (MLA_NOPE + MLA_V)), MLA_KV_RANK ** -0.5),
        'mla_qk_q_g': gain((L, MLA_QK)),
        'mla_qk_k_g': gain((L, MLA_QK)),
        'mla_w_branch': nrm((L, MLA_HEADS * MLA_V, D), (MLA_HEADS * MLA_V) ** -0.5),
        'w_o': nrm((L, D, D), D ** -0.5),
        'norm_ffn2': gain((L, D)),
        'ffn2_w1': nrm((L, D, F), D ** -0.5),
        'ffn2_w3': nrm((L, D, F), D ** -0.5),
        'ffn2_w2': nrm((L, F, D), F ** -0.5),
    }

def reference(x, positions,
              norm_ffn1, ffn1_w1, ffn1_w3, ffn1_w2,
              norm_mix, w_in,
              rw_mu, rw_w0, rw_w_up, rw_a0, rw_a_up, rw_g_up, rw_k_k, rw_k_a, rw_r_k,
              rw_v0, rw_v_down, rw_v_up, rw_gn_g, rw_gn_b, rw_w_branch,
              cv_dw_w, cv_dw_b, cv_ln_g, cv_ln_b, cv_w_branch,
              mla_q_norm, mla_w_uq, mla_kv_norm, mla_w_ukv, mla_qk_q_g, mla_qk_k_g, mla_w_branch,
              w_o,
              norm_ffn2, ffn2_w1, ffn2_w3, ffn2_w2):
    B, S, D = x.shape
    cos, sin = rope_angles(positions)
    splits = [RW_COLS, RW_COLS + CV_COLS, RW_COLS + CV_COLS + MLA_COLS]
    v_first = None
    for i in range(DEPTH):
        x = x + 0.5 * swiglu(rms_norm(x, norm_ffn1[i]), ffn1_w1[i], ffn1_w3[i], ffn1_w2[i])
        h = rms_norm(x, norm_mix[i])
        proj = h @ w_in[i]
        p_rw, p_cv, p_mla, p_gate = jnp.split(proj, splits, axis=-1)
        vres = None if i == 0 else (rw_v0[i - 1], rw_v_down[i - 1], rw_v_up[i - 1])
        y_rw, v_first = rwkv7_branch(p_rw, h, v_first, vres, rw_mu[i], rw_w0[i], rw_w_up[i],
                                     rw_a0[i], rw_a_up[i], rw_g_up[i], rw_k_k[i], rw_k_a[i],
                                     rw_r_k[i], rw_gn_g[i], rw_gn_b[i], rw_w_branch[i])
        y_cv = conformer_conv_branch(p_cv, cv_dw_w[i], cv_dw_b[i], cv_ln_g[i], cv_ln_b[i],
                                     cv_w_branch[i])
        y_mla = mla_branch(p_mla, cos, sin, mla_q_norm[i], mla_w_uq[i], mla_kv_norm[i],
                           mla_w_ukv[i], mla_qk_q_g[i], mla_qk_k_g[i], mla_w_branch[i])
        gates = jax.nn.sigmoid(p_gate).reshape(B, S, N_BRANCH, D)
        merged = gates[:, :, 0] * y_rw + gates[:, :, 1] * y_cv + gates[:, :, 2] * y_mla
        x = x + merged @ w_o[i]
        x = x + 0.5 * swiglu(rms_norm(x, norm_ffn2[i]), ffn2_w1[i], ffn2_w3[i], ffn2_w2[i])
    return x


_drawn_inputs = setup_inputs


def setup_inputs(seed=0):
    import zlib

    import numpy as np

    out = dict(_drawn_inputs(seed))
    spreads = {}
    factors = {'norm_ffn1': 4.245,
     'norm_mix': 3.114,
     'rw_a0': 3.82,
     'rw_k_k': 5.694,
     'rw_k_a': 2.671,
     'rw_v0': 6.962,
     'rw_gn_g': 8.0,
     'rw_gn_b': 6.997,
     'cv_dw_b': 3.376,
     'cv_ln_g': 5.386,
     'cv_ln_b': 6.257,
     'mla_q_norm': 8.0,
     'mla_kv_norm': 8.0,
     'mla_qk_q_g': 8.0,
     'mla_qk_k_g': 8.0,
     'norm_ffn2': 5.391}
    for name, (base, spread) in spreads.items():
        noise = np.random.default_rng([zlib.crc32(name.encode()), seed]).standard_normal(out[name].shape)
        drawn = base * np.exp(spread * noise) if base else spread * noise
        out[name] = jnp.asarray(drawn.astype(out[name].dtype))
    for name, factor in factors.items():
        out[name] = (out[name] * factor).astype(out[name].dtype)
    return out
```

```python
import numpy as np
from contextlib import ExitStack
import concourse.bass as bass
import concourse.mybir as mybir

F = mybir.dt.float32
R = mybir.dt.float32r
BF = mybir.dt.bfloat16
ALU = mybir.AluOpType
ACT = mybir.ActivationFunctionType
AX = mybir.AxisListType

P = 128
D = 1024
S = 256
DEPTH = 2
FF = 2816
KC = D // P
NFF = FF // P
NT = S // P
C = 64
NCH = S // C
H = 8
HD = 64
RW = H * HD
RC = RW // P
CV = 512
TAPS = 31
HALF = TAPS // 2
QR, KVR, ROPE, NOPE = 384, 256, 32, 64
QK = NOPE + ROPE
QC, KVC = QR // P, KVR // P
NORM_EPS, GN_EPS, LN_EPS = 1e-6, 64e-5, 1e-5
DECAY = float(np.exp(-0.5))
SCALE = float(QK) ** -0.5
LEVELS = 6

N_RW, N_VD, N_MLA, N_CV = 15, 1, 6, 8
T_FFN1 = 0
T_RW = T_FFN1 + 3 * NFF
T_VD = T_RW + N_RW
T_MLA = T_VD + N_VD
T_CV = T_MLA + N_MLA
T_BR = T_CV + N_CV
T_WO = T_BR + 3 * (RC + KC)
T_FFN2 = T_WO + KC
T_END = T_FFN2 + 3 * NFF
RAW, HL = 6, 3
TILES = -(-T_END // RAW) * RAW
BRANCH_ORDER = (2, 1, 0)
RW_COLS, CV_COLS, MLA_COLS = 1920, 1024, 672

VEC = {}
NV = 0
for _name, _n in (("norm_ffn1", KC), ("norm_mix", KC), ("norm_ffn2", KC), ("mu", N_RW), ("w0", 2 * RC),
                  ("a0", 2 * RC), ("k_k", RC), ("k_a", RC), ("r_k", RC), ("v0", RC), ("gn_g", RC),
                  ("gn_b", RC), ("cv_b", RC), ("ln_g", RC), ("ln_b", RC), ("q_norm", QC),
                  ("kv_norm", KVC), ("qk_q_g", 1), ("qk_k_g", 1), ("cv_w", RC * TAPS), ("keep", 1),
                  ("first", 1)):
    VEC[_name] = NV
    NV += _n

CST = {}
NC = 0
for _name, _n in (("ident", P), ("ones", P), ("mean64", P), ("ident64", C), ("rot", QK), ("es", RC * H),
                  ("eb", RC * P), ("e96", H * H), ("b96", H * QK), ("scan", 2 * S), ("freq", 1), ("eps", 4)):
    CST[_name] = NC
    NC += _n
M1, LEV = 4 * P, 8 * P
NM = LEV + 2 * (LEVELS - 1) * P
MAGIC = 1.5 * 2.0 ** 23
PI_IN = float(np.nextafter(np.float32(np.pi), np.float32(0)))


def two_pi_parts(n=4, bits=9):
    rest, parts = 2 * np.pi, []
    for _ in range(n):
        q = 2.0 ** (np.floor(np.log2(rest)) - bits + 1)
        parts.append(float(np.floor(rest / q) * q))
        rest -= parts[-1]
    return parts + [float(np.float32(rest))]


TWO_PI = two_pi_parts()
ROPE_STEPS = 4 + len(TWO_PI) + 3 + 2


def constants():
    c = np.zeros((P, NC), np.float32)

    def put(name, a):
        a = np.asarray(a, np.float32).reshape(a.shape[0], -1)
        c[:a.shape[0], CST[name]:CST[name] + a.shape[1]] = a

    i = np.arange(P)
    put("ident", np.eye(P))
    put("ones", np.ones((P, P)))
    put("mean64", (i[:, None] // HD == i[None] // HD) / HD)
    put("ident64", np.tile(np.eye(C), (2, 1)))
    rot = np.zeros((QK, QK))
    for m in range(ROPE // 2):
        rot[NOPE + ROPE // 2 + m, NOPE + m] = -1.0
        rot[NOPE + m, NOPE + ROPE // 2 + m] = 1.0
    put("rot", rot)
    es = np.zeros((P, RC, H))
    eb = np.zeros((H, RC, P))
    for j in range(RC):
        for p in range(P):
            es[p, j, 2 * j + p // HD] = 1
            eb[2 * j + p // HD, j, p] = 1
    put("es", es)
    put("eb", eb)
    e96 = np.zeros((QK, H, H))
    b96 = np.zeros((H, H, QK))
    for h in range(H):
        e96[:, h, h] = 1
        b96[h, h, :] = 1
    put("e96", e96)
    put("b96", b96)
    same = i[:, None] // C == i[None] // C
    lt = i[:, None] < i[None]
    tm = np.zeros((P, 2, 2, P))
    for d, m in enumerate((lt, lt.T)):
        tm[:, d, 0] = same & m
        tm[:, d, 1] = same & (m | np.eye(P, dtype=bool))
    
    m1 = np.zeros((P, 2, 2, P))
    lev = np.zeros((P, 2, LEVELS - 1, P))
    for n in range(LEVELS):
        h = 2 ** n
        block = (i[:, None] // (2 * h) == i[None] // (2 * h)) & (i[:, None] // h > i[None] // h)
        for d, m in enumerate((block, block.T)):
            if n == 0:
                m1[:, d, 0], m1[:, d, 1] = -1.0 * m, -1.0 * m.T
            else:
                lev[:, d, n - 1] = m
    masks = np.concatenate([v.reshape(P, -1) for v in (tm, m1, lev)], 1).astype(np.float32)
    sc = np.ones((P, 2, S))
    sc[:, 0, ::C] = 0
    sc[:, 1, C - 1::C] = 0
    put("scan", sc)
    freq = 10000.0 ** (-np.arange(0, ROPE, 2) / ROPE)
    f = np.zeros((P, 1))
    f[NOPE:QK, 0] = np.tile(freq, 2)
    put("freq", f)
    put("eps", np.tile(np.array([NORM_EPS, GN_EPS, LN_EPS, 0.0]), (P, 1)))
    return c, masks


class Steps:

    def __init__(self, sem, name, known):
        self.sem, self.name, self.known = sem, name, known
        self.now, self.n, self.layer = {}, 0, 0

    def mark(self, key):
        self.n += 1
        assert key not in self.now, key
        self.now[key] = self.n
        return self.sem, 1

    def at(self, key):
        if self.known is None:
            return self.sem, 1
        total, values = self.known[self.name]
        return self.sem, self.layer * total + values[key]

    def counted(self):
        return self.n, self.now


def program(nc, x, pos, stream, vecs, cst_in, msk_in, lora, wuq_in, wukv_in, out, known):
    ctx = ExitStack()
    with ctx:
        def sb(name, shape, dt=F):
            return ctx.enter_context(nc.sbuf_tensor(name, shape, dt))

        def sem(name):
            return ctx.enter_context(nc.semaphore(name))

        xT = sb("xT", [P, KC, S])
        h_hi = sb("h_hi", [P, KC, S], R)
        h_lo = sb("h_lo", [P, KC, S], R)
        raw = sb("raw", [P, RAW, D])
        whi = sb("whi", [P, HL, D], R)
        wlo = sb("wlo", [P, HL, D], R)
        u_hi = sb("u_hi", [P, RC, S], R)
        u_lo = sb("u_lo", [P, RC, S], R)
        g_hi, g_lo = u_hi[:, 0:2, :], u_lo[:, 0:2, :]
        gs = sb("gs", [P, 2, S])
        msk = sb("masks", [P, NM], BF)
        cst = sb("consts", [P, NC])
        vec_t = sb("vec_t", [P, NV])
        lo_w = sb("lo_w", [P, 4, RW])
        zero_b = sb("zero_b", [1, 512], BF)
        vfirst = sb("vfirst", [P, RC, S])
        cosT = sb("cosT", [P, S])
        sinT = sb("sinT", [P, S])
        ARENA = 24400
        arena = sb("arena", [P, ARENA])
        bank = [ctx.enter_context(nc.psum_tensor(f"bank{i}", [P, 512], F)) for i in range(8)]

        def view(at, *shape):
            n = int(np.prod(shape))
            assert at + n <= ARENA, (at, shape)
            v = arena[:, at:at + n]
            if len(shape) == 2:
                v = v.rearrange("p (a b) -> p a b", b=shape[1])
            elif len(shape) == 3:
                v = v.rearrange("p (a b c) -> p a b c", b=shape[1], c=shape[2])
            elif len(shape) == 4:
                v = v.rearrange("p (a b c d) -> p a b c d", b=shape[1], c=shape[2], d=shape[3])
            return v

        Q1 = RC * S
        r_, k_, v_ = view(0, RC, S), view(Q1, RC, S), view(2 * Q1, RC, S)
        wag = view(3 * Q1, 4, S)
        merged = view(4 * Q1, KC, S)
        M0 = 6 * Q1
        g_s, g_f = view(0, 2, S), view(2 * S, 2, S)
        ang = view(S, 4, S)
        sq = view(M0, KC, S)
        lat = view(M0, QC + KVC, S)
        rope_in = view(M0 + 5 * S, S)
        UP0 = M0 + 6 * S
        upad = view(UP0, RC, S + TAPS - 1)
        CVO = UP0 + RC * (S + TAPS - 1)
        cvo = view(CVO, RC, S)
        MB = CVO + Q1
        pp = view(MB, 2, 4, S + 2)
        pt = view(MB + 8 * (S + 2), 4, S)
        nrm = view(MB + 4 * Q1, 2, S)
        sq_lat = view(MB + 5 * Q1, QC + KVC, S)
        qf = view(MB, H, S)
        kf = view(MB + 2 * Q1, H, S)
        hs = view(MB + 4 * Q1, H, S)
        vm = view(MB + 6 * Q1, NT, RW)
        prob = view(MB + 4 * Q1, 2, 2, S)
        probT = view(MB + 5 * Q1, 2, 2, S)
        rn8 = view(MB + 7 * Q1, 2, S)
        wuq = view(MB + 7 * Q1 + 2 * S, QC, H * QK)
        W2 = MB + 7 * Q1 + 2 * S + QC * H * QK
        wukv = view(W2, KVC, H * (NOPE + 64))
        mx = view(W2 + 2048, 2, 4)
        cv_tmp = view(W2 + 2048 + 8, 2, S)
        cv_sq = view(MB, RC, S)
        cv_st = view(MB + Q1, 3, S)
        kk = view(M0, RC, S)
        kds = view(M0 + Q1, RC, S)
        osum = view(M0 + 2 * Q1, RC, S)
        vt = view(M0 + 3 * Q1, NT, RW)
        kr = view(M0 + 4 * Q1, RC, NT, 2, P)
        bt = view(M0 + 6 * Q1, RC, S)
        kt = view(M0 + 7 * Q1, RC, S)
        tk = view(M0 + 8 * Q1, 3, NT, RW)
        ptr = view(M0 + 11 * Q1, RC, NCH, C)
        qw = view(M0 + 12 * Q1, RC, NCH, HD)
        G0 = M0 + 13 * Q1
        wch = view(G0, RC, NCH)
        G1 = G0 + RC * NCH
        tA, tB, tC_, tD = (view(G1 + i * Q1, RC, S) for i in range(4))
        g1 = view(G1, 2, NT, 2, P)
        g2 = view(G1 + Q1, 2, NT, 2, P)
        mn = view(G1 + 2 * Q1, 2, 2, NT, P)
        zz = view(G1 + 3 * Q1, 2, NT, P)
        xs = view(G1 + 3 * Q1 + 512, 2, NT, HD)
        ys = view(G1 + 3 * Q1 + 768, 2, NT, HD)
        gv = view(G1 + 4 * Q1, 2, NT, HD)
        rn_rw = view(G1 + 4 * Q1 + 256, 2, S)
        tmp_s = view(G1, RC, HD)

        def cc(name, n, at=0, rows=P):
            o = CST[name] + at
            return cst[0:rows, o:o + n]

        def vv(name, i=0, a=0, b=P):
            o = VEC[name] + i
            return vec_t[a:b, o:o + 1]

        ident = cc("ident", P)

        raw_in = [sem(f"raw_in{i}") for i in range(RAW)]
        hi_ready = sem("hi_ready")
        lo_ready = sem("lo_ready")
        tile_used = sem("tile_used")
        consts_in = sem("consts_in")
        masks_in = sem("masks_in")
        x_in = sem("x_in")
        x_ready = sem("x_ready")
        vec_in = sem("vec_in")
        lora_in = sem("lora_in")
        uk_in = sem("uk_in")
        zeros_set = sem("zeros_set")
        rope_v, rope_a = sem("rope_v"), sem("rope_a")
        sig_ready = sem("sig_ready")
        as_ready = sem("as_ready")
        g_ready = sem("g_ready")
        ghi_ready = sem("ghi_ready")
        glo_ready = sem("glo_ready")
        vec = Steps(sem("vector_step"), "vec", known)
        act = Steps(sem("scalar_step"), "act", known)
        ten = Steps(sem("tensor_step"), "ten", known)
        poo = Steps(sem("pool_step"), "poo", known)
        out_done = sem("out_done")

        def need(eng, *events):
            for s, value in events:
                eng.wait_ge(s, value)

        settles = sem("settles")

        def settled(eng):
            eng.sem_inc(settles, 1)

        def layers(eng):
            loop = eng.Fori(0, DEPTH)
            L = loop.__enter__()
            for steps in (vec, act, ten, poo):
                steps.layer = L
            return loop, L

        block = ctx.enter_context(nc.Block())

        @block.sync
        def _(sp):
            def load(tile, s, n):
                sp.wait_ge(lo_ready, n + 1)
                sp.dma_start(raw[:, s, :], tile).then_inc(raw_in[s], 16)

            with sp.Fori(0, DEPTH * TILES // RAW) as g:
                for s in range(RAW):
                    load(stream[g * RAW + s], s, g * RAW + s)
            for s in range(HL):
                load(stream[DEPTH * TILES + s], s, DEPTH * TILES + s)
            need(sp, (vec.sem, 1) if known is None else (vec.sem, DEPTH * known["vec"][0]))
            sp.dma_start(out, xT[:, :, :]).then_inc(out_done, 16)
            sp.wait_ge(out_done, 16)

        @block.gpsimd
        def _(pool):
            pool.dma_start(cst[:, :], cst_in).then_inc(consts_in, 16)
            pool.dma_start(arena[:, 2048:2048 + NM], msk_in).then_inc(masks_in, 16)
            pool.dma_start(xT[:, :, :], x).then_inc(x_in, 16)
            pool.dma_start(vec_t[:, :], vecs[0]).then_inc(vec_in, 16)
            pool.dma_start(lo_w[:, :, :], lora[0]).then_inc(lora_in, 16)
            pool.dma_start(wuq, wuq_in[0]).then_inc(uk_in, 16)
            pool.dma_start(wukv, wukv_in[0]).then_inc(uk_in, 16)
            pool.dma_start(arena[:, 0:S].bitcast(mybir.dt.int32), pos).then_inc(x_in, 16)
            nc.gpsimd.memset(vfirst[:, :, :], 0.0).then_inc(zeros_set, 1)
            nc.gpsimd.memset(zero_b[:, :], 0.0).then_inc(zeros_set, 1)
            loop, L = layers(pool)
            need(pool, vec.at(("h lo", 1, KC - 1)))
            settled(pool)
            nc.gpsimd.memset(upad[:, :, 0:HALF], 0.0).then_inc(*poo.mark("pad left"))
            nc.gpsimd.memset(upad[:, :, HALF + S:], 0.0).then_inc(*poo.mark("pad right"))
            for c in range(2, 4):
                need(pool, vec.at(("glu", c)))
                if c == 2:
                    pool.wait_ge(vec_in, L * 16 + 16)
                settled(pool)
                for t in range(TAPS):
                    w = vv("cv_w", c * TAPS + t)
                    src = upad[:, c, t:t + S]
                    if t == 0:
                        if c == 2:
                            need(pool, poo.at("pad left"), poo.at("pad right"))
                            settled(pool)
                        nc.gpsimd.tensor_scalar(cvo[:, c, :], src, w, vv("cv_b", c), ALU.mult, ALU.add)\
                            .then_inc(*poo.mark(("conv", c, 0)))
                    else:
                        nc.gpsimd.tensor_scalar(cv_tmp[:, t % 2, :], src, w, None, ALU.mult)\
                            .then_inc(*poo.mark(("tap", c, t)))
                        need(pool, poo.at(("tap", c, t)))
                        nc.gpsimd.tensor_tensor(cvo[:, c, :], cvo[:, c, :], cv_tmp[:, t % 2, :], ALU.add)\
                            .then_inc(*poo.mark(("conv", c, t)))
            need(pool, ten.at("norm 2"), vec.at(("h", 2, KC - 1)))
            pool.dma_start(vec_t[:, :], vecs[L + 1]).then_inc(vec_in, 16)
            pool.dma_start(lo_w[:, :, :], lora[L + 1]).then_inc(lora_in, 16)
            pool.dma_start(wuq, wuq_in[L + 1]).then_inc(uk_in, 16)
            pool.dma_start(wukv, wukv_in[L + 1]).then_inc(uk_in, 16)
            loop.__exit__(None, None, None)
            pool.wait_ge(vec_in, (DEPTH + 1) * 16)
            pool.wait_ge(lora_in, (DEPTH + 1) * 16)
            pool.wait_ge(uk_in, (DEPTH + 1) * 32)

        @block.tensor
        def _(pe):
            TE = nc.tensor

            def products(o, wh, wl, hi, lo, first, last, **kw):
                TE.matmul(o, wh, hi, start=first, stop=False, **kw)
                TE.matmul(o, wh, lo, start=False, stop=False, **kw)
                return TE.matmul(o, wl, hi, start=False, stop=last, **kw)

            def col_tile(n, slot, o, hi, lo):
                pe.wait_ge(lo_ready, n + 1 + RAW)
                for k in range(KC):
                    last = products(o, whi[:, slot, k * P:(k + 1) * P], wlo[:, slot, k * P:(k + 1) * P],
                                    hi[:, k, :], lo[:, k, :], k == 0, k == KC - 1)
                last.then_inc(tile_used, 1)

            def row_tile(n, slot, hi, lo, first):
                pe.wait_ge(lo_ready, n + 1 + RAW)
                for m in range(KC):
                    last = products(bank[m // 2][:, (m % 2) * S:(m % 2 + 1) * S],
                                    whi[:, slot, m * P:(m + 1) * P], wlo[:, slot, m * P:(m + 1) * P],
                                    hi, lo, first and m % 2 == 0, False, skip_group_check=True)
                last.then_inc(tile_used, 1)

            pe.wait_ge(consts_in, 16)
            pe.wait_ge(zeros_set, 2)
            for _ in range(HL):
                TE.matmul(bank[7][:, 0:P], zero_b[0:1, 0:P], zero_b[0:1, 0:P], start=True, stop=True)\
                    .then_inc(tile_used, 1)
            loop, L = layers(pe)

            def norm(i):
                need(pe, act.at(("squares", i)))
                if i == 1:
                    need(pe, vec.at(("residual", 0, 3)))
                for k in range(KC):
                    m = TE.matmul(bank[6][:, 0:S], cc("ones", P), sq[:, k, :], start=k == 0, stop=k == KC - 1)
                m.then_inc(*ten.mark(f"norm {i}"))

            def ffn(f, tile0):
                base = (2 * L + f) * NFF
                t0 = L * TILES + tile0

                def up(j, s, n, slot):
                    pe.wait_ge(g_ready, base + j + 1)
                    for half in range(2):
                        col_tile(t0 + n + half, (slot + half) % HL, bank[4 + s][:, half * S:(half + 1) * S],
                                 h_hi, h_lo)

                def down(j, s, n, slot):
                    pe.wait_ge(glo_ready, base + j + 1)
                    row_tile(t0 + n, slot % HL, g_hi[:, s, :], g_lo[:, s, :], False)

                need(pe, vec.at(("h lo", 2 * f, KC - 1)))
                for b in range(4):
                    TE.matmul(bank[b][:, :], zero_b[0:1, 0:P], zero_b[0:1, :], start=True, stop=True)
                up(0, 0, 0, tile0)
                with pe.Fori(0, (NFF - 2) // 2) as it:
                    for q in range(2):
                        n = it * 6 + (2 + 3 * q)
                        up(it * 2 + (q + 1), (q + 1) % 2, n, tile0 + 2 + 3 * q)
                        down(it * 2 + q, q, n + 2, tile0 + 4 + 3 * q)
                up(NFF - 1, 1, 3 * NFF - 4, tile0 + 3 * NFF - 4)
                down(NFF - 2, 0, 3 * NFF - 2, tile0 + 3 * NFF - 2)
                down(NFF - 1, 1, 3 * NFF - 1, tile0 + 3 * NFF - 1)

            norm(0)
            ffn(0, T_FFN1)
            norm(1)

            need(pe, vec.at(("h lo", 1, KC - 1)))
            for i in range(T_BR - T_RW):
                n = T_RW + i
                if i >= 4:
                    val = n - 4 >= T_CV and (n - 4 - T_CV) % 2 == 0
                    need(pe, vec.at(("glu", (n - 4 - T_CV) // 2)) if val else act.at(("column", i - 4)))
                col_tile(L * TILES + n, n % HL, bank[4 + i % 4][:, 0:S], h_hi, h_lo)

            need(pe, act.at("latent squares"))
            for a, b, o in ((0, QC, 0), (QC, QC + KVC, S)):
                for c in range(a, b):
                    m = TE.matmul(bank[0][:, o:o + S], cc("ones", P), sq_lat[:, c, :], start=c == a, stop=c == b - 1)
            m.then_inc(*ten.mark("latent norms"))
            need(pe, vec.at("latents normed"))
            pe.wait_ge(uk_in, L * 32 + 32)
            for h in range(H):
                if h == 4:
                    need(pe, vec.at(("glu", 3)))
                for c in range(KVC):
                    m = TE.matmul(bank[2 + h // 2][0:NOPE, (h % 2) * S:(h % 2 + 1) * S],
                                  wukv[:, c, h * 128:h * 128 + NOPE], lat[:, QC + c, :],
                                  start=c == 0, stop=c == KVC - 1)
                if h % 2:
                    m.then_inc(*ten.mark(("k", h // 2)))
            for h in range(H):
                if h % 2 == 0:
                    need(pe, act.at(("k", h // 2)))
                for c in range(QC):
                    m = TE.matmul(bank[2 + h // 2][0:QK, (h % 2) * S:(h % 2 + 1) * S],
                                  wuq[:, c, h * QK:(h + 1) * QK], lat[:, c, :],
                                  start=c == 0, stop=c == QC - 1)
                if h % 2:
                    m.then_inc(*ten.mark(("q", h // 2)))
            wv = wukv.rearrange("p c (h n) -> p c h n", n=128)
            for t in range(NT):
                for c in range(KVC):
                    m = TE.matmul(bank[t][:, :], lat[:, QC + c, t * P:(t + 1) * P],
                                  wv[:, c, :, NOPE:], start=c == 0, stop=c == KVC - 1)
                m.then_inc(*ten.mark(("v", t)))
            for w in ("k", "q"):
                need(pe, act.at(f"{w} squares"))
                if w == "k":
                    need(pe, act.at(("v", NT - 1)))
                    need(pe, act.at(("q", 3)))
                else:
                    need(pe, vec.at("k turned"))
                for h in range(H):
                    m = TE.matmul(bank[0][0:H, 0:S], cc("e96", H, h * H, QK), hs[0:QK, h, :],
                                  start=h == 0, stop=h == H - 1)
                m.then_inc(*ten.mark(f"{w} sums"))
                need(pe, vec.at(f"{w} inverse"))
                for h in range(H):
                    m = TE.matmul(bank[1 + h // 2][0:QK, (h % 2) * S:(h % 2 + 1) * S],
                                  cc("b96", QK, h * QK, H), rn8[0:H, 0, :], start=True, stop=True)
                m.then_inc(*ten.mark(f"{w} spread"))
                need(pe, vec.at(f"{w} normed"))
                src = kf if w == "k" else qf
                for g in range(4):
                    m = TE.matmul(bank[1 + g][0:QK, :], cc("rot", QK, 0, QK), src[0:QK, 2 * g:2 * g + 2, :],
                                  start=True, stop=True)
                m.then_inc(*ten.mark(f"{w} rotated"))
            need(pe, vec.at("q turned"))

            def scores(h):
                if h >= 2:
                    need(pe, act.at(("exp", h - 2, 1)))
                for t in range(NT):
                    m = TE.matmul(bank[5 + h % 2][:, t * S:(t + 1) * S], qf[0:QK, h, t * P:(t + 1) * P],
                                  kf[0:QK, h, :], start=True, stop=True)
                m.then_inc(*ten.mark(("scores", h)))

            def mix(h):
                need(pe, vec.at(("prob", h, 1)))
                if h >= 2:
                    need(pe, act.at(("probT", h - 2)))
                for t in range(NT):
                    for b in range(NT):
                        m = TE.transpose(bank[1 + h % 2][:, b * S + t * P:b * S + (t + 1) * P],
                                         prob[:, h % 2, t, b * P:(b + 1) * P], ident)
                m.then_inc(*ten.mark(("probT", h)))
                need(pe, act.at(("probT", h)))
                if h >= 4 and h % 2 == 0:
                    need(pe, vec.at(("u", 2, h // 2 - 2)))
                r = HD * (h % 2)
                for b in range(NT):
                    m = TE.matmul(bank[3 + (h // 2) % 2][r:r + HD, 0:S], vm[:, b, h * HD:(h + 1) * HD],
                                  probT[:, h % 2, b, :], start=b == 0, stop=b == NT - 1)
                m.then_inc(*ten.mark(("attended", h)))

            scores(0)
            for h in range(H):
                if h + 1 < H:
                    scores(h + 1)
                mix(h)

            def branch(order, b):
                t0 = T_BR + order * (RC + KC)
                if order:
                    need(pe, vec.at(("merge", BRANCH_ORDER[order - 1], KC - 1)))
                need(pe, vec.at(("u", b, RC - 1)))
                for c in range(RC):
                    row_tile(L * TILES + t0 + c, (t0 + c) % HL, u_hi[:, c, :], u_lo[:, c, :], c == 0)
                for c in range(KC):
                    if c >= 4:
                        need(pe, act.at(("gate", b, c - 4)))
                    n = t0 + RC + c
                    col_tile(L * TILES + n, n % HL, bank[4 + c % 4][:, 0:S], h_hi, h_lo)

            branch(0, 2)

            need(pe, act.at(("gate", 2, KC - 1)))
            need(pe, vec.at(("conv", 1, TAPS - 1)), poo.at(("conv", 3, TAPS - 1)))
            for c in range(RC):
                m = TE.matmul(bank[4][:, 0:S], cc("ones", P), cvo[:, c, :], start=c == 0, stop=c == RC - 1)
            m.then_inc(*ten.mark("cv mean"))
            need(pe, act.at("cv squares"))
            for c in range(RC):
                m = TE.matmul(bank[5][:, 0:S], cc("ones", P), cv_sq[:, c, :], start=c == 0, stop=c == RC - 1)
            m.then_inc(*ten.mark("cv var"))
            branch(1, 1)

            need(pe, act.at(("gate", 1, KC - 1)))
            need(pe, act.at("key squares"))
            for j in range(RC):
                m = TE.matmul(bank[4][0:H, 0:S], cc("es", H, j * H), tA[:, j, :], start=j == 0, stop=j == RC - 1)
            m.then_inc(*ten.mark("key sums"))
            need(pe, vec.at("key inverse"))
            for j in range(RC):
                m = TE.matmul(bank[5 + j // 2][:, (j % 2) * S:(j % 2 + 1) * S], cc("eb", P, j * P, H),
                              rn_rw[0:H, 0, :], start=True, stop=True)
            m.then_inc(*ten.mark("key spread"))
            need(pe, act.at(("column", T_VD - T_RW)))
            need(pe, vec.at(("merge", 1, KC - 1)))
            for c in range(RC):
                m = TE.matmul(bank[c // 2][:, (c % 2) * S:(c % 2 + 1) * S], lo_w[0:32, 3, c * P:(c + 1) * P],
                              wag[0:32, 3, :], start=True, stop=True)
            m.then_inc(*ten.mark("nu"))
            need(pe, vec.at("values"))
            need(pe, act.at("nu"))
            for t in range(NT):
                for c in range(RC):
                    m = TE.transpose(bank[2 + t][:, c * P:(c + 1) * P], v_[:, c, t * P:(t + 1) * P], ident)
            m.then_inc(*ten.mark("vt"))

            for d in range(2):
                need(pe, act.at("wag"))
                if d == 0:
                    need(pe, vec.at("kk"), act.at("vt"))
                else:
                    need(pe, vec.at(("osum", 0)))
                for b0, col in ((0, 0), (2, 1)):
                    for c in range(RC):
                        m = TE.matmul(bank[b0 + c // 2][:, (c % 2) * S:(c % 2 + 1) * S],
                                      lo_w[HD * d:HD * d + HD, col, c * P:(c + 1) * P],
                                      wag[HD * d:HD * d + HD, col, :], start=True, stop=True)
                    m.then_inc(*ten.mark(("lora", d, col)))
                need(pe, vec.at(("kr", d)), vec.at(("bt", d)), vec.at(("kt", d)))
                if d == 0:
                    need(pe, vec.at("kk"))
                need(pe, act.at(("icl", d)), act.at(("sw", d)))
                for i in range(3):
                    for t in range(NT):
                        q = i * NT + t
                        for c in range(RC):
                            src = (kr[:, c, t, 0, :], bt[:, c, t * P:(t + 1) * P], kt[:, c, t * P:(t + 1) * P])[i]
                            m = TE.transpose(bank[q][:, c * P:(c + 1) * P], src, ident)
                        m.then_inc(*ten.mark(("tk", d, q)))
                need(pe, act.at(("tk", d, 5)))
                for h0 in range(0, H, 2):
                    pair = (h0, h0 + 1)
                    bk = {h: [bank[4 * (h % 2) + i] for i in range(4)] for h in pair}
                    if h0:
                        for h in pair:
                            need(pe, vec.at(("qw", d, h - 2)), vec.at(("o", d, h - 2)))
                    for h in pair:
                        r, j = HD * (h % 2), h // 2
                        for t in range(NT):
                            TE.matmul(bk[h][0][:, t * S:(t + 1) * S], bt[r:r + HD, j, t * P:(t + 1) * P],
                                      kr[r:r + HD, j, t, :, :], start=True, stop=True)
                        for t in range(NT):
                            TE.matmul(bk[h][1][:, t * S:(t + 1) * S], kt[r:r + HD, j, t * P:(t + 1) * P],
                                      kr[r:r + HD, j, t, :, :], start=True, stop=True)
                        for t in range(NT):
                            m = TE.matmul(bk[h][2][:, t * P:(t + 1) * P], kr[r:r + HD, j, t, 0, :],
                                          bt[r:r + HD, j, t * P:(t + 1) * P], start=True, stop=True)
                        m.then_inc(*ten.mark(("pairs", d, h)))
                    for lv in range(1, LEVELS):
                        for h in pair:
                            s = h % 2
                            need(pe, vec.at(("mn", d, h, lv - 1)))
                            for t in range(NT):
                                m = TE.matmul(bk[h][2][:, t * P:(t + 1) * P], g1[:, s, t, 0, :], mn[:, s, 0, t, :],
                                              start=True, stop=True)
                            m.then_inc(*ten.mark(("z", d, h, lv)))
                        for h in pair:
                            s = h % 2
                            need(pe, vec.at(("z", d, h, lv)))
                            for t in range(NT):
                                if lv < LEVELS - 1:
                                    TE.matmul(bk[h][3][:, t * P:(t + 1) * P], mn[:, s, 1, t, :], zz[:, s, t, :],
                                              start=True, stop=True)
                                m = TE.matmul(bk[h][3][:, S + t * P:S + (t + 1) * P], zz[:, s, t, :],
                                              mn[:, s, 1, t, :], start=True, stop=True)
                            m.then_inc(*ten.mark(("mz", d, h, lv)))
                    for h in pair:
                        s = h % 2
                        for t in range(NT):
                            m = TE.matmul(bk[h][2][:, S + t * HD:S + (t + 1) * HD], g2[:, s, t, 0, :],
                                          vt[:, t, h * HD:(h + 1) * HD], start=True, stop=True)
                        m.then_inc(*ten.mark(("gv", d, h)))
                    for h in pair:
                        s = h % 2
                        need(pe, vec.at(("mn", d, h, LEVELS - 1)), act.at(("gv", d, h)))
                        for t in range(NT):
                            TE.matmul(bk[h][3][:, t * HD:(t + 1) * HD], mn[:, s, 1, t, :],
                                      tk[:, 0, t, h * HD:(h + 1) * HD], start=True, stop=True)
                        for t in range(NT):
                            m = TE.matmul(bk[h][3][:, P + t * HD:P + (t + 1) * HD], mn[:, s, 1, t, :],
                                          gv[:, s, t, :], start=True, stop=True)
                        m.then_inc(*ten.mark(("xy", d, h)))
                    for h in pair:
                        s, r, j = h % 2, HD * (h % 2), h // 2
                        need(pe, act.at(("x", d, h)))
                        for t in range(NT):
                            m = TE.matmul(bk[h][2][r:r + HD, t * P:(t + 1) * P], xs[:, s, t, :], g1[:, s, t, 1, :],
                                          start=True, stop=True)
                        m.then_inc(*ten.mark(("rx", d, h)))
                        need(pe, act.at(("y", d, h)))
                        for t in range(NT):
                            o = bk[h][0][r:r + HD, t * P:(t + 1) * P]
                            TE.matmul(o, vt[:, t, h * HD:(h + 1) * HD], g2[:, s, t, 1, :], start=True, stop=False)
                            m = TE.matmul(o, ys[:, s, t, :], g1[:, s, t, 1, :], start=False, stop=True)
                        m.then_inc(*ten.mark(("o", d, h)))
                        for half in range(2):
                            q = HD * half
                            b = bk[h][1 + 2 * half]
                            for t in range(NT):
                                TE.matmul(b[r:r + HD, t * C:(t + 1) * C], xs[q:q + HD, s, t, :],
                                          tk[q:q + HD, 1, t, h * HD:(h + 1) * HD], start=True, stop=True)
                            for t in range(NT):
                                o = b[r:r + HD, P + t * HD:P + (t + 1) * HD]
                                TE.matmul(o, tk[q:q + HD, 2, t, h * HD:(h + 1) * HD],
                                          vt[q:q + HD, t, h * HD:(h + 1) * HD], start=True, stop=False)
                                m = TE.matmul(o, tk[q:q + HD, 1, t, h * HD:(h + 1) * HD], ys[q:q + HD, s, t, :],
                                              start=False, stop=True)
                        m.then_inc(*ten.mark(("pq", d, h)))
                chunks = range(NCH) if d == 0 else range(NCH - 1, -1, -1)
                need(pe, vec.at(("qw", d, H - 1)), vec.at(("o", d, H - 1)), vec.at(("qw", d, H - 2)), vec.at(("o", d, H - 2)))
                for i in (1, 2):
                    c, before = chunks[i], chunks[i - 1]
                    if i == 2:
                        need(pe, vec.at(("state", d, 1, 1)))
                    settled(pe)
                    for h in range(H):
                        r, j = HD * (h % 2), h // 2
                        m = TE.matmul(bank[h % 2][r:r + HD, j * HD:(j + 1) * HD], ptr[r:r + HD, j, c, :],
                                      qw[r:r + HD, j, before, :], start=True, stop=True)
                    m.then_inc(*ten.mark(("state", d, i)))
                need(pe, vec.at(("state", d, 2, 1)))
                settled(pe)
                for i in (1, 2, 3):
                    c, before = chunks[i], chunks[i - 1]
                    for h in range(H):
                        r, j = HD * (h % 2), h // 2
                        m = TE.matmul(bank[2 + h % 2 + 2 * (j // 2)][r:r + HD, (j % 2) * S + c * C:(j % 2) * S + (c + 1) * C],
                                      qw[r:r + HD, j, before, :], kr[r:r + HD, j, c // 2, 1, (c % 2) * C:(c % 2 + 1) * C],
                                      start=True, stop=True)
                m.then_inc(*ten.mark(("inter", d)))

            need(pe, vec.at(("osum", 1)), vec.at("bonus terms"))
            for b in range(2):
                m = TE.matmul(bank[b][:, :], cc("mean64", P), osum[:, 2 * b:2 * b + 2, :], start=True, stop=True)
            m.then_inc(*ten.mark("gn mean"))
            for b in range(2):
                m = TE.matmul(bank[6 + b][:, :], cc("mean64", P), tA[:, 2 * b:2 * b + 2, :], start=True, stop=True)
            m.then_inc(*ten.mark("bonus"))
            for c in range(RC):
                m = TE.matmul(bank[2 + c // 2][:, (c % 2) * S:(c % 2 + 1) * S], lo_w[:, 2, c * P:(c + 1) * P],
                              wag[:, 2, :], start=True, stop=True)
            m.then_inc(*ten.mark("g"))
            need(pe, act.at("gn squares"))
            for j in range(RC):
                m = TE.matmul(bank[4][0:H, 0:S], cc("es", H, j * H), tB[:, j, :], start=j == 0, stop=j == RC - 1)
            m.then_inc(*ten.mark("gn sums"))
            need(pe, vec.at("gn inverse"))
            for j in range(RC):
                m = TE.matmul(bank[j // 2][:, (j % 2) * S:(j % 2 + 1) * S], cc("eb", P, j * P, H),
                              rn_rw[0:H, 1, :], start=True, stop=True)
            m.then_inc(*ten.mark("gn spread"))
            branch(2, 0)

            need(pe, vec.at(("m lo", KC - 1)))
            need(pe, act.at(("gate", 0, KC - 1)))
            for c in range(KC):
                if c >= 4:
                    need(pe, vec.at(("x mixed", c - 4)))
                n = T_WO + c
                col_tile(L * TILES + n, n % HL, bank[4 + c % 4][:, 0:S], h_hi, h_lo)
            need(pe, vec.at(("x mixed", KC - 1)))
            norm(2)
            ffn(1, T_FFN2)
            for n in range(T_END, TILES):
                pe.wait_ge(lo_ready, L * TILES + n + 1 + RAW)
                TE.matmul(bank[7][:, 0:P], zero_b[0:1, 0:P], zero_b[0:1, 0:P], start=True, stop=True)\
                    .then_inc(tile_used, 1)
            loop.__exit__(None, None, None)

        @block.scalar
        def _(sc):
            SE = nc.scalar

            def hi(L, it, m):
                sc.wait_ge(raw_in[m % RAW], (L * (TILES // RAW) + it + (m // RAW + 1)) * 16)
                sc.wait_ge(tile_used, L * TILES + it * 6 + (m + 1))
                SE.copy(whi[:, m % HL, :], raw[:, m % RAW, :]).then_inc(hi_ready, 1)

            for m in range(HL):
                hi(0, 0, m)
            sc.wait_ge(rope_v, ROPE_STEPS)
            SE.activation(sinT[:, :], ang[:, 0, :], ACT.Sin).then_inc(rope_a, 1)
            SE.activation(cosT[:, :], ang[:, 1, :], ACT.Sin).then_inc(rope_a, 1)
            SE.preload_act_table(ACT.Sigmoid)
            loop, L = layers(sc)

            def used(n):
                sc.wait_ge(tile_used, L * TILES + n + 1 + HL)

            def norm(i):
                if i:
                    need(sc, vec.at(("residual", 0, 3) if i == 1 else ("x mixed", KC - 1)))
                else:
                    sc.wait_ge(x_ready, L + 1)
                SE.activation(sq, xT[:, :, :], ACT.Square).then_inc(*act.mark(("squares", i)))
                need(sc, ten.at(f"norm {i}"))
                SE.activation(nrm[:, 0, :], bank[6][:, 0:S], ACT.Sqrt, bias=cc("eps", 1, 0), scale=1.0 / D)\
                    .then_inc(*act.mark(("rms", i)))
                SE.preload_act_table(ACT.Sigmoid)
                for c in range(KC):
                    need(sc, vec.at(("h", i, c)))
                    SE.copy(h_hi[:, c, :], sq[:, c, :]).then_inc(*act.mark(("h hi", i, c)))

            def ffn(f, tile0):
                def chunk(it, j, s, m, down):
                    base = (2 * L + f) * NFF
                    hi(L, it, m + HL)
                    sc.wait_ge(tile_used, L * TILES + it * 6 + (m + 2 + HL))
                    SE.activation(g_s[:, s, :], bank[4 + s][:, 0:S], ACT.Sigmoid).then_inc(sig_ready, 1)
                    hi(L, it, m + 1 + HL)
                    sc.wait_ge(g_ready, base + j + 3)
                    SE.copy(g_hi[:, s, :], g_f[:, s, :]).then_inc(ghi_ready, 1)
                    if down:
                        hi(L, it, m + 2 + HL)

                chunk(0, 0, 0, tile0, False)
                with sc.Fori(0, (NFF - 2) // 2) as it:
                    for q in range(2):
                        chunk(it, it * 2 + (q + 1), (q + 1) % 2, tile0 + 2 + 3 * q, True)
                chunk(0, NFF - 1, 1, tile0 + 3 * NFF - 4, True)
                hi(L, 0, tile0 + 3 * NFF - 1 + HL)

            norm(0)
            ffn(0, T_FFN1)
            norm(1)
            for i in range(T_BR - T_RW):
                n = T_RW + i
                src = bank[4 + i % 4][:, 0:S]
                used(n)
                if n < T_VD:
                    g = i // 4
                    if i == 0:
                        need(sc, vec.at("pp edges"))
                    if g >= 2:
                        need(sc, vec.at(("mixed", g - 2)))
                    SE.copy(pp[:, g % 2, i % 4, 1:S + 1], src).then_inc(*act.mark(("column", i)))
                elif n < T_MLA:
                    need(sc, vec.at(("mixed", 3)))
                    SE.copy(wag[0:32, 3, :], bank[4 + i % 4][0:32, 0:S]).then_inc(*act.mark(("column", i)))
                elif n < T_MLA + QC + KVC:
                    SE.copy(lat[:, n - T_MLA, :], src).then_inc(*act.mark(("column", i)))
                elif n < T_CV:
                    SE.copy(rope_in[NOPE:QK, :], bank[4 + i % 4][NOPE:QK, 0:S]).then_inc(*act.mark(("column", i)))
                elif (n - T_CV) % 2:
                    c = (n - T_CV) // 2
                    if c >= 2:
                        need(sc, vec.at(("glu", c - 2)))
                    SE.activation(gs[:, c % 2, :], src, ACT.Sigmoid).then_inc(*act.mark(("column", i)))
                hi(L, 0, n + HL)

            need(sc, act.at(("column", T_MLA - T_RW + QC + KVC - 1)))
            SE.activation(sq_lat, lat, ACT.Square).then_inc(*act.mark("latent squares"))
            need(sc, ten.at("latent norms"))
            SE.activation(nrm[:, 0, :], bank[0][:, 0:S], ACT.Sqrt, bias=cc("eps", 1, 0), scale=1.0 / QR)
            SE.activation(nrm[:, 1, :], bank[0][:, S:2 * S], ACT.Sqrt, bias=cc("eps", 1, 0), scale=1.0 / KVR)\
                .then_inc(*act.mark("latent rms"))
            for g in range(4):
                need(sc, ten.at(("k", g)))
                SE.copy(kf[0:NOPE, 2 * g:2 * g + 2, :], bank[2 + g][0:NOPE, :].rearrange("p (h t) -> p h t", h=2))\
                    .then_inc(*act.mark(("k", g)))
            for g in range(4):
                need(sc, ten.at(("q", g)))
                SE.copy(qf[0:QK, 2 * g:2 * g + 2, :], bank[2 + g][0:QK, :].rearrange("p (h t) -> p h t", h=2))\
                    .then_inc(*act.mark(("q", g)))
            for t in range(NT):
                need(sc, ten.at(("v", t)))
                SE.copy(vm[:, t, :], bank[t][:, :]).then_inc(*act.mark(("v", t)))
            for w, src in (("k", kf), ("q", qf)):
                if w == "k":
                    need(sc, vec.at("rope keys"), act.at(("k", 3)))
                else:
                    need(sc, vec.at("k turned"), act.at(("q", 3)))
                SE.activation(hs[0:QK], src[0:QK], ACT.Square).then_inc(*act.mark(f"{w} squares"))
                need(sc, ten.at(f"{w} sums"))
                SE.activation(rn8[0:H, 0, :], bank[0][0:H, 0:S], ACT.Sqrt, bias=cc("eps", 1, 0, H), scale=1.0 / QK)\
                    .then_inc(*act.mark(f"{w} rms"))

            def exps(h):
                need(sc, ten.at(("scores", h)), vec.at(("max", h)))
                if h >= 2:
                    need(sc, ten.at(("probT", h - 2)))
                for t in range(NT):
                    SE.activation(prob[:, h % 2, t, :], bank[5 + h % 2][:, t * S:(t + 1) * S], ACT.Exp,
                                  bias=mx[:, h % 2, t:t + 1], scale=SCALE, accum_out=mx[:, h % 2, 2 + t:3 + t])\
                        .then_inc(*act.mark(("exp", h, t)))

            exps(0)
            for h in range(H):
                if h + 1 < H:
                    exps(h + 1)
                if h >= 2:
                    need(sc, ten.at(("attended", h - 2)))
                need(sc, ten.at(("probT", h)))
                SE.copy(probT[:, h % 2, :, :], bank[1 + h % 2][:, :].rearrange("p (b t) -> p b t", b=2))\
                    .then_inc(*act.mark(("probT", h)))
                if h % 2:
                    j = h // 2
                    need(sc, ten.at(("attended", h)))
                    SE.copy(u_hi[:, j, :], bank[3 + j % 2][:, 0:S]).then_inc(*act.mark(("u hi", 2, j)))

            def branch(order, b):
                t0 = T_BR + order * (RC + KC)
                for c in range(RC):
                    hi(L, 0, t0 + c + HL)
                for c in range(KC):
                    n = t0 + RC + c
                    if c >= 2:
                        need(sc, vec.at(("merge", b, c - 2)))
                    elif order:
                        need(sc, vec.at(("merge", BRANCH_ORDER[order - 1], KC - 2 + c)))
                    else:
                        need(sc, vec.at(("glu", 2 + c)))
                    used(n)
                    SE.activation(gs[:, c % 2, :], bank[4 + c % 4][:, 0:S], ACT.Sigmoid)\
                        .then_inc(*act.mark(("gate", b, c)))
                    hi(L, 0, n + HL)

            branch(0, 2)

            need(sc, ten.at("cv mean"))
            SE.mul(cv_st[:, 0, :], bank[4][:, 0:S], 1.0 / CV).then_inc(*act.mark("cv mean"))
            need(sc, vec.at(("cv centred", RC - 1)))
            SE.activation(cv_sq, cvo, ACT.Square).then_inc(*act.mark("cv squares"))
            need(sc, ten.at("cv var"))
            SE.activation(cv_st[:, 1, :], bank[5][:, 0:S], ACT.Sqrt, bias=cc("eps", 1, 2), scale=1.0 / CV)\
                .then_inc(*act.mark("cv rms"))
            SE.preload_act_table(ACT.Sigmoid)
            for c in range(RC):
                need(sc, vec.at(("cv normed", c)))
                SE.activation(cv_sq[:, c, :], cvo[:, c, :], ACT.Sigmoid, bias=vv("ln_b", c))\
                    .then_inc(*act.mark(("cv sigmoid", c)))
            sc.wait_ge(tile_used, L * TILES + T_BR + RC + HL)
            for c in range(RC):
                need(sc, vec.at(("cv act", c)))
                SE.copy(u_hi[:, c, :], cvo[:, c, :]).then_inc(*act.mark(("u hi", 1, c)))
            branch(1, 1)

            need(sc, vec.at("key scaled"))
            SE.activation(tA, kk, ACT.Square).then_inc(*act.mark("key squares"))
            need(sc, ten.at("key sums"))
            SE.activation(rn_rw[0:H, 0, :], bank[4][0:H, 0:S], ACT.Sqrt).then_inc(*act.mark("key rms"))
            SE.preload_act_table(ACT.Sigmoid)
            need(sc, vec.at(("mixed", 3)))
            SE.activation(wag[:, 0, :], wag[:, 0, :], ACT.Tanh).then_inc(*act.mark("wag tanh"))
            SE.activation(wag[:, 2, :], wag[:, 2, :], ACT.Sigmoid).then_inc(*act.mark("wag"))
            need(sc, ten.at("nu"))
            for c in range(RC):
                m = SE.activation(tB[:, c, :], bank[c // 2][:, (c % 2) * S:(c % 2 + 1) * S], ACT.Sigmoid,
                                  bias=vv("v0", c))
            m.then_inc(*act.mark("nu"))
            need(sc, ten.at("vt"))
            for t in range(NT):
                m = SE.copy(vt[:, t, :], bank[2 + t][:, :])
            m.then_inc(*act.mark("vt"))

            for d in range(2):
                if d:
                    need(sc, vec.at(("o", 0, H - 1)), vec.at(("qw", 0, H - 1)), ten.at(("pq", 0, H - 1)))
                else:
                    need(sc, vec.at("values"), vec.at("kk"))
                need(sc, ten.at(("lora", d, 0)))
                for c in range(RC):
                    m = SE.activation(tA[:, c, :], bank[c // 2][:, (c % 2) * S:(c % 2 + 1) * S], ACT.Sigmoid,
                                      bias=vv("w0", d * RC + c))
                m.then_inc(*act.mark(("sw", d)))
                need(sc, ten.at(("lora", d, 1)))
                for c in range(RC):
                    m = SE.activation(tB[:, c, :], bank[2 + c // 2][:, (c % 2) * S:(c % 2 + 1) * S], ACT.Sigmoid,
                                      bias=vv("a0", d * RC + c))
                m.then_inc(*act.mark(("icl", d)))
                SE.preload_act_table(ACT.Exp)
                need(sc, vec.at(("before", d)))
                SE.activation(tA, tC_, ACT.Exp, scale=-DECAY).then_inc(*act.mark(("w", d)))
                SE.activation(tD, tD, ACT.Exp, scale=-DECAY).then_inc(*act.mark(("wx", d)))
                need(sc, act.at(("w", d)))
                SE.activation(tC_, tC_, ACT.Exp, scale=DECAY).then_inc(*act.mark(("winv", d)))
                for q in range(6):
                    need(sc, ten.at(("tk", d, q)))
                    SE.copy(tk[:, q // NT, q % NT, :], bank[q][:, :]).then_inc(*act.mark(("tk", d, q)))
                for h0 in range(0, H, 2):
                    for h in (h0, h0 + 1):
                        need(sc, ten.at(("gv", d, h)))
                        SE.copy(gv[:, h % 2, :, :], bank[4 * (h % 2) + 2][:, S:S + P].rearrange("p (t c) -> p t c", t=NT))\
                            .then_inc(*act.mark(("gv", d, h)))
                    for h in (h0, h0 + 1):
                        b = bank[4 * (h % 2) + 3]
                        need(sc, ten.at(("xy", d, h)))
                        SE.copy(xs[:, h % 2, :, :], b[:, 0:P].rearrange("p (t c) -> p t c", t=NT))\
                            .then_inc(*act.mark(("x", d, h)))
                        SE.mul(ys[:, h % 2, :, :], b[:, P:2 * P].rearrange("p (t c) -> p t c", t=NT), -1.0)\
                            .then_inc(*act.mark(("y", d, h)))
            need(sc, vec.at("gn centred"))
            SE.activation(tB, osum, ACT.Square).then_inc(*act.mark("gn squares"))
            need(sc, ten.at("gn sums"))
            SE.activation(rn_rw[0:H, 1, :], bank[4][0:H, 0:S], ACT.Sqrt, bias=cc("eps", 1, 1, H), scale=1.0 / HD)\
                .then_inc(*act.mark("gn rms"))
            sc.wait_ge(tile_used, L * TILES + T_BR + 2 * RC + KC + HL)
            for c in range(RC):
                need(sc, vec.at(("rw out", c)))
                SE.copy(u_hi[:, c, :], osum[:, c, :]).then_inc(*act.mark(("u hi", 0, c)))
            SE.preload_act_table(ACT.Sigmoid)
            branch(2, 0)
            for c in range(KC):
                need(sc, vec.at(("merge", 0, KC - 1)))
                used(T_WO - 1)
                SE.copy(h_hi[:, c, :], merged[:, c, :]).then_inc(*act.mark(("m hi", c)))
            for c in range(KC):
                hi(L, 0, T_WO + c + HL)
            norm(2)
            ffn(1, T_FFN2)
            for n in range(T_END, TILES):
                hi(L, 0, n + HL)
            loop.__exit__(None, None, None)

        @block.vector
        def _(ve):
            V = nc.vector
            TT, TS, STT = V.tensor_tensor, V.tensor_scalar, V.scalar_tensor_tensor

            def lo(L, it, m):
                ve.wait_ge(hi_ready, L * TILES + it * 6 + (m + 1))
                TT(wlo[:, m % HL, :], raw[:, m % RAW, :], whi[:, m % HL, :].bitcast(F), ALU.subtract)\
                    .then_inc(lo_ready, 1)

            for i in range(RAW):
                V.memset(gs[:, 0, i:i + 1], 0.0).then_inc(lo_ready, 1)
            for i in range(RAW, RAW + 2):
                V.memset(gs[:, 0, i:i + 1], 0.0).then_inc(g_ready, 1)
            ve.wait_ge(consts_in, 16)
            ve.wait_ge(masks_in, 16)
            V.tensor_copy(msk[:, :], arena[:, 2048:2048 + NM])
            ve.wait_ge(x_in, 32)
            steps = [0]

            def chain(ins):
                steps[0] += 1
                ins.then_inc(rope_v, 1)
                ve.wait_ge(rope_v, steps[0])

            chain(V.tensor_copy(ang[:, 2, :], arena[:, 0:S].bitcast(mybir.dt.int32)))
            chain(TS(ang[:, 0, :], ang[:, 2, :], cc("freq", 1), None, ALU.mult))
            chain(TS(ang[:, 3, :], ang[:, 0, :], 1.0 / (2 * np.pi), MAGIC, ALU.mult, ALU.add))
            chain(TS(ang[:, 3, :], ang[:, 3, :], MAGIC, None, ALU.subtract))
            for part in TWO_PI:
                chain(STT(ang[:, 0, :], ang[:, 3, :], -part, ang[:, 0, :], ALU.mult, ALU.add))
            chain(TS(ang[:, 1, :], ang[:, 0, :], float(np.pi / 2), None, ALU.add))
            chain(TS(ang[:, 3, :], ang[:, 1, :], float(np.pi), None, ALU.is_gt))
            chain(STT(ang[:, 1, :], ang[:, 3, :], float(-2 * np.pi), ang[:, 1, :], ALU.mult, ALU.add))
            for i in range(2):
                chain(TS(ang[:, i, :], ang[:, i, :], PI_IN, -PI_IN, ALU.min, ALU.max))
            assert steps[0] == ROPE_STEPS
            ve.wait_ge(rope_a, 2)
            V.memset(gs[:, 0, 0:1], 0.0).then_inc(x_ready, 1)
            for m in range(HL):
                lo(0, 0, m)
            loop, L = layers(ve)
            ve.wait_ge(vec_in, L * 16 + 16)
            ve.wait_ge(lora_in, L * 16 + 16)

            def used(n):
                ve.wait_ge(tile_used, L * TILES + n + 1 + HL)

            def norm(i):
                gain = ("norm_ffn1", "norm_mix", "norm_ffn2")[i]
                need(ve, act.at(("rms", i)))
                V.reciprocal(nrm[:, 1, :], nrm[:, 0, :]).then_inc(*vec.mark(("rstd", i)))
                need(ve, vec.at(("rstd", i)))
                for c in range(KC):
                    STT(sq[:, c, :], xT[:, c, :], vv(gain, c), nrm[:, 1, :], ALU.mult, ALU.mult)\
                        .then_inc(*vec.mark(("h", i, c)))
                for c in range(KC):
                    need(ve, act.at(("h hi", i, c)))
                    TT(h_lo[:, c, :], sq[:, c, :], h_hi[:, c, :].bitcast(F), ALU.subtract)\
                        .then_inc(*vec.mark(("h lo", i, c)))

            def ffn(f, tile0):
                def chunk(it, j, s, m, down):
                    base = (2 * L + f) * NFF
                    lo(L, it, m + HL)
                    ve.wait_ge(sig_ready, base + j + 1)
                    TT(g_s[:, s, :], g_s[:, s, :], bank[4 + s][:, 0:S], ALU.mult).then_inc(as_ready, 1)
                    ve.wait_ge(as_ready, base + j + 1)
                    TT(g_f[:, s, :], g_s[:, s, :], bank[4 + s][:, S:2 * S], ALU.mult).then_inc(g_ready, 1)
                    lo(L, it, m + 1 + HL)
                    ve.wait_ge(ghi_ready, base + j + 1)
                    TT(g_lo[:, s, :], g_f[:, s, :], g_hi[:, s, :].bitcast(F), ALU.subtract).then_inc(glo_ready, 1)
                    if down:
                        lo(L, it, m + 2 + HL)

                chunk(0, 0, 0, tile0, False)
                with ve.Fori(0, (NFF - 2) // 2) as it:
                    for q in range(2):
                        chunk(it, it * 2 + (q + 1), (q + 1) % 2, tile0 + 2 + 3 * q, True)
                chunk(0, NFF - 1, 1, tile0 + 3 * NFF - 4, True)
                lo(L, 0, tile0 + 3 * NFF - 1 + HL)
                used(tile0 + 3 * NFF - 1)
                for b in range(4):
                    x2 = xT[:, 2 * b:2 * b + 2, :]
                    m = STT(x2, bank[b][:, :].rearrange("p (c t) -> p c t", c=2), 0.5, x2, ALU.mult, ALU.add)
                    m.then_inc(*vec.mark(("residual", f, b)))

            norm(0)
            ffn(0, T_FFN1)
            norm(1)
            V.memset(pp[:, :, :, 0:1], 0.0)
            V.memset(pp[:, :, :, S + 1:S + 2], 0.0).then_inc(*vec.mark("pp edges"))

            def shift_mix(g):
                n = 4 if g < 3 else 3
                dst = (r_, k_, v_, wag)[g]
                need(ve, act.at(("column", 4 * g + n - 1)), vec.at("pp edges"))
                p_ = pp[:, g % 2, 0:n, 1:S + 1]
                if g:
                    need(ve, vec.at(("mixed", g - 1)))
                TT(pt[:, 0:n, :], pp[:, g % 2, 0:n, 0:S], pp[:, g % 2, 0:n, 2:S + 2], ALU.add)\
                    .then_inc(*vec.mark(("sum", g)))
                need(ve, vec.at(("sum", g)))
                STT(pt[:, 0:n, :], pt[:, 0:n, :], 0.5, p_, ALU.mult, ALU.subtract).then_inc(*vec.mark(("shift", g)))
                need(ve, vec.at(("shift", g)))
                for c in range(n):
                    m = STT(dst[:, c, :], pt[:, c, :], vv("mu", 4 * g + c), pp[:, g % 2, c, 1:S + 1],
                            ALU.mult, ALU.add)
                m.then_inc(*vec.mark(("mixed", g)))

            for i in range(T_BR - T_RW):
                n = T_RW + i
                lo(L, 0, n + HL)
                if n < T_VD and (i % 4 == 3 or i == N_RW - 1):
                    shift_mix(i // 4)
                if n >= T_CV and (n - T_CV) % 2:
                    c = (n - T_CV) // 2
                    need(ve, act.at(("column", i)), poo.at("pad right"))
                    TT(upad[:, c, HALF:HALF + S], gs[:, c % 2, :], bank[4 + (i - 1) % 4][:, 0:S], ALU.mult)\
                        .then_inc(*vec.mark(("glu", c)))

            need(ve, act.at("latent rms"))
            V.reciprocal(nrm[:, :, :], nrm[:, :, :]).then_inc(*vec.mark("latent inverse"))
            need(ve, vec.at("latent inverse"))
            for c in range(QC + KVC):
                q = c < QC
                m = STT(lat[:, c, :], lat[:, c, :], vv("q_norm", c) if q else vv("kv_norm", c - QC),
                        nrm[:, 0 if q else 1, :], ALU.mult, ALU.mult)
            m.then_inc(*vec.mark("latents normed"))
            need(ve, act.at(("column", T_CV - 1 - T_RW)))
            V.tensor_copy(kf[NOPE:QK], rope_in[NOPE:QK].unsqueeze(1).broadcast_to([ROPE, H, S]))\
                .then_inc(*vec.mark("rope keys"))
            for w, x_ in (("k", kf), ("q", qf)):
                need(ve, act.at(f"{w} rms"))
                V.reciprocal(rn8[0:H, 0, :], rn8[0:H, 0, :]).then_inc(*vec.mark(f"{w} inverse"))
                need(ve, ten.at(f"{w} spread"))
                for g in range(4):
                    xg = x_[0:QK, 2 * g:2 * g + 2, :]
                    m = STT(xg, xg, vv(f"qk_{w}_g", 0, 0, QK),
                            bank[1 + g][0:QK, :].rearrange("p (h t) -> p h t", h=2), ALU.mult, ALU.mult)
                m.then_inc(*vec.mark(f"{w} normed"))
                need(ve, ten.at(f"{w} rotated"))
                for g in range(4):
                    m = TT(hs[0:QK, 2 * g:2 * g + 2, :], bank[1 + g][0:QK, :].rearrange("p (h t) -> p h t", h=2),
                           sinT[0:QK].unsqueeze(1).broadcast_to([QK, 2, S]), ALU.mult)
                m.then_inc(*vec.mark(f"{w} sine part"))
                TT(x_[0:QK], x_[0:QK], cosT[0:QK].unsqueeze(1).broadcast_to([QK, H, S]), ALU.mult)\
                    .then_inc(*vec.mark(f"{w} cosine part"))
                need(ve, vec.at(f"{w} cosine part"))
                TT(x_[0:QK], x_[0:QK], hs[0:QK], ALU.add).then_inc(*vec.mark(f"{w} turned"))

            def head_max(h):
                need(ve, ten.at(("scores", h)))
                if h >= 2:
                    need(ve, vec.at(("prob", h - 2, 1)))
                V.reduce_max(mx[:, h % 2, 0:2], bank[5 + h % 2][:, :].rearrange("p (t k) -> p t k", t=NT), AX.X)\
                    .then_inc(*vec.mark(("rawmax", h)))
                need(ve, vec.at(("rawmax", h)))
                TS(mx[:, h % 2, 0:2], mx[:, h % 2, 0:2], -SCALE, None, ALU.mult).then_inc(*vec.mark(("max", h)))

            head_max(0)
            for h in range(H):
                if h + 1 < H:
                    head_max(h + 1)
                need(ve, act.at(("exp", h, 1)))
                V.reciprocal(mx[:, h % 2, 2:4], mx[:, h % 2, 2:4]).then_inc(*vec.mark(("invsum", h)))
                need(ve, vec.at(("invsum", h)))
                for t in range(NT):
                    TS(prob[:, h % 2, t, :], prob[:, h % 2, t, :], mx[:, h % 2, 2 + t:3 + t], None, ALU.mult)\
                        .then_inc(*vec.mark(("prob", h, t)))
                if h % 2:
                    j = h // 2
                    need(ve, act.at(("u hi", 2, j)))
                    TT(u_lo[:, j, :], bank[3 + j % 2][:, 0:S], u_hi[:, j, :].bitcast(F), ALU.subtract)\
                        .then_inc(*vec.mark(("u", 2, j)))

            taps = [(c, t) for t in range(TAPS) for c in range(2)]

            def conv(n):
                for c, t in [taps.pop(0) for _ in range(min(n, len(taps)))]:
                    src = upad[:, c, t:t + S]
                    if t == 0:
                        need(ve, vec.at(("glu", 3)))
                        m = TS(cvo[:, c, :], src, vv("cv_w", c * TAPS), vv("cv_b", c), ALU.mult, ALU.add)
                    else:
                        need(ve, vec.at(("conv", c, t - 1)))
                        m = STT(cvo[:, c, :], src, vv("cv_w", c * TAPS + t), cvo[:, c, :], ALU.mult, ALU.add)
                    m.then_inc(*vec.mark(("conv", c, t)))

            def branch(order, b, between):
                t0 = T_BR + order * (RC + KC)
                for c in range(RC):
                    lo(L, 0, t0 + c + HL)
                    between()
                for c in range(KC):
                    n = t0 + RC + c
                    need(ve, act.at(("gate", b, c)))
                    acc = bank[c // 2][:, (c % 2) * S:(c % 2 + 1) * S]
                    if order == 0:
                        TT(merged[:, c, :], gs[:, c % 2, :], acc, ALU.mult).then_inc(*vec.mark(("merge", b, c)))
                    else:
                        TT(gs[:, c % 2, :], gs[:, c % 2, :], acc, ALU.mult).then_inc(*vec.mark(("gated", b, c)))
                        need(ve, vec.at(("gated", b, c)))
                        TT(merged[:, c, :], merged[:, c, :], gs[:, c % 2, :], ALU.add)\
                            .then_inc(*vec.mark(("merge", b, c)))
                    lo(L, 0, n + HL)
                    between()

            branch(0, 2, lambda: conv(6))
            conv(len(taps))

            need(ve, act.at("cv mean"))
            for c in range(RC):
                TT(cvo[:, c, :], cvo[:, c, :], cv_st[:, 0, :], ALU.subtract).then_inc(*vec.mark(("cv centred", c)))
            need(ve, act.at("cv rms"))
            V.reciprocal(cv_st[:, 2, :], cv_st[:, 1, :]).then_inc(*vec.mark("cv inverse"))
            need(ve, vec.at("cv inverse"))
            for c in range(RC):
                STT(cvo[:, c, :], cvo[:, c, :], vv("ln_g", c), cv_st[:, 2, :], ALU.mult, ALU.mult)\
                    .then_inc(*vec.mark(("cv normed", c)))
            for c in range(RC):
                need(ve, act.at(("cv sigmoid", c)))
                STT(cvo[:, c, :], cvo[:, c, :], vv("ln_b", c), cv_sq[:, c, :], ALU.add, ALU.mult)\
                    .then_inc(*vec.mark(("cv act", c)))
            for c in range(RC):
                need(ve, act.at(("u hi", 1, c)))
                TT(u_lo[:, c, :], cvo[:, c, :], u_hi[:, c, :].bitcast(F), ALU.subtract).then_inc(*vec.mark(("u", 1, c)))
            branch(1, 1, lambda: None)

            for c in range(RC):
                m = TS(kk[:, c, :], k_[:, c, :], vv("k_k", c), None, ALU.mult)
            m.then_inc(*vec.mark("key scaled"))
            need(ve, act.at("key rms"))
            TS(rn_rw[0:H, 0, :], rn_rw[0:H, 0, :], 1e-12, None, ALU.max).then_inc(*vec.mark("key floor"))
            need(ve, vec.at("key floor"))
            V.reciprocal(rn_rw[0:H, 0, :], rn_rw[0:H, 0, :]).then_inc(*vec.mark("key inverse"))
            need(ve, ten.at("key spread"))
            for b in range(2):
                m = TT(kk[:, 2 * b:2 * b + 2, :], kk[:, 2 * b:2 * b + 2, :],
                       bank[5 + b][:, :].rearrange("p (c t) -> p c t", c=2), ALU.mult)
            m.then_inc(*vec.mark("kk"))
            TT(tC_, vfirst[:, :, :], v_, ALU.subtract).then_inc(*vec.mark("v difference"))
            need(ve, act.at("nu"), vec.at("v difference"))
            TT(tC_, tC_, tB, ALU.mult).then_inc(*vec.mark("v share"))
            need(ve, vec.at("v share"))
            STT(v_, tC_, vv("keep"), v_, ALU.mult, ALU.add).then_inc(*vec.mark("values"))
            need(ve, vec.at("values"))
            TT(tD, v_, vfirst[:, :, :], ALU.subtract).then_inc(*vec.mark("first difference"))
            need(ve, vec.at("first difference"))
            STT(vfirst[:, :, :], tD, vv("first"), vfirst[:, :, :], ALU.mult, ALU.add)\
                .then_inc(*vec.mark("first values"))

            kr_kk = kr[:, :, :, 0, :]
            kr_r = kr[:, :, :, 1, :]
            by_tile = lambda a: a.rearrange("p c (t q) -> p c t q", t=NT)
            for d in range(2):
                need(ve, act.at(("sw", d)))
                if d == 0:
                    need(ve, vec.at("first values"))
                for c in range(RC):
                    m_, s_, o_ = cc("scan", S, d * S), tA[:, c, :], tC_[:, c, :]
                    if d:
                        m_, s_, o_ = (a[:, ::-1] for a in (m_, s_, o_))
                    m = V.tensor_tensor_scan(o_, m_, s_, 0.0, ALU.mult, ALU.add)
                m.then_inc(*vec.mark(("scan", d)))
                need(ve, vec.at(("scan", d)))
                TT(tD, tC_, tA, ALU.subtract).then_inc(*vec.mark(("before", d)))
                need(ve, act.at(("w", d)))
                TT(kr_r, by_tile(r_), by_tile(tA), ALU.mult)
                edge = C - 1 if d == 0 else 0
                V.tensor_copy(wch, tA.rearrange("p c (n e) -> p c n e", e=C)[:, :, :, edge]).then_inc(*vec.mark(("wch", d)))
                need(ve, act.at(("wx", d)))
                TT(kr_kk, by_tile(kk), by_tile(tD), ALU.mult).then_inc(*vec.mark(("kr", d)))
                need(ve, act.at(("icl", d)))
                TT(bt, kk, tB, ALU.mult).then_inc(*vec.mark(("b", d)))
                need(ve, act.at(("winv", d)), vec.at(("b", d)), vec.at(("kr", d)))
                TT(bt, bt, tC_, ALU.mult).then_inc(*vec.mark(("bt", d)))
                for c in range(RC):
                    m = TS(tD[:, c, :], tB[:, c, :], -1.0, vv("k_a", c), ALU.add, ALU.mult)
                m.then_inc(*vec.mark(("ka", d)))
                need(ve, vec.at(("ka", d)))
                STT(tD, tD, 1.0, k_, ALU.add, ALU.mult).then_inc(*vec.mark(("kdir", d)))
                need(ve, vec.at(("kdir", d)))
                if d == 0:
                    V.tensor_copy(kds, tD).then_inc(*vec.mark("kds 0"))
                else:
                    TT(kds, kds, tD, ALU.add).then_inc(*vec.mark("kds 1"))
                TT(kt, tD, tC_, ALU.mult).then_inc(*vec.mark(("kt", d)))
                need(ve, vec.at(("kt", d)))

                tm = msk[:, d * 2 * P:(d + 1) * 2 * P].rearrange("p (i t) -> p i t", i=2)
                tm = tm.unsqueeze(1).broadcast_to([P, NT, 2, P])
                m1 = msk[:, M1 + d * 2 * P:M1 + (d + 1) * 2 * P].rearrange("p (i t) -> p i t", i=2)
                flat = lambda a: a.rearrange("p t n -> p (t n)")
                for h0 in range(0, H, 2):
                    pair = (h0, h0 + 1)
                    for h in pair:
                        s, b = h % 2, 4 * (h % 2)
                        need(ve, ten.at(("pairs", d, h)))
                        TT(g1[:, s], bank[b][:, :].rearrange("p (t i n) -> p t i n", t=NT, i=2), tm, ALU.mult)\
                            .then_inc(*vec.mark(("g1", d, h)))
                        TT(g2[:, s], bank[b + 1][:, :].rearrange("p (t i n) -> p t i n", t=NT, i=2), tm, ALU.mult)\
                            .then_inc(*vec.mark(("g2", d, h)))
                        TT(mn[:, s, 0], bank[b + 2][:, 0:S].rearrange("p (t n) -> p t n", t=NT),
                           m1[:, 0:1, :].broadcast_to([P, NT, P]), ALU.mult)
                        need(ve, vec.at(("g1", d, h)))
                        TT(mn[:, s, 1], g1[:, s, :, 0, :], m1[:, 1:2, :].broadcast_to([P, NT, P]), ALU.mult)\
                            .then_inc(*vec.mark(("m1", d, h)))
                        need(ve, vec.at(("m1", d, h)))
                        mn4 = mn[:, s].rearrange("p i t n -> p (i t) n")
                        TT(mn4, mn4, ident.unsqueeze(1).broadcast_to([P, 2 * NT, P]), ALU.add)\
                            .then_inc(*vec.mark(("mn", d, h, 0)))
                    for lv in range(1, LEVELS):
                        o = LEV + (d * (LEVELS - 1) + lv - 1) * P
                        mask = msk[:, o:o + P].unsqueeze(1).broadcast_to([P, NT, P])
                        for h in pair:
                            s, b = h % 2, 4 * (h % 2)
                            need(ve, ten.at(("z", d, h, lv)))
                            TT(zz[:, s], bank[b + 2][:, 0:S].rearrange("p (t n) -> p t n", t=NT), mask, ALU.mult)\
                                .then_inc(*vec.mark(("z", d, h, lv)))
                        for h in pair:
                            s, b = h % 2, 4 * (h % 2)
                            need(ve, ten.at(("mz", d, h, lv)))
                            if lv < LEVELS - 1:
                                mn4 = mn[:, s].rearrange("p i t n -> p (i t) n")
                                TT(mn4, mn4, bank[b + 3][:, :].rearrange("p (i n) -> p i n", n=P), ALU.subtract)\
                                    .then_inc(*vec.mark(("mn", d, h, lv)))
                            else:
                                TT(mn[:, s, 1], mn[:, s, 1], bank[b + 3][:, S:].rearrange("p (i n) -> p i n", n=P),
                                   ALU.subtract).then_inc(*vec.mark(("mn", d, h, lv)))
                    for h in pair:
                        s, b, r, j = h % 2, 4 * (h % 2), HD * (h % 2), h // 2
                        need(ve, ten.at(("rx", d, h)))
                        w = kr[r:r + HD, j, :, 1, :]
                        TT(w, w, bank[b + 2][r:r + HD, 0:S].rearrange("p (t n) -> p t n", t=NT), ALU.subtract)\
                            .then_inc(*vec.mark(("rx", d, h)))
                        need(ve, ten.at(("o", d, h)))
                        if d == 0:
                            V.tensor_copy(osum[r:r + HD, j, :], bank[b][r:r + HD, 0:S]).then_inc(*vec.mark(("o", d, h)))
                        else:
                            TT(osum[r:r + HD, j, :], osum[r:r + HD, j, :], bank[b][r:r + HD, 0:S], ALU.add)\
                                .then_inc(*vec.mark(("o", d, h)))
                        need(ve, ten.at(("pq", d, h)))
                        for half in range(2):
                            pq = bank[b + 1 + 2 * half]
                            by2 = lambda a: a[r:r + HD, j].rearrange("p (t e) n -> p e t n", e=2)[:, half]
                            TT(by2(ptr), cc("ident64", C)[r:r + HD].unsqueeze(1).broadcast_to([HD, NT, C]),
                               pq[r:r + HD, 0:P].rearrange("p (t n) -> p t n", t=NT), ALU.subtract)
                            wb = wch[r:r + HD, j].rearrange("p (t e) -> p e t", e=2)[:, half]
                            m = TT(by2(qw), pq[r:r + HD, P:2 * P].rearrange("p (t n) -> p t n", t=NT),
                                   wb.unsqueeze(2).broadcast_to([HD, NT, HD]), ALU.mult)
                        m.then_inc(*vec.mark(("qw", d, h)))
                chunks = range(NCH) if d == 0 else range(NCH - 1, -1, -1)
                for i in (1, 2):
                    c = chunks[i]
                    need(ve, ten.at(("state", d, i)), vec.at(("qw", d, H - 1)))
                    if i == 2:
                        need(ve, vec.at(("state", d, 1, 1)))
                    for e in range(2):
                        r = HD * e
                        dst = tmp_s[r:r + HD]
                        TT(dst, bank[e][r:r + HD, 0:S].rearrange("p (j n) -> p j n", j=RC),
                           wch[r:r + HD, :, c].unsqueeze(2).broadcast_to([HD, RC, HD]), ALU.mult)\
                            .then_inc(*vec.mark(("decayed", d, i, e)))
                    for e in range(2):
                        r = HD * e
                        need(ve, vec.at(("decayed", d, i, e)))
                        TT(qw[r:r + HD, :, c, :], qw[r:r + HD, :, c, :], tmp_s[r:r + HD], ALU.add)\
                            .then_inc(*vec.mark(("state", d, i, e)))
                need(ve, ten.at(("inter", d)), vec.at(("o", d, H - 1)))
                a, z = (C, S) if d == 0 else (0, S - C)
                for e in range(2):
                    for g in range(2):
                        r = HD * e
                        o = osum[r:r + HD, 2 * g:2 * g + 2, a:z]
                        m = TT(o, o, bank[2 + e + 2 * g][r:r + HD, :].rearrange("p (j t) -> p j t", j=2)[:, :, a:z],
                               ALU.add)
                m.then_inc(*vec.mark(("osum", d)))

            for c in range(RC):
                m = STT(tA[:, c, :], kds[:, c, :], vv("r_k", c), r_[:, c, :], ALU.mult, ALU.mult)
            m.then_inc(*vec.mark("bonus terms"))
            need(ve, ten.at("gn mean"), vec.at(("osum", 1)))
            for b in range(2):
                o = osum[:, 2 * b:2 * b + 2, :]
                m = TT(o, o, bank[b][:, :].rearrange("p (c t) -> p c t", c=2), ALU.subtract)
            m.then_inc(*vec.mark("gn centred"))
            need(ve, ten.at("bonus"))
            for b in range(2):
                m = STT(tC_[:, 2 * b:2 * b + 2, :], bank[6 + b][:, :].rearrange("p (c t) -> p c t", c=2), 0.5 * HD,
                        v_[:, 2 * b:2 * b + 2, :], ALU.mult, ALU.mult)
            m.then_inc(*vec.mark("bonus"))
            need(ve, act.at("gn rms"))
            V.reciprocal(rn_rw[0:H, 1, :], rn_rw[0:H, 1, :]).then_inc(*vec.mark("gn inverse"))
            need(ve, ten.at("gn spread"), vec.at("bonus"), vec.at("gn centred"))
            half_bank = lambda b0, c: bank[b0 + c // 2][:, (c % 2) * S:(c % 2 + 1) * S]
            for c in range(RC):
                STT(osum[:, c, :], osum[:, c, :], vv("gn_g", c), half_bank(0, c), ALU.mult, ALU.mult)\
                    .then_inc(*vec.mark(("gn normed", c)))
            for c in range(RC):
                need(ve, vec.at(("gn normed", c)))
                STT(osum[:, c, :], osum[:, c, :], vv("gn_b", c), tC_[:, c, :], ALU.add, ALU.add)\
                    .then_inc(*vec.mark(("gn bonus", c)))
            need(ve, ten.at("g"))
            for c in range(RC):
                need(ve, vec.at(("gn bonus", c)))
                TT(osum[:, c, :], osum[:, c, :], half_bank(2, c), ALU.mult).then_inc(*vec.mark(("rw out", c)))
            for c in range(RC):
                need(ve, act.at(("u hi", 0, c)), vec.at(("rw out", c)))
                TT(u_lo[:, c, :], osum[:, c, :], u_hi[:, c, :].bitcast(F), ALU.subtract).then_inc(*vec.mark(("u", 0, c)))
            branch(2, 0, lambda: None)
            for c in range(KC):
                need(ve, act.at(("m hi", c)), vec.at(("merge", 0, KC - 1)))
                TT(h_lo[:, c, :], merged[:, c, :], h_hi[:, c, :].bitcast(F), ALU.subtract)\
                    .then_inc(*vec.mark(("m lo", c)))
            for c in range(KC):
                used(T_WO + c)
                TT(xT[:, c, :], xT[:, c, :], bank[4 + c % 4][:, 0:S], ALU.add).then_inc(*vec.mark(("x mixed", c)))
                lo(L, 0, T_WO + c + HL)
            norm(2)
            ffn(1, T_FFN2)
            V.memset(gs[:, 0, 0:1], 0.0).then_inc(x_ready, 1)
            need(ve, vec.at(("residual", 1, 3)))
            for n in range(T_END, TILES):
                lo(L, 0, n + HL)
            loop.__exit__(None, None, None)

    return {s.name: s.counted() for s in (vec, act, ten, poo)}


def laid_out(inputs):
    a = {n: np.ascontiguousarray(v) for n, v in inputs.items()}
    f = np.float32

    def col(w, c0):
        return w[:, c0:c0 + P].reshape(-1, P, P).transpose(1, 0, 2).reshape(P, -1)

    stream = np.zeros((DEPTH * TILES + HL, P, D), f)
    vecs = np.zeros((DEPTH + 1, P, NV), f)
    lora = np.zeros((DEPTH + 1, P, 4 * RW), f)
    wuq = np.zeros((DEPTH + 1, P, QC * H * QK), f)
    wukv = np.zeros((DEPTH + 1, P, KVC * H * 128), f)
    for l in range(DEPTH):
        r = max(l - 1, 0)
        T = stream[l * TILES:(l + 1) * TILES]
        for f_, t0 in (("ffn1", T_FFN1), ("ffn2", T_FFN2)):
            w1, w3, w2 = (a[f"{f_}_{w}"][l] for w in ("w1", "w3", "w2"))
            for j in range(NFF):
                up = t0 + (0 if j == 0 else 3 * j - 1)
                T[up], T[up + 1] = col(w1, j * P), col(w3, j * P)
                T[t0 + min(3 * j + 4, 3 * NFF - 2 + (j == NFF - 1))] = w2[j * P:(j + 1) * P]
        w_in = a["w_in"][l]
        for i in range(N_RW):
            T[T_RW + i] = col(w_in, i * P)
        vd = np.zeros((D, P), f)
        vd[:, :32] = a["rw_v_down"][r]
        T[T_VD] = col(vd, 0)
        m0 = RW_COLS + CV_COLS
        for i in range(QC + KVC):
            T[T_MLA + i] = col(w_in, m0 + i * P)
        T[T_MLA + QC + KVC] = col(w_in, m0 + QR + KVR - NOPE)
        for c in range(RC):
            T[T_CV + 2 * c] = col(w_in, RW_COLS + c * P)
            T[T_CV + 2 * c + 1] = col(w_in, RW_COLS + CV + c * P)
        for order, b in enumerate(BRANCH_ORDER):
            t0 = T_BR + order * (RC + KC)
            w = a[("rw_w_branch", "cv_w_branch", "mla_w_branch")[b]][l]
            for c in range(RC):
                T[t0 + c] = w[c * P:(c + 1) * P]
            for c in range(KC):
                T[t0 + RC + c] = col(w_in, m0 + MLA_COLS + b * D + c * P)
        for c in range(KC):
            T[T_WO + c] = col(a["w_o"][l], c * P)

        def put(name, v, at=0):
            v = v.reshape(-1, P).T if v.size % P == 0 else np.pad(v, (0, P - v.size))[:, None]
            vecs[l, :, VEC[name] + at:VEC[name] + at + v.shape[1]] = v

        for name in ("norm_ffn1", "norm_mix", "norm_ffn2"):
            put(name, a[name][l])
        put("mu", a["rw_mu"][l])
        for d in range(2):
            put("w0", a["rw_w0"][l, d], d * RC)
            put("a0", a["rw_a0"][l, d], d * RC)
            lora[l, d * HD:(d + 1) * HD, 0:RW] = a["rw_w_up"][l, d]
            lora[l, d * HD:(d + 1) * HD, RW:2 * RW] = a["rw_a_up"][l, d]
        for name, src in (("k_k", "rw_k_k"), ("k_a", "rw_k_a"), ("gn_g", "rw_gn_g"), ("gn_b", "rw_gn_b"),
                          ("cv_b", "cv_dw_b"), ("ln_g", "cv_ln_g"), ("ln_b", "cv_ln_b"), ("q_norm", "mla_q_norm"),
                          ("kv_norm", "mla_kv_norm"), ("qk_q_g", "mla_qk_q_g"), ("qk_k_g", "mla_qk_k_g")):
            put(name, a[src][l])
        put("r_k", a["rw_r_k"][l].reshape(-1))
        put("v0", a["rw_v0"][r])
        vecs[l, :, VEC["cv_w"]:VEC["cv_w"] + RC * TAPS] = \
            a["cv_dw_w"][l].reshape(TAPS, RC, P).transpose(2, 1, 0).reshape(P, -1)
        vecs[l, :, VEC["keep"]] = float(l > 0)
        vecs[l, :, VEC["first"]] = float(l == 0)
        lora[l, :, 2 * RW:3 * RW] = a["rw_g_up"][l]
        lora[l, :32, 3 * RW:] = a["rw_v_up"][r]
        wuq[l] = a["mla_w_uq"][l].reshape(QC, P, -1).transpose(1, 0, 2).reshape(P, -1)
        wukv[l] = a["mla_w_ukv"][l].reshape(KVC, P, -1).transpose(1, 0, 2).reshape(P, -1)
    x = np.ascontiguousarray(a["x"][0].T.reshape(KC, P, S).transpose(1, 0, 2))
    pos = np.ascontiguousarray(np.broadcast_to(a["positions"][0], (P, S)))
    c, m = constants()
    return {"x": x, "pos": pos, "stream": stream, "vecs": vecs, "cst": c, "msk": m, "lora": lora,
            "wuq": wuq, "wukv": wukv}


def kernel(**inputs):
    import concourse.bacc as bacc
    from concourse.bass_utils import run_bass_kernel_spmd

    arrays = laid_out(inputs)

    def build(known):
        nc = bacc.Bacc("TRN2", target_bir_lowering=False, num_devices=1)
        args = [nc.dram_tensor(f"in_{n}", v.shape, mybir.dt.from_np(v.dtype), kind="ExternalInput").ap()
                for n, v in arrays.items()]
        out = nc.dram_tensor("out", (P, KC, S), F, kind="ExternalOutput").ap()
        return nc, program(nc, *args, out, known)

    _, known = build(None)
    nc, _ = build(known)
    r = run_bass_kernel_spmd(nc, [{f"in_{n}": v for n, v in arrays.items()}], core_ids=[0])
    y = r.results[0]["out"]
    return np.ascontiguousarray(y.transpose(2, 1, 0).reshape(1, S, D))
```

```python
import numpy as np
from contextlib import ExitStack
import concourse.bass as bass
import concourse.mybir as mybir

F = mybir.dt.float32
R = mybir.dt.float32r
BF = mybir.dt.bfloat16
ALU = mybir.AluOpType
ACT = mybir.ActivationFunctionType
AX = mybir.AxisListType

P = 128
D = 1024
S = 256
DEPTH = 2
FF = 2816
KC = D // P
NFF = FF // P
NT = S // P
C = 64
NCH = S // C
H = 8
HD = 64
RW = H * HD
RC = RW // P
CV = 512
TAPS = 31
HALF = TAPS // 2
QR, KVR, ROPE, NOPE = 384, 256, 32, 64
QK = NOPE + ROPE
QC, KVC = QR // P, KVR // P
NORM_EPS, GN_EPS, LN_EPS = 1e-6, 64e-5, 1e-5
DECAY = float(np.exp(-0.5))
SCALE = float(QK) ** -0.5
LEVELS = 6

N_RW, N_VD, N_MLA, N_CV = 15, 1, 6, 8
T_FFN1 = 0
T_MLA = T_FFN1 + 3 * NFF
T_CV = T_MLA + N_MLA
T_RW = T_CV + N_CV
T_VD = T_RW + N_RW
T_BR = T_VD + N_VD
T_WO = T_BR + 3 * (RC + KC)
T_FFN2 = T_WO + KC
T_END = T_FFN2 + 3 * NFF
RAW, HL = 3, 3
LOOP = 6
TILES = -(-T_END // LOOP) * LOOP
BRANCH_ORDER = (2, 1, 0)
RW_COLS, CV_COLS, MLA_COLS = 1920, 1024, 672

VEC = {}
NV = 0
for _name, _n in (("norm_ffn1", KC), ("norm_mix", KC), ("norm_ffn2", KC), ("mu", N_RW), ("w0", 2 * RC),
                  ("a0", 2 * RC), ("k_k", RC), ("k_a", RC), ("r_k", RC), ("v0", RC), ("gn_g", RC),
                  ("gn_b", RC), ("cv_b", RC), ("ln_g", RC), ("ln_b", RC), ("q_norm", QC),
                  ("kv_norm", KVC), ("qk_q_g", 1), ("qk_k_g", 1), ("cv_w", RC * TAPS), ("keep", 1),
                  ("first", 1)):
    VEC[_name] = NV
    NV += _n

CST = {}
NC = 0
for _name, _n in (("ident", P), ("ones", P), ("mean64", P), ("ident64", C), ("rot", QK), ("es", RC * H),
                  ("eb", RC * P), ("e96", H * H), ("b96", H * QK), ("scan", 2 * S), ("freq", 1), ("eps", 4)):
    CST[_name] = NC
    NC += _n
M1, LEV = 4 * P, 8 * P
NM = LEV + 2 * (LEVELS - 1) * P
MAGIC = 1.5 * 2.0 ** 23
PI_IN = float(np.nextafter(np.float32(np.pi), np.float32(0)))


def two_pi_parts(n=4, bits=9):
    rest, parts = 2 * np.pi, []
    for _ in range(n):
        q = 2.0 ** (np.floor(np.log2(rest)) - bits + 1)
        parts.append(float(np.floor(rest / q) * q))
        rest -= parts[-1]
    return parts + [float(np.float32(rest))]


TWO_PI = two_pi_parts()
ROPE_STEPS = 4 + 2 * len(TWO_PI) + 3 + 2


def constants():
    c = np.zeros((P, NC), np.float32)

    def put(name, a):
        a = np.asarray(a, np.float32).reshape(a.shape[0], -1)
        c[:a.shape[0], CST[name]:CST[name] + a.shape[1]] = a

    i = np.arange(P)
    put("ident", np.eye(P))
    put("ones", np.ones((P, P)))
    put("mean64", (i[:, None] // HD == i[None] // HD) / HD)
    put("ident64", np.tile(np.eye(C), (2, 1)))
    rot = np.zeros((QK, QK))
    for m in range(ROPE // 2):
        rot[NOPE + ROPE // 2 + m, NOPE + m] = -1.0
        rot[NOPE + m, NOPE + ROPE // 2 + m] = 1.0
    put("rot", rot)
    es = np.zeros((P, RC, H))
    eb = np.zeros((H, RC, P))
    for j in range(RC):
        for p in range(P):
            es[p, j, 2 * j + p // HD] = 1
            eb[2 * j + p // HD, j, p] = 1
    put("es", es)
    put("eb", eb)
    e96 = np.zeros((QK, H, H))
    b96 = np.zeros((H, H, QK))
    for h in range(H):
        e96[:, h, h] = 1
        b96[h, h, :] = 1
    put("e96", e96)
    put("b96", b96)
    same = i[:, None] // C == i[None] // C
    lt = i[:, None] < i[None]
    tm = np.zeros((P, 2, 2, P))
    for d, m in enumerate((lt, lt.T)):
        tm[:, d, 0] = same & m
        tm[:, d, 1] = same & (m | np.eye(P, dtype=bool))
    
    m1 = np.zeros((P, 2, 2, P))
    lev = np.zeros((P, 2, LEVELS - 1, P))
    for n in range(LEVELS):
        h = 2 ** n
        block = (i[:, None] // (2 * h) == i[None] // (2 * h)) & (i[:, None] // h > i[None] // h)
        for d, m in enumerate((block, block.T)):
            if n == 0:
                m1[:, d, 0], m1[:, d, 1] = -1.0 * m, -1.0 * m.T
            else:
                lev[:, d, n - 1] = m
    masks = np.concatenate([v.reshape(P, -1) for v in (tm, m1, lev)], 1).astype(np.float32)
    sc = np.ones((P, 2, S))
    sc[:, 0, ::C] = 0
    sc[:, 1, C - 1::C] = 0
    put("scan", sc)
    freq = 10000.0 ** (-np.arange(0, ROPE, 2) / ROPE)
    f = np.zeros((P, 1))
    f[NOPE:QK, 0] = np.tile(freq, 2)
    put("freq", f)
    put("eps", np.tile(np.array([NORM_EPS, GN_EPS, LN_EPS, 0.0]), (P, 1)))
    return c, masks


PIECES = KC
FILL_A = {"latent squares": 8, "latents normed": 24, "k squares": 12, "k inverse": 10, "k normed": 8,
          "k turned": 24, "q inverse": 10, "q normed": 8, "q turned": 24}
FILL_A.update({("head", h): 8 for h in range(H)})
FILL_R = {"key sums": 8, "key inverse": 8, "values": 8, "cv mean": 8, "cv var": 8}
for _d in range(2):
    FILL_R.update({("lora", _d): 8, ("kr", _d): 20})
    for _h in range(0, H, 2):
        FILL_R.update({(_d, _h, "pairs"): 7})
        FILL_R.update({(_d, _h, _l, _i): 0 for _l in range(1, LEVELS) for _i in range(2)})
        FILL_R.update({(_d, _h, "x"): 3, (_d, _h, "o"): 2})
assert sum(FILL_A.values()) == PIECES * (T_BR - T_CV)
assert sum(FILL_R.values()) == PIECES * 2 * (RC + KC)


class Filling:

    def __init__(self, plan, work, unit):
        self.plan, self.work, self.unit, self.points, self.done = plan, work, unit, list(plan), 0
        self.pieces = 0

    def at(self, point):
        assert self.points.pop(0) == point, point
        self.pieces += self.plan[point]
        while self.done < self.pieces // self.unit:
            next(self.work)
            self.done += 1


class Steps:

    def __init__(self, sem, name, known):
        self.sem, self.name, self.known = sem, name, known
        self.now, self.n, self.layer = {}, 0, 0

    def mark(self, key):
        self.n += 1
        assert key not in self.now, key
        self.now[key] = self.n
        return self.sem, 1

    def at(self, key):
        if self.known is None:
            return self.sem, 1
        total, values = self.known[self.name]
        return self.sem, self.layer * total + values[key]

    def counted(self):
        return self.n, self.now


def program(nc, x, pos, stream, vecs, cst_in, msk_in, lora, wuq_in, wukv_in, out, known):
    ctx = ExitStack()
    with ctx:
        def sb(name, shape, dt=F):
            return ctx.enter_context(nc.sbuf_tensor(name, shape, dt))

        def sem(name):
            return ctx.enter_context(nc.semaphore(name))

        xT = sb("xT", [P, KC, S])
        h_hi = sb("h_hi", [P, KC, S], R)
        h_lo = sb("h_lo", [P, KC, S], R)
        raw = sb("raw", [P, RAW, D])
        whi = sb("whi", [P, HL, D], R)
        wlo = sb("wlo", [P, HL, D], R)
        u_hi = sb("u_hi", [P, RC, S], R)
        u_lo = sb("u_lo", [P, RC, S], R)
        c_hi = sb("c_hi", [P, RC, S], R)
        c_lo = sb("c_lo", [P, RC, S], R)
        g_hi, g_lo = u_hi[:, 0:2, :], u_lo[:, 0:2, :]
        gs = sb("gs", [P, 2, S])
        msk = sb("masks", [P, NM], BF)
        cst = sb("consts", [P, NC])
        vec_t = sb("vec_t", [P, NV])
        lo_w = sb("lo_w", [P, 4, RW])
        zero_b = sb("zero_b", [1, 512], BF)
        vfirst = sb("vfirst", [P, RC, S])
        cosT = sb("cosT", [P, S])
        sinT = sb("sinT", [P, S])
        ARENA = 24420
        arena = sb("arena", [P, ARENA])
        bank = [ctx.enter_context(nc.psum_tensor(f"bank{i}", [P, 512], F)) for i in range(8)]

        def view(at, *shape):
            n = int(np.prod(shape))
            assert at + n <= ARENA, (at, shape)
            v = arena[:, at:at + n]
            if len(shape) == 2:
                v = v.rearrange("p (a b) -> p a b", b=shape[1])
            elif len(shape) == 3:
                v = v.rearrange("p (a b c) -> p a b c", b=shape[1], c=shape[2])
            elif len(shape) == 4:
                v = v.rearrange("p (a b c d) -> p a b c d", b=shape[1], c=shape[2], d=shape[3])
            return v

        Q1 = RC * S
        r_, k_, v_ = view(0, RC, S), view(Q1, RC, S), view(2 * Q1, RC, S)
        wag = view(3 * Q1, 4, S)
        merged = view(4 * Q1, KC, S)
        pp = view(4 * Q1, 4, S + 2)
        pt = view(4 * Q1 + 4 * (S + 2), 4, S)
        M0 = 6 * Q1 + 16
        pos_i = view(M0 + 3 * Q1, S)
        ang = view(M0 + 3 * Q1 + S, 4, S)
        g_s, g_f = view(0, 2, S), view(2 * S, 2, S)
        sq = view(M0, KC, S)
        lat = view(M0, QC + KVC, S)
        rope_in = view(M0 + 5 * S, S)
        UP0 = M0 + 6 * S
        upad = view(UP0, RC, S + TAPS - 1)
        CVO = UP0 + RC * (S + TAPS - 1)
        cvo = view(CVO, RC, S)
        MB = CVO + Q1
        nrm = view(MB + 4 * Q1, 2, S)
        sq_lat = view(MB + 5 * Q1, QC + KVC, S)
        qf = view(MB, H, S)
        kf = view(MB + 2 * Q1, H, S)
        hs = view(MB + 4 * Q1, H, S)
        vm = view(MB + 6 * Q1, NT, RW)
        prob = view(MB + 4 * Q1, 2, 2, S)
        probT = view(MB + 5 * Q1, 2, 2, S)
        rn8 = view(MB + 7 * Q1, 2, S)
        wuq = view(MB + 7 * Q1 + 2 * S, QC, H * QK)
        W2 = MB + 7 * Q1 + 2 * S + QC * H * QK
        wukv = view(W2, KVC, H * (NOPE + 64))
        mx = view(W2 + 2048, 2, 4)
        cv_tmp = view(W2 + 2048 + 8, 2, S)
        cv_sq = view(MB, RC, S)
        cv_st = view(MB + Q1, 3, S)
        kk = view(M0, RC, S)
        kds = view(M0 + Q1, RC, S)
        osum = view(M0 + 2 * Q1, RC, S)
        vt = view(M0 + 3 * Q1, NT, RW)
        kr = view(M0 + 4 * Q1, RC, NT, 2, P)
        bt = view(M0 + 6 * Q1, RC, S)
        kt = view(M0 + 7 * Q1, RC, S)
        tk = view(M0 + 8 * Q1, 3, NT, RW)
        ptr = view(M0 + 11 * Q1, RC, NCH, C)
        qw = view(M0 + 12 * Q1, RC, NCH, HD)
        G0 = M0 + 13 * Q1
        wch = view(G0, RC, NCH)
        G1 = G0 + RC * NCH
        tA, tB, tC_, tD = (view(G1 + i * Q1, RC, S) for i in range(4))
        g1 = view(G1, 2, NT, 2, P)
        g2 = view(G1 + Q1, 2, NT, 2, P)
        mn = view(G1 + 2 * Q1, 2, 2, NT, P)
        zz = view(G1 + 3 * Q1, 2, NT, P)
        xs = view(G1 + 3 * Q1 + 512, 2, NT, HD)
        ys = view(G1 + 3 * Q1 + 768, 2, NT, HD)
        gv = view(G1 + 4 * Q1, 2, NT, HD)
        rn_rw = view(G1 + 4 * Q1 + 256, 2, S)
        tmp_s = view(G1, RC, HD)

        def cc(name, n, at=0, rows=P):
            o = CST[name] + at
            return cst[0:rows, o:o + n]

        def vv(name, i=0, a=0, b=P):
            o = VEC[name] + i
            return vec_t[a:b, o:o + 1]

        ident = cc("ident", P)

        raw_in = [sem(f"raw_in{i}") for i in range(RAW)]
        hi_ready = sem("hi_ready")
        lo_ready = sem("lo_ready")
        tile_used = sem("tile_used")
        consts_in = sem("consts_in")
        masks_in = sem("masks_in")
        x_in = sem("x_in")
        pos_in = sem("pos_in")
        x_ready = sem("x_ready")
        vec_in = sem("vec_in")
        lora_in = sem("lora_in")
        uk_in = sem("uk_in")
        zeros_set = sem("zeros_set")
        rope_v, rope_a = sem("rope_v"), sem("rope_a")
        sig_ready = sem("sig_ready")
        as_ready = sem("as_ready")
        g_ready = sem("g_ready")
        ghi_ready = sem("ghi_ready")
        glo_ready = sem("glo_ready")
        vec = Steps(sem("vector_step"), "vec", known)
        act = Steps(sem("scalar_step"), "act", known)
        ten = Steps(sem("tensor_step"), "ten", known)
        poo = Steps(sem("pool_step"), "poo", known)
        out_done = sem("out_done")

        settles = sem("settles")

        def settled(eng):
            eng.sem_inc(settles, 1)

        def layers(eng):
            loop = eng.Fori(0, DEPTH)
            L = loop.__enter__()
            for steps in (vec, act, ten, poo):
                steps.layer = L
            return loop, L

        block = ctx.enter_context(nc.Block())

        @block.sync
        def _(sp):
            def load(tile, s, n):
                sp.wait_ge(lo_ready, n + 1)
                sp.dma_start(raw[:, s, :], tile).then_inc(raw_in[s], 16)

            sp.dma_start(xT[:, :, :], x).then_inc(x_in, 16)
            sp.dma_start(cst[:, :], cst_in).then_inc(consts_in, 16)
            with sp.Fori(0, DEPTH * TILES // RAW) as g:
                for s in range(RAW):
                    load(stream[g * RAW + s], s, g * RAW + s)
            for s in range(HL):
                load(stream[DEPTH * TILES + s], s, DEPTH * TILES + s)
            sp.wait_ge(*((vec.sem, 1) if known is None else (vec.sem, DEPTH * known["vec"][0])))
            sp.dma_start(out, xT[:, :, :]).then_inc(out_done, 16)
            sp.wait_ge(out_done, 16)

        @block.gpsimd
        def _(pool):
            pool.dma_start(vec_t[:, :], vecs[0]).then_inc(vec_in, 16)
            pool.dma_start(pos_i.bitcast(mybir.dt.int32), pos).then_inc(pos_in, 16)
            pool.dma_start(arena[:, 2048:2048 + NM], msk_in).then_inc(masks_in, 16)
            pool.dma_start(lo_w[:, :, :], lora[0]).then_inc(lora_in, 16)
            pool.dma_start(wuq, wuq_in[0]).then_inc(uk_in, 16)
            pool.dma_start(wukv, wukv_in[0]).then_inc(uk_in, 16)
            nc.gpsimd.memset(vfirst[:, :, :], 0.0).then_inc(zeros_set, 1)
            nc.gpsimd.memset(zero_b[:, :], 0.0).then_inc(zeros_set, 1)
            pool.wait_ge(pos_in, 16)
            pool.wait_ge(consts_in, 16)
            steps = [0]
            G = nc.gpsimd

            def chain(ins):
                steps[0] += 1
                ins.then_inc(rope_v, 1)
                pool.wait_ge(rope_v, steps[0])

            chain(G.tensor_copy(ang[:, 2, :], pos_i.bitcast(mybir.dt.int32)))
            chain(G.tensor_scalar(ang[:, 0, :], ang[:, 2, :], cc("freq", 1), None, ALU.mult))
            chain(G.tensor_scalar(ang[:, 3, :], ang[:, 0, :], 1.0 / (2 * np.pi), MAGIC, ALU.mult, ALU.add))
            chain(G.tensor_scalar(ang[:, 3, :], ang[:, 3, :], MAGIC, None, ALU.subtract))
            for part in TWO_PI:
                chain(G.tensor_scalar(ang[:, 2, :], ang[:, 3, :], -part, None, ALU.mult))
                chain(G.tensor_tensor(ang[:, 0, :], ang[:, 0, :], ang[:, 2, :], ALU.add))
            chain(G.tensor_scalar(ang[:, 1, :], ang[:, 0, :], float(np.pi / 2), None, ALU.add))
            chain(G.tensor_scalar(ang[:, 3, :], ang[:, 1, :], float(np.pi), float(-2 * np.pi), ALU.is_gt, ALU.mult))
            chain(G.tensor_tensor(ang[:, 1, :], ang[:, 1, :], ang[:, 3, :], ALU.add))
            for i in range(2):
                chain(G.tensor_scalar(ang[:, i, :], ang[:, i, :], PI_IN, -PI_IN, ALU.min, ALU.max))
            assert steps[0] == ROPE_STEPS
            loop, L = layers(pool)
            pool.wait_ge(*vec.at(("h lo", 1, KC - 1)))
            settled(pool)
            nc.gpsimd.memset(upad[:, :, 0:HALF], 0.0).then_inc(*poo.mark("pad left"))
            nc.gpsimd.memset(upad[:, :, HALF + S:], 0.0).then_inc(*poo.mark("pad right"))
            for c in range(2, 4):
                pool.wait_ge(*vec.at(("glu", c)))
                if c == 2:
                    pool.wait_ge(vec_in, L * 16 + 16)
                settled(pool)
                for t in range(TAPS):
                    w = vv("cv_w", c * TAPS + t)
                    src = upad[:, c, t:t + S]
                    if t == 0:
                        if c == 2:
                            pool.wait_ge(*poo.at("pad left"))
                            pool.wait_ge(*poo.at("pad right"))
                            settled(pool)
                        nc.gpsimd.tensor_scalar(cvo[:, c, :], src, w, vv("cv_b", c), ALU.mult, ALU.add)\
                            .then_inc(*poo.mark(("conv", c, 0)))
                    else:
                        nc.gpsimd.tensor_scalar(cv_tmp[:, t % 2, :], src, w, None, ALU.mult)\
                            .then_inc(*poo.mark(("tap", c, t)))
                        pool.wait_ge(*poo.at(("tap", c, t)))
                        nc.gpsimd.tensor_tensor(cvo[:, c, :], cvo[:, c, :], cv_tmp[:, t % 2, :], ALU.add)\
                            .then_inc(*poo.mark(("conv", c, t)))
            pool.wait_ge(*ten.at("norm 2"))
            pool.wait_ge(*vec.at(("h", 2, KC - 1)))
            pool.dma_start(vec_t[:, :], vecs[L + 1]).then_inc(vec_in, 16)
            pool.dma_start(lo_w[:, :, :], lora[L + 1]).then_inc(lora_in, 16)
            pool.dma_start(wuq, wuq_in[L + 1]).then_inc(uk_in, 16)
            pool.dma_start(wukv, wukv_in[L + 1]).then_inc(uk_in, 16)
            loop.__exit__(None, None, None)
            pool.wait_ge(vec_in, (DEPTH + 1) * 16)
            pool.wait_ge(lora_in, (DEPTH + 1) * 16)
            pool.wait_ge(uk_in, (DEPTH + 1) * 32)

        @block.tensor
        def _(pe):
            TE = nc.tensor

            def products(o, wh, wl, hi, lo, first, last, **kw):
                TE.matmul(o, wh, hi, start=first, stop=False, **kw)
                TE.matmul(o, wh, lo, start=False, stop=False, **kw)
                return TE.matmul(o, wl, hi, start=False, stop=last, **kw)

            def col_tile(n, slot, o, hi, lo):
                pe.wait_ge(lo_ready, n + 1 + RAW)
                for k in range(KC):
                    last = products(o, whi[:, slot, k * P:(k + 1) * P], wlo[:, slot, k * P:(k + 1) * P],
                                    hi[:, k, :], lo[:, k, :], k == 0, k == KC - 1)
                last.then_inc(tile_used, 1)

            def row_tile(n, slot, hi, lo, first):
                pe.wait_ge(lo_ready, n + 1 + RAW)
                for m in range(KC):
                    last = products(bank[m // 2][:, (m % 2) * S:(m % 2 + 1) * S],
                                    whi[:, slot, m * P:(m + 1) * P], wlo[:, slot, m * P:(m + 1) * P],
                                    hi, lo, first and m % 2 == 0, False, skip_group_check=True)
                last.then_inc(tile_used, 1)

            pe.wait_ge(consts_in, 16)
            pe.wait_ge(zeros_set, 2)
            for _ in range(HL):
                TE.matmul(bank[7][:, 0:P], zero_b[0:1, 0:P], zero_b[0:1, 0:P], start=True, stop=True)\
                    .then_inc(tile_used, 1)
            loop, L = layers(pe)

            def norm(i):
                pe.wait_ge(*act.at(("squares", i)))
                if i == 1:
                    pe.wait_ge(*vec.at(("residual", 0, 3)))
                for k in range(KC):
                    m = TE.matmul(bank[6][:, 0:S], cc("ones", P), sq[:, k, :], start=k == 0, stop=k == KC - 1)
                m.then_inc(*ten.mark(f"norm {i}"))

            def ffn(f, tile0):
                base = (2 * L + f) * NFF
                t0 = L * TILES + tile0

                def up(j, s, n, slot):
                    pe.wait_ge(g_ready, base + j + 1)
                    for half in range(2):
                        col_tile(t0 + n + half, (slot + half) % HL, bank[4 + s][:, half * S:(half + 1) * S],
                                 h_hi, h_lo)

                def down(j, s, n, slot):
                    pe.wait_ge(glo_ready, base + j + 1)
                    row_tile(t0 + n, slot % HL, g_hi[:, s, :], g_lo[:, s, :], False)

                pe.wait_ge(*vec.at(("h lo", 2 * f, KC - 1)))
                for b in range(4):
                    TE.matmul(bank[b][:, :], zero_b[0:1, 0:P], zero_b[0:1, :], start=True, stop=True)
                up(0, 0, 0, tile0)
                with pe.Fori(0, (NFF - 2) // 2) as it:
                    for q in range(2):
                        n = it * LOOP + (2 + 3 * q)
                        up(it * 2 + (q + 1), (q + 1) % 2, n, tile0 + 2 + 3 * q)
                        down(it * 2 + q, q, n + 2, tile0 + 4 + 3 * q)
                up(NFF - 1, 1, 3 * NFF - 4, tile0 + 3 * NFF - 4)
                down(NFF - 2, 0, 3 * NFF - 2, tile0 + 3 * NFF - 2)
                down(NFF - 1, 1, 3 * NFF - 1, tile0 + 3 * NFF - 1)

            norm(0)
            ffn(0, T_FFN1)
            norm(1)

            pe.wait_ge(*vec.at(("h lo", 1, KC - 1)))
            for i in range(N_MLA):
                n = T_MLA + i
                col_tile(L * TILES + n, n % HL, bank[i][:, 0:S], h_hi, h_lo)

            def tile_pieces(n, o, banks_free=None):
                pe.wait_ge(lo_ready, L * TILES + n + 1 + RAW)
                for k in range(KC):
                    last = products(o, whi[:, n % HL, k * P:(k + 1) * P], wlo[:, n % HL, k * P:(k + 1) * P],
                                    h_hi[:, k, :], h_lo[:, k, :], k == 0, k == KC - 1)
                    if k == KC - 1:
                        last.then_inc(tile_used, 1)
                    yield

            def fill_a():
                for n in range(T_CV, T_BR):
                    if n >= T_CV + 2:
                        val = n - 2 < T_RW and (n - 2 - T_CV) % 2 == 0
                        pe.wait_ge(*(vec.at(("glu", (n - 2 - T_CV) // 2)) if val else act.at(("column", n - 2))))
                    yield from tile_pieces(n, bank[6 + (n - T_CV) % 2][:, 0:S])

            def branch_pieces(order, b, bank0, nb, hi, lo):
                t0 = T_BR + order * (RC + KC)
                for c in range(0, KC, 2):
                    n = t0 + 3 * (c // 2)
                    pe.wait_ge(lo_ready, L * TILES + n + 1 + RAW)
                    for e in range(2):
                        back = KC * order + c + e - nb
                        if back >= 0:
                            pe.wait_ge(*vec.at(("merge", BRANCH_ORDER[back // KC], back % KC)))
                        for k in range(RC):
                            w = slice((RC * e + k) * P, (RC * e + k + 1) * P)
                            last = products(bank[bank0 + (c + e) % nb][:, 0:S], whi[:, n % HL, w], wlo[:, n % HL, w],
                                            hi[:, k, :], lo[:, k, :], k == 0, k == RC - 1)
                            if e == 1 and k == RC - 1:
                                last.then_inc(tile_used, 1)
                            yield
                    for e in range(2):
                        yield from tile_pieces(n + 1 + e, bank[bank0 + (c + e) % nb][:, S:2 * S])

            def fill_r():
                pe.wait_ge(*act.at(("column", T_VD - 1)))
                pe.wait_ge(*act.at(("column", T_VD)))
                pe.wait_ge(*vec.at(("u", 2, RC - 1)))
                yield from branch_pieces(0, 2, 6, 2, u_hi, u_lo)
                pe.wait_ge(*vec.at(("u", 1, RC - 1)))
                yield from branch_pieces(1, 1, 6, 2, c_hi, c_lo)

            fa = Filling(FILL_A, fill_a(), 1)
            fr = Filling(FILL_R, fill_r(), 1)

            fa.at("latent squares")
            pe.wait_ge(*act.at("latent squares"))
            for a, b, o in ((0, QC, 0), (QC, QC + KVC, S)):
                for c in range(a, b):
                    m = TE.matmul(bank[0][:, o:o + S], cc("ones", P), sq_lat[:, c, :], start=c == a, stop=c == b - 1)
            m.then_inc(*ten.mark("latent norms"))
            fa.at("latents normed")
            pe.wait_ge(*vec.at("latents normed"))
            pe.wait_ge(uk_in, L * 32 + 32)
            for h in range(H):
                for c in range(KVC):
                    m = TE.matmul(bank[2 + h // 2][0:NOPE, (h % 2) * S:(h % 2 + 1) * S],
                                  wukv[:, c, h * 128:h * 128 + NOPE], lat[:, QC + c, :],
                                  start=c == 0, stop=c == KVC - 1)
                if h % 2:
                    m.then_inc(*ten.mark(("k", h // 2)))
            for h in range(H):
                if h % 2 == 0:
                    pe.wait_ge(*act.at(("k", h // 2)))
                for c in range(QC):
                    m = TE.matmul(bank[2 + h // 2][0:QK, (h % 2) * S:(h % 2 + 1) * S],
                                  wuq[:, c, h * QK:(h + 1) * QK], lat[:, c, :],
                                  start=c == 0, stop=c == QC - 1)
                if h % 2:
                    m.then_inc(*ten.mark(("q", h // 2)))
            wv = wukv.rearrange("p c (h n) -> p c h n", n=128)
            for t in range(NT):
                for c in range(KVC):
                    m = TE.matmul(bank[t][:, :], lat[:, QC + c, t * P:(t + 1) * P],
                                  wv[:, c, :, NOPE:], start=c == 0, stop=c == KVC - 1)
                m.then_inc(*ten.mark(("v", t)))
            for w in ("k", "q"):
                fa.at("k squares" if w == "k" else "k turned")
                pe.wait_ge(*act.at(f"{w} squares"))
                if w == "k":
                    pe.wait_ge(*act.at(("v", NT - 1)))
                    pe.wait_ge(*act.at(("q", 3)))
                else:
                    pe.wait_ge(*vec.at("k turned"))
                for h in range(H):
                    m = TE.matmul(bank[0][0:H, 0:S], cc("e96", H, h * H, QK), hs[0:QK, h, :],
                                  start=h == 0, stop=h == H - 1)
                m.then_inc(*ten.mark(f"{w} sums"))
                fa.at(f"{w} inverse")
                pe.wait_ge(*vec.at(f"{w} inverse"))
                for h in range(H):
                    m = TE.matmul(bank[1 + h // 2][0:QK, (h % 2) * S:(h % 2 + 1) * S],
                                  cc("b96", QK, h * QK, H), rn8[0:H, 0, :], start=True, stop=True)
                m.then_inc(*ten.mark(f"{w} spread"))
                fa.at(f"{w} normed")
                pe.wait_ge(*vec.at(f"{w} normed"))
                src = kf if w == "k" else qf
                for g in range(4):
                    m = TE.matmul(bank[1 + g][0:QK, :], cc("rot", QK, 0, QK), src[0:QK, 2 * g:2 * g + 2, :],
                                  start=True, stop=True)
                m.then_inc(*ten.mark(f"{w} rotated"))
            fa.at("q turned")
            pe.wait_ge(*vec.at("q turned"))

            def scores(h):
                if h >= 2:
                    pe.wait_ge(*act.at(("exp", h - 2, 1)))
                for t in range(NT):
                    m = TE.matmul(bank[5 * (h % 2)][:, t * S:(t + 1) * S], qf[0:QK, h, t * P:(t + 1) * P],
                                  kf[0:QK, h, :], start=True, stop=True)
                m.then_inc(*ten.mark(("scores", h)))

            def mix(h):
                pe.wait_ge(*vec.at(("prob", h, 1)))
                if h >= 2:
                    pe.wait_ge(*act.at(("probT", h - 2)))
                for t in range(NT):
                    for b in range(NT):
                        m = TE.transpose(bank[1 + h % 2][:, b * S + t * P:b * S + (t + 1) * P],
                                         prob[:, h % 2, t, b * P:(b + 1) * P], ident)
                m.then_inc(*ten.mark(("probT", h)))
                pe.wait_ge(*act.at(("probT", h)))
                if h >= 4 and h % 2 == 0:
                    pe.wait_ge(*vec.at(("u", 2, h // 2 - 2)))
                r = HD * (h % 2)
                for b in range(NT):
                    m = TE.matmul(bank[3 + (h // 2) % 2][r:r + HD, 0:S], vm[:, b, h * HD:(h + 1) * HD],
                                  probT[:, h % 2, b, :], start=b == 0, stop=b == NT - 1)
                m.then_inc(*ten.mark(("attended", h)))

            scores(0)
            for h in range(H):
                if h + 1 < H:
                    scores(h + 1)
                fa.at(("head", h))
                mix(h)

            pe.wait_ge(*vec.at(("u", 2, RC - 1)))
            fr.at("key sums")
            pe.wait_ge(*act.at("key squares"))
            for j in range(RC):
                m = TE.matmul(bank[4][0:H, 0:S], cc("es", H, j * H), tA[:, j, :], start=j == 0, stop=j == RC - 1)
            m.then_inc(*ten.mark("key sums"))
            fr.at("key inverse")
            pe.wait_ge(*act.at(("column", T_VD)))
            for c in range(RC):
                m = TE.matmul(bank[c // 2][:, (c % 2) * S:(c % 2 + 1) * S], lo_w[0:32, 3, c * P:(c + 1) * P],
                              wag[0:32, 3, :], start=True, stop=True)
            m.then_inc(*ten.mark("nu"))
            pe.wait_ge(*vec.at("key inverse"))
            for j in range(RC):
                m = TE.matmul(bank[2 + j // 2][:, (j % 2) * S:(j % 2 + 1) * S], cc("eb", P, j * P, H),
                              rn_rw[0:H, 0, :], start=True, stop=True)
            m.then_inc(*ten.mark("key spread"))
            fr.at("values")
            pe.wait_ge(*vec.at(("conv", 1, TAPS - 1)))
            pe.wait_ge(*poo.at(("conv", 3, TAPS - 1)))
            pe.wait_ge(*act.at("key rms"))
            for c in range(RC):
                m = TE.matmul(bank[4][:, 0:S], cc("ones", P), cvo[:, c, :], start=c == 0, stop=c == RC - 1)
            m.then_inc(*ten.mark("cv mean"))
            fr.at("cv mean")
            pe.wait_ge(*act.at("cv squares"))
            for c in range(RC):
                m = TE.matmul(bank[5][:, 0:S], cc("ones", P), cv_sq[:, c, :], start=c == 0, stop=c == RC - 1)
            m.then_inc(*ten.mark("cv var"))
            fr.at("cv var")
            pe.wait_ge(*vec.at("values"))
            pe.wait_ge(*vec.at(("u", 1, RC - 1)))
            for t in range(NT):
                for c in range(RC):
                    m = TE.transpose(bank[4 + t][:, c * P:(c + 1) * P], v_[:, c, t * P:(t + 1) * P], ident)
            m.then_inc(*ten.mark("vt"))

            for d in range(2):
                pe.wait_ge(*act.at("wag"))
                if d == 0:
                    pe.wait_ge(*vec.at("kk"))
                    pe.wait_ge(*act.at("vt"))
                    pe.wait_ge(*act.at("nu"))
                else:
                    pe.wait_ge(*vec.at(("osum", 0)))
                for b0, col in ((0, 0), (2, 1)):
                    for c in range(RC):
                        m = TE.matmul(bank[b0 + c // 2][:, (c % 2) * S:(c % 2 + 1) * S],
                                      lo_w[HD * d:HD * d + HD, col, c * P:(c + 1) * P],
                                      wag[HD * d:HD * d + HD, col, :], start=True, stop=True)
                    m.then_inc(*ten.mark(("lora", d, col)))
                fr.at(("lora", d))
                fr.at(("kr", d))
                pe.wait_ge(*vec.at(("kr", d)))
                pe.wait_ge(*vec.at(("bt", d)))
                pe.wait_ge(*vec.at(("kt", d)))
                if d == 0:
                    pe.wait_ge(*vec.at("kk"))
                pe.wait_ge(*act.at(("icl", d)))
                pe.wait_ge(*act.at(("sw", d)))
                for i in range(3):
                    for t in range(NT):
                        q = i * NT + t
                        for c in range(RC):
                            src = (kr[:, c, t, 0, :], bt[:, c, t * P:(t + 1) * P], kt[:, c, t * P:(t + 1) * P])[i]
                            m = TE.transpose(bank[q][:, c * P:(c + 1) * P], src, ident)
                        m.then_inc(*ten.mark(("tk", d, q)))
                pe.wait_ge(*act.at(("tk", d, 5)))
                for h0 in range(0, H, 2):
                    pair = (h0, h0 + 1)
                    bk = {h: [bank[3 * (h % 2) + i] for i in (0, 1, 2, 0)] for h in pair}
                    if h0:
                        for h in pair:
                            pe.wait_ge(*vec.at(("qw", d, h - 2)))
                            pe.wait_ge(*vec.at(("o", d, h - 2)))
                    for h in pair:
                        r, j = HD * (h % 2), h // 2
                        for t in range(NT):
                            TE.matmul(bk[h][0][:, t * S:(t + 1) * S], bt[r:r + HD, j, t * P:(t + 1) * P],
                                      kr[r:r + HD, j, t, :, :], start=True, stop=True)
                        for t in range(NT):
                            TE.matmul(bk[h][1][:, t * S:(t + 1) * S], kt[r:r + HD, j, t * P:(t + 1) * P],
                                      kr[r:r + HD, j, t, :, :], start=True, stop=True)
                        for t in range(NT):
                            m = TE.matmul(bk[h][2][:, t * P:(t + 1) * P], kr[r:r + HD, j, t, 0, :],
                                          bt[r:r + HD, j, t * P:(t + 1) * P], start=True, stop=True)
                        m.then_inc(*ten.mark(("pairs", d, h)))
                    fr.at((d, h0, "pairs"))
                    for lv in range(1, LEVELS):
                        fr.at((d, h0, lv, 0))
                        for h in pair:
                            s = h % 2
                            pe.wait_ge(*vec.at(("mn", d, h, lv - 1)))
                            for t in range(NT):
                                m = TE.matmul(bk[h][2][:, t * P:(t + 1) * P], g1[:, s, t, 0, :], mn[:, s, 0, t, :],
                                              start=True, stop=True)
                            m.then_inc(*ten.mark(("z", d, h, lv)))
                        fr.at((d, h0, lv, 1))
                        for h in pair:
                            s = h % 2
                            pe.wait_ge(*vec.at(("z", d, h, lv)))
                            for t in range(NT):
                                if lv < LEVELS - 1:
                                    TE.matmul(bk[h][3][:, t * P:(t + 1) * P], mn[:, s, 1, t, :], zz[:, s, t, :],
                                              start=True, stop=True)
                                m = TE.matmul(bk[h][3][:, S + t * P:S + (t + 1) * P], zz[:, s, t, :],
                                              mn[:, s, 1, t, :], start=True, stop=True)
                            m.then_inc(*ten.mark(("mz", d, h, lv)))
                    for h in pair:
                        s = h % 2
                        for t in range(NT):
                            m = TE.matmul(bk[h][2][:, S + t * HD:S + (t + 1) * HD], g2[:, s, t, 0, :],
                                          vt[:, t, h * HD:(h + 1) * HD], start=True, stop=True)
                        m.then_inc(*ten.mark(("gv", d, h)))
                    for h in pair:
                        s = h % 2
                        pe.wait_ge(*vec.at(("mn", d, h, LEVELS - 1)))
                        pe.wait_ge(*act.at(("gv", d, h)))
                        for t in range(NT):
                            TE.matmul(bk[h][3][:, t * HD:(t + 1) * HD], mn[:, s, 1, t, :],
                                      tk[:, 0, t, h * HD:(h + 1) * HD], start=True, stop=True)
                        for t in range(NT):
                            m = TE.matmul(bk[h][3][:, P + t * HD:P + (t + 1) * HD], mn[:, s, 1, t, :],
                                          gv[:, s, t, :], start=True, stop=True)
                        m.then_inc(*ten.mark(("xy", d, h)))
                    fr.at((d, h0, "x"))
                    for h in pair:
                        pe.wait_ge(*act.at(("x", d, h)))
                    for t in range(NT):
                        for h in pair:
                            s, r = h % 2, HD * (h % 2)
                            m = TE.matmul(bk[h][2][r:r + HD, t * P:(t + 1) * P], xs[:, s, t, :], g1[:, s, t, 1, :],
                                          start=True, stop=True)
                            if t == NT - 1:
                                m.then_inc(*ten.mark(("rx", d, h)))
                    for h in pair:
                        pe.wait_ge(*act.at(("y", d, h)))
                    for t in range(NT):
                        for h in pair:
                            s, r = h % 2, HD * (h % 2)
                            TE.matmul(bk[h][0][r:r + HD, t * P:(t + 1) * P], vt[:, t, h * HD:(h + 1) * HD],
                                      g2[:, s, t, 1, :], start=True, stop=False)
                        for h in pair:
                            s, r = h % 2, HD * (h % 2)
                            m = TE.matmul(bk[h][0][r:r + HD, t * P:(t + 1) * P], ys[:, s, t, :], g1[:, s, t, 1, :],
                                          start=False, stop=True)
                            if t == NT - 1:
                                m.then_inc(*ten.mark(("o", d, h)))
                    fr.at((d, h0, "o"))
                    for half in range(2):
                        q = HD * half
                        if half:
                            for h in pair:
                                pe.wait_ge(*vec.at(("rx", d, h)))
                            settled(pe)
                        for t in range(NT):
                            for h in pair:
                                s, r = h % 2, HD * (h % 2)
                                TE.matmul(bk[h][1 + half][r:r + HD, t * C:(t + 1) * C], xs[q:q + HD, s, t, :],
                                          tk[q:q + HD, 1, t, h * HD:(h + 1) * HD], start=True, stop=True)
                        for t in range(NT):
                            for h in pair:
                                s, r = h % 2, HD * (h % 2)
                                TE.matmul(bk[h][1 + half][r:r + HD, P + t * HD:P + (t + 1) * HD],
                                          tk[q:q + HD, 2, t, h * HD:(h + 1) * HD],
                                          vt[q:q + HD, t, h * HD:(h + 1) * HD], start=True, stop=False)
                            for h in pair:
                                s, r = h % 2, HD * (h % 2)
                                m = TE.matmul(bk[h][1 + half][r:r + HD, P + t * HD:P + (t + 1) * HD],
                                              tk[q:q + HD, 1, t, h * HD:(h + 1) * HD], ys[q:q + HD, s, t, :],
                                              start=False, stop=True)
                                if half and t == NT - 1:
                                    m.then_inc(*ten.mark(("pq", d, h)))
                chunks = range(NCH) if d == 0 else range(NCH - 1, -1, -1)
                pe.wait_ge(*vec.at(("qw", d, H - 1)))
                pe.wait_ge(*vec.at(("o", d, H - 1)))
                pe.wait_ge(*vec.at(("qw", d, H - 2)))
                pe.wait_ge(*vec.at(("o", d, H - 2)))
                for i in (1, 2):
                    c, before = chunks[i], chunks[i - 1]
                    if i == 2:
                        pe.wait_ge(*vec.at(("state", d, 1, 1)))
                    settled(pe)
                    for h in range(H):
                        r, j = HD * (h % 2), h // 2
                        m = TE.matmul(bank[h % 2][r:r + HD, j * HD:(j + 1) * HD], ptr[r:r + HD, j, c, :],
                                      qw[r:r + HD, j, before, :], start=True, stop=True)
                    m.then_inc(*ten.mark(("state", d, i)))
                pe.wait_ge(*vec.at(("state", d, 2, 1)))
                settled(pe)
                for i in (1, 2, 3):
                    c, before = chunks[i], chunks[i - 1]
                    for h in range(H):
                        r, j = HD * (h % 2), h // 2
                        m = TE.matmul(bank[2 + h % 2 + 2 * (j // 2)][r:r + HD, (j % 2) * S + c * C:(j % 2) * S + (c + 1) * C],
                                      qw[r:r + HD, j, before, :], kr[r:r + HD, j, c // 2, 1, (c % 2) * C:(c % 2 + 1) * C],
                                      start=True, stop=True)
                m.then_inc(*ten.mark(("inter", d)))

            pe.wait_ge(*vec.at(("osum", 1)))
            pe.wait_ge(*vec.at("bonus terms"))
            for b in range(2):
                m = TE.matmul(bank[b][:, :], cc("mean64", P), osum[:, 2 * b:2 * b + 2, :], start=True, stop=True)
            m.then_inc(*ten.mark("gn mean"))
            for b in range(2):
                m = TE.matmul(bank[6 + b][:, :], cc("mean64", P), tA[:, 2 * b:2 * b + 2, :], start=True, stop=True)
            m.then_inc(*ten.mark("bonus"))
            for c in range(RC):
                m = TE.matmul(bank[2 + c // 2][:, (c % 2) * S:(c % 2 + 1) * S], lo_w[:, 2, c * P:(c + 1) * P],
                              wag[:, 2, :], start=True, stop=True)
            m.then_inc(*ten.mark("g"))
            pe.wait_ge(*act.at("gn squares"))
            for j in range(RC):
                m = TE.matmul(bank[4][0:H, 0:S], cc("es", H, j * H), tB[:, j, :], start=j == 0, stop=j == RC - 1)
            m.then_inc(*ten.mark("gn sums"))
            pe.wait_ge(*vec.at("gn inverse"))
            for j in range(RC):
                m = TE.matmul(bank[j // 2][:, (j % 2) * S:(j % 2 + 1) * S], cc("eb", P, j * P, H),
                              rn_rw[0:H, 1, :], start=True, stop=True)
            m.then_inc(*ten.mark("gn spread"))
            pe.wait_ge(*vec.at(("u", 0, RC - 1)))
            for _ in branch_pieces(2, 0, 4, 4, u_hi, u_lo):
                pass

            pe.wait_ge(*vec.at(("m lo", KC - 1)))
            pe.wait_ge(*act.at(("gate", 0, KC - 1)))
            for c in range(KC):
                if c >= 4:
                    pe.wait_ge(*vec.at(("x mixed", c - 4)))
                n = T_WO + c
                col_tile(L * TILES + n, n % HL, bank[4 + c % 4][:, 0:S], h_hi, h_lo)
            pe.wait_ge(*vec.at(("x mixed", KC - 1)))
            norm(2)
            ffn(1, T_FFN2)
            for n in range(T_END, TILES):
                pe.wait_ge(lo_ready, L * TILES + n + 1 + RAW)
                TE.matmul(bank[7][:, 0:P], zero_b[0:1, 0:P], zero_b[0:1, 0:P], start=True, stop=True)\
                    .then_inc(tile_used, 1)
            loop.__exit__(None, None, None)

        @block.scalar
        def _(sc):
            SE = nc.scalar

            def hi(L, it, m):
                sc.wait_ge(raw_in[m % RAW], (L * (TILES // RAW) + it * (LOOP // RAW) + (m // RAW + 1)) * 16)
                sc.wait_ge(tile_used, L * TILES + it * LOOP + (m + 1))
                SE.copy(whi[:, m % HL, :], raw[:, m % RAW, :]).then_inc(hi_ready, 1)

            for m in range(HL):
                hi(0, 0, m)
            sc.wait_ge(rope_v, ROPE_STEPS)
            SE.activation(sinT[:, :], ang[:, 0, :], ACT.Sin).then_inc(rope_a, 1)
            SE.activation(cosT[:, :], ang[:, 1, :], ACT.Sin).then_inc(rope_a, 1)
            SE.preload_act_table(ACT.Sigmoid)
            loop, L = layers(sc)

            def used(n):
                sc.wait_ge(tile_used, L * TILES + n + 1 + HL)

            def norm(i):
                if i:
                    sc.wait_ge(*(vec.at(("residual", 0, 3) if i == 1 else ("x mixed", KC - 1))))
                else:
                    sc.wait_ge(x_ready, L + 1)
                SE.activation(sq, xT[:, :, :], ACT.Square).then_inc(*act.mark(("squares", i)))
                sc.wait_ge(*ten.at(f"norm {i}"))
                SE.activation(nrm[:, 0, :], bank[6][:, 0:S], ACT.Sqrt, bias=cc("eps", 1, 0), scale=1.0 / D)\
                    .then_inc(*act.mark(("rms", i)))
                SE.preload_act_table(ACT.Sigmoid)
                for c in range(KC):
                    sc.wait_ge(*vec.at(("h", i, c)))
                    SE.copy(h_hi[:, c, :], sq[:, c, :]).then_inc(*act.mark(("h hi", i, c)))

            def ffn(f, tile0):
                def chunk(it, j, s, m, down):
                    base = (2 * L + f) * NFF
                    hi(L, it, m + HL)
                    sc.wait_ge(tile_used, L * TILES + it * LOOP + (m + 2 + HL))
                    SE.activation(g_s[:, s, :], bank[4 + s][:, 0:S], ACT.Sigmoid).then_inc(sig_ready, 1)
                    hi(L, it, m + 1 + HL)
                    sc.wait_ge(g_ready, base + j + 3)
                    SE.copy(g_hi[:, s, :], g_f[:, s, :]).then_inc(ghi_ready, 1)
                    if down:
                        hi(L, it, m + 2 + HL)

                chunk(0, 0, 0, tile0, False)
                with sc.Fori(0, (NFF - 2) // 2) as it:
                    for q in range(2):
                        chunk(it, it * 2 + (q + 1), (q + 1) % 2, tile0 + 2 + 3 * q, True)
                chunk(0, NFF - 1, 1, tile0 + 3 * NFF - 4, True)
                hi(L, 0, tile0 + 3 * NFF - 1 + HL)

            norm(0)
            ffn(0, T_FFN1)
            norm(1)
            for i in range(N_MLA):
                n = T_MLA + i
                used(n)
                if i < QC + KVC:
                    SE.copy(lat[:, i, :], bank[i][:, 0:S]).then_inc(*act.mark(("column", n)))
                else:
                    SE.copy(rope_in[NOPE:QK, :], bank[i][NOPE:QK, 0:S]).then_inc(*act.mark(("column", n)))
                hi(L, 0, n + HL)

            def fill_a():
                for n in range(T_CV, T_BR):
                    src = bank[6 + (n - T_CV) % 2]
                    used(n)
                    if n < T_RW:
                        if (n - T_CV) % 2:
                            c = (n - T_CV) // 2
                            if c >= 2:
                                sc.wait_ge(*vec.at(("glu", c - 2)))
                            SE.activation(gs[:, c % 2, :], src[:, 0:S], ACT.Sigmoid).then_inc(*act.mark(("column", n)))
                    elif n < T_VD:
                        i = n - T_RW
                        sc.wait_ge(*(vec.at(("mixed", i // 4 - 1) if i >= 4 else "pp edges")))
                        SE.copy(pp[:, i % 4, 1:S + 1], src[:, 0:S]).then_inc(*act.mark(("column", n)))
                    else:
                        sc.wait_ge(*vec.at(("mixed", 3)))
                        SE.copy(wag[0:32, 3, :], src[0:32, 0:S]).then_inc(*act.mark(("column", n)))
                    hi(L, 0, n + HL)
                    yield

            def branch_tiles(order, b, bank0, nb):
                t0 = T_BR + order * (RC + KC)
                for c in range(0, KC, 2):
                    n = t0 + 3 * (c // 2)
                    hi(L, 0, n + HL)
                    yield
                    for e in range(2):
                        back = KC * order + c + e - 2
                        sc.wait_ge(*(vec.at(("merge", BRANCH_ORDER[back // KC], back % KC) if back >= 0 else ("glu", RC + back))))
                        used(n + 1 + e)
                        SE.activation(gs[:, e, :], bank[bank0 + (c + e) % nb][:, S:2 * S], ACT.Sigmoid)\
                            .then_inc(*act.mark(("gate", b, c + e)))
                        hi(L, 0, n + 1 + e + HL)
                        yield

            def fill_r():
                yield from branch_tiles(0, 2, 6, 2)
                yield from branch_tiles(1, 1, 6, 2)

            fa = Filling(FILL_A, fill_a(), PIECES)
            fr = Filling(FILL_R, fill_r(), PIECES)

            sc.wait_ge(*act.at(("column", T_MLA + QC + KVC - 1)))
            SE.activation(sq_lat, lat, ACT.Square).then_inc(*act.mark("latent squares"))
            fa.at("latent squares")
            sc.wait_ge(*ten.at("latent norms"))
            SE.activation(nrm[:, 0, :], bank[0][:, 0:S], ACT.Sqrt, bias=cc("eps", 1, 0), scale=1.0 / QR)
            SE.activation(nrm[:, 1, :], bank[0][:, S:2 * S], ACT.Sqrt, bias=cc("eps", 1, 0), scale=1.0 / KVR)\
                .then_inc(*act.mark("latent rms"))
            fa.at("latents normed")
            for g in range(4):
                sc.wait_ge(*ten.at(("k", g)))
                SE.copy(kf[0:NOPE, 2 * g:2 * g + 2, :], bank[2 + g][0:NOPE, :].rearrange("p (h t) -> p h t", h=2))\
                    .then_inc(*act.mark(("k", g)))
            for g in range(4):
                sc.wait_ge(*ten.at(("q", g)))
                SE.copy(qf[0:QK, 2 * g:2 * g + 2, :], bank[2 + g][0:QK, :].rearrange("p (h t) -> p h t", h=2))\
                    .then_inc(*act.mark(("q", g)))
            for t in range(NT):
                sc.wait_ge(*ten.at(("v", t)))
                SE.copy(vm[:, t, :], bank[t][:, :]).then_inc(*act.mark(("v", t)))
            for w, src in (("k", kf), ("q", qf)):
                if w == "k":
                    sc.wait_ge(*vec.at("rope keys"))
                    sc.wait_ge(*act.at(("k", 3)))
                else:
                    fa.at("k turned")
                    sc.wait_ge(*vec.at("k turned"))
                    sc.wait_ge(*act.at(("q", 3)))
                SE.activation(hs[0:QK], src[0:QK], ACT.Square).then_inc(*act.mark(f"{w} squares"))
                if w == "k":
                    fa.at("k squares")
                sc.wait_ge(*ten.at(f"{w} sums"))
                SE.activation(rn8[0:H, 0, :], bank[0][0:H, 0:S], ACT.Sqrt, bias=cc("eps", 1, 0, H), scale=1.0 / QK)\
                    .then_inc(*act.mark(f"{w} rms"))
                fa.at(f"{w} inverse")
                fa.at(f"{w} normed")
            fa.at("q turned")

            def exps(h):
                sc.wait_ge(*ten.at(("scores", h)))
                sc.wait_ge(*vec.at(("max", h)))
                if h >= 2:
                    sc.wait_ge(*ten.at(("probT", h - 2)))
                for t in range(NT):
                    SE.activation(prob[:, h % 2, t, :], bank[5 * (h % 2)][:, t * S:(t + 1) * S], ACT.Exp,
                                  bias=mx[:, h % 2, t:t + 1], scale=SCALE, accum_out=mx[:, h % 2, 2 + t:3 + t])\
                        .then_inc(*act.mark(("exp", h, t)))

            exps(0)
            for h in range(H):
                if h + 1 < H:
                    exps(h + 1)
                fa.at(("head", h))
                if h >= 2:
                    sc.wait_ge(*ten.at(("attended", h - 2)))
                sc.wait_ge(*ten.at(("probT", h)))
                SE.copy(probT[:, h % 2, :, :], bank[1 + h % 2][:, :].rearrange("p (b t) -> p b t", b=2))\
                    .then_inc(*act.mark(("probT", h)))
                if h % 2:
                    j = h // 2
                    sc.wait_ge(*ten.at(("attended", h)))
                    SE.copy(u_hi[:, j, :], bank[3 + j % 2][:, 0:S]).then_inc(*act.mark(("u hi", 2, j)))

            sc.wait_ge(*vec.at("key scaled"))
            SE.activation(tA, kk, ACT.Square).then_inc(*act.mark("key squares"))
            SE.preload_act_table(ACT.Sigmoid)
            sc.wait_ge(*vec.at(("mixed", 3)))
            SE.activation(wag[:, 0, :], wag[:, 0, :], ACT.Tanh).then_inc(*act.mark("wag tanh"))
            SE.activation(wag[:, 2, :], wag[:, 2, :], ACT.Sigmoid).then_inc(*act.mark("wag"))
            fr.at("key sums")
            sc.wait_ge(*ten.at("key sums"))
            SE.activation(rn_rw[0:H, 0, :], bank[4][0:H, 0:S], ACT.Sqrt).then_inc(*act.mark("key rms"))
            SE.preload_act_table(ACT.Sigmoid)
            fr.at("key inverse")
            sc.wait_ge(*ten.at("nu"))
            for c in range(RC):
                m = SE.activation(tB[:, c, :], bank[c // 2][:, (c % 2) * S:(c % 2 + 1) * S], ACT.Sigmoid,
                                  bias=vv("v0", c))
            m.then_inc(*act.mark("nu"))
            fr.at("values")
            sc.wait_ge(*ten.at("cv mean"))
            SE.mul(cv_st[:, 0, :], bank[4][:, 0:S], 1.0 / CV).then_inc(*act.mark("cv mean"))
            sc.wait_ge(*vec.at(("cv centred", RC - 1)))
            SE.activation(cv_sq, cvo, ACT.Square).then_inc(*act.mark("cv squares"))
            fr.at("cv mean")
            sc.wait_ge(*ten.at("cv var"))
            SE.activation(cv_st[:, 1, :], bank[5][:, 0:S], ACT.Sqrt, bias=cc("eps", 1, 2), scale=1.0 / CV)\
                .then_inc(*act.mark("cv rms"))
            SE.preload_act_table(ACT.Sigmoid)
            fr.at("cv var")
            for c in range(RC):
                sc.wait_ge(*vec.at(("cv normed", c)))
                SE.activation(cv_sq[:, c, :], cvo[:, c, :], ACT.Sigmoid, bias=vv("ln_b", c))\
                    .then_inc(*act.mark(("cv sigmoid", c)))
            for c in range(RC):
                sc.wait_ge(*vec.at(("cv act", c)))
                SE.copy(c_hi[:, c, :], cvo[:, c, :]).then_inc(*act.mark(("u hi", 1, c)))
            sc.wait_ge(*ten.at("vt"))
            for t in range(NT):
                m = SE.copy(vt[:, t, :], bank[4 + t][:, :])
            m.then_inc(*act.mark("vt"))

            for d in range(2):
                if d:
                    sc.wait_ge(*vec.at(("o", 0, H - 1)))
                    sc.wait_ge(*vec.at(("qw", 0, H - 1)))
                    sc.wait_ge(*ten.at(("pq", 0, H - 1)))
                else:
                    sc.wait_ge(*vec.at("values"))
                    sc.wait_ge(*vec.at("kk"))
                sc.wait_ge(*ten.at(("lora", d, 0)))
                for c in range(RC):
                    m = SE.activation(tA[:, c, :], bank[c // 2][:, (c % 2) * S:(c % 2 + 1) * S], ACT.Sigmoid,
                                      bias=vv("w0", d * RC + c))
                m.then_inc(*act.mark(("sw", d)))
                sc.wait_ge(*ten.at(("lora", d, 1)))
                for c in range(RC):
                    m = SE.activation(tB[:, c, :], bank[2 + c // 2][:, (c % 2) * S:(c % 2 + 1) * S], ACT.Sigmoid,
                                      bias=vv("a0", d * RC + c))
                m.then_inc(*act.mark(("icl", d)))
                fr.at(("lora", d))
                SE.preload_act_table(ACT.Exp)
                sc.wait_ge(*vec.at(("before", d)))
                SE.activation(tA, tC_, ACT.Exp, scale=-DECAY).then_inc(*act.mark(("w", d)))
                SE.activation(tD, tD, ACT.Exp, scale=-DECAY).then_inc(*act.mark(("wx", d)))
                sc.wait_ge(*act.at(("w", d)))
                SE.activation(tC_, tC_, ACT.Exp, scale=DECAY).then_inc(*act.mark(("winv", d)))
                SE.preload_act_table(ACT.Sigmoid)
                fr.at(("kr", d))
                for q in range(6):
                    sc.wait_ge(*ten.at(("tk", d, q)))
                    SE.copy(tk[:, q // NT, q % NT, :], bank[q][:, :]).then_inc(*act.mark(("tk", d, q)))
                for h0 in range(0, H, 2):
                    fr.at((d, h0, "pairs"))
                    for lv in range(1, LEVELS):
                        fr.at((d, h0, lv, 0))
                        fr.at((d, h0, lv, 1))
                    for h in (h0, h0 + 1):
                        sc.wait_ge(*ten.at(("gv", d, h)))
                        SE.copy(gv[:, h % 2, :, :], bank[3 * (h % 2) + 2][:, S:S + P].rearrange("p (t c) -> p t c", t=NT))\
                            .then_inc(*act.mark(("gv", d, h)))
                    for h in (h0, h0 + 1):
                        b = bank[3 * (h % 2)]
                        sc.wait_ge(*ten.at(("xy", d, h)))
                        SE.copy(xs[:, h % 2, :, :], b[:, 0:P].rearrange("p (t c) -> p t c", t=NT))\
                            .then_inc(*act.mark(("x", d, h)))
                        SE.mul(ys[:, h % 2, :, :], b[:, P:2 * P].rearrange("p (t c) -> p t c", t=NT), -1.0)\
                            .then_inc(*act.mark(("y", d, h)))
                    fr.at((d, h0, "x"))
                    fr.at((d, h0, "o"))
            sc.wait_ge(*vec.at("gn centred"))
            SE.activation(tB, osum, ACT.Square).then_inc(*act.mark("gn squares"))
            sc.wait_ge(*ten.at("gn sums"))
            SE.activation(rn_rw[0:H, 1, :], bank[4][0:H, 0:S], ACT.Sqrt, bias=cc("eps", 1, 1, H), scale=1.0 / HD)\
                .then_inc(*act.mark("gn rms"))
            used(T_BR + RC + KC - 1)
            for c in range(RC):
                sc.wait_ge(*vec.at(("rw out", c)))
                SE.copy(u_hi[:, c, :], osum[:, c, :]).then_inc(*act.mark(("u hi", 0, c)))
            SE.preload_act_table(ACT.Sigmoid)
            for _ in branch_tiles(2, 0, 4, 4):
                pass
            for c in range(KC):
                sc.wait_ge(*vec.at(("merge", 0, KC - 1)))
                used(T_WO - 1)
                SE.copy(h_hi[:, c, :], merged[:, c, :]).then_inc(*act.mark(("m hi", c)))
            for c in range(KC):
                hi(L, 0, T_WO + c + HL)
            norm(2)
            ffn(1, T_FFN2)
            for n in range(T_END, TILES):
                hi(L, 0, n + HL)
            loop.__exit__(None, None, None)

        @block.vector
        def _(ve):
            V = nc.vector
            TT, TS, STT = V.tensor_tensor, V.tensor_scalar, V.scalar_tensor_tensor

            def lo(L, it, m):
                ve.wait_ge(hi_ready, L * TILES + it * LOOP + (m + 1))
                TT(wlo[:, m % HL, :], raw[:, m % RAW, :], whi[:, m % HL, :].bitcast(F), ALU.subtract)\
                    .then_inc(lo_ready, 1)

            for i in range(RAW):
                V.memset(gs[:, 0, i:i + 1], 0.0).then_inc(lo_ready, 1)
            for i in range(RAW, RAW + 2):
                V.memset(gs[:, 0, i:i + 1], 0.0).then_inc(g_ready, 1)
            ve.wait_ge(consts_in, 16)
            ve.wait_ge(masks_in, 16)
            V.tensor_copy(msk[:, :], arena[:, 2048:2048 + NM])
            ve.wait_ge(x_in, 16)
            V.memset(gs[:, 0, RAW + 2:RAW + 3], 0.0).then_inc(x_ready, 1)
            for m in range(HL):
                lo(0, 0, m)
            loop, L = layers(ve)
            ve.wait_ge(vec_in, L * 16 + 16)
            ve.wait_ge(lora_in, L * 16 + 16)

            def used(n):
                ve.wait_ge(tile_used, L * TILES + n + 1 + HL)

            def norm(i):
                gain = ("norm_ffn1", "norm_mix", "norm_ffn2")[i]
                ve.wait_ge(*act.at(("rms", i)))
                V.reciprocal(nrm[:, 1, :], nrm[:, 0, :]).then_inc(*vec.mark(("rstd", i)))
                ve.wait_ge(*vec.at(("rstd", i)))
                for c in range(KC):
                    STT(sq[:, c, :], xT[:, c, :], vv(gain, c), nrm[:, 1, :], ALU.mult, ALU.mult)\
                        .then_inc(*vec.mark(("h", i, c)))
                for c in range(KC):
                    ve.wait_ge(*act.at(("h hi", i, c)))
                    TT(h_lo[:, c, :], sq[:, c, :], h_hi[:, c, :].bitcast(F), ALU.subtract)\
                        .then_inc(*vec.mark(("h lo", i, c)))

            def ffn(f, tile0):
                def chunk(it, j, s, m, down):
                    base = (2 * L + f) * NFF
                    lo(L, it, m + HL)
                    ve.wait_ge(sig_ready, base + j + 1)
                    TT(g_s[:, s, :], g_s[:, s, :], bank[4 + s][:, 0:S], ALU.mult).then_inc(as_ready, 1)
                    ve.wait_ge(as_ready, base + j + 1)
                    TT(g_f[:, s, :], g_s[:, s, :], bank[4 + s][:, S:2 * S], ALU.mult).then_inc(g_ready, 1)
                    lo(L, it, m + 1 + HL)
                    ve.wait_ge(ghi_ready, base + j + 1)
                    TT(g_lo[:, s, :], g_f[:, s, :], g_hi[:, s, :].bitcast(F), ALU.subtract).then_inc(glo_ready, 1)
                    if down:
                        lo(L, it, m + 2 + HL)

                chunk(0, 0, 0, tile0, False)
                with ve.Fori(0, (NFF - 2) // 2) as it:
                    for q in range(2):
                        chunk(it, it * 2 + (q + 1), (q + 1) % 2, tile0 + 2 + 3 * q, True)
                chunk(0, NFF - 1, 1, tile0 + 3 * NFF - 4, True)
                lo(L, 0, tile0 + 3 * NFF - 1 + HL)
                used(tile0 + 3 * NFF - 1)
                for b in range(4):
                    x2 = xT[:, 2 * b:2 * b + 2, :]
                    m = STT(x2, bank[b][:, :].rearrange("p (c t) -> p c t", c=2), 0.5, x2, ALU.mult, ALU.add)
                    m.then_inc(*vec.mark(("residual", f, b)))

            norm(0)
            ffn(0, T_FFN1)
            norm(1)
            for i in range(N_MLA):
                lo(L, 0, T_MLA + i + HL)
            V.memset(pp[:, :, 0:1], 0.0)
            V.memset(pp[:, :, S + 1:S + 2], 0.0).then_inc(*vec.mark("pp edges"))

            def shift_mix(g):
                n = 4 if g < 3 else 3
                dst = (r_, k_, v_, wag)[g]
                ve.wait_ge(*act.at(("column", T_RW + 4 * g + n - 1)))
                ve.wait_ge(*vec.at("pp edges"))
                if g:
                    ve.wait_ge(*vec.at(("mixed", g - 1)))
                TT(pt[:, 0:n, :], pp[:, 0:n, 0:S], pp[:, 0:n, 2:S + 2], ALU.add).then_inc(*vec.mark(("sum", g)))
                ve.wait_ge(*vec.at(("sum", g)))
                STT(pt[:, 0:n, :], pt[:, 0:n, :], 0.5, pp[:, 0:n, 1:S + 1], ALU.mult, ALU.subtract)\
                    .then_inc(*vec.mark(("shift", g)))
                ve.wait_ge(*vec.at(("shift", g)))
                for c in range(n):
                    m = STT(dst[:, c, :], pt[:, c, :], vv("mu", 4 * g + c), pp[:, c, 1:S + 1], ALU.mult, ALU.add)
                m.then_inc(*vec.mark(("mixed", g)))

            def fill_a():
                for n in range(T_CV, T_BR):
                    lo(L, 0, n + HL)
                    if n < T_RW and (n - T_CV) % 2:
                        c = (n - T_CV) // 2
                        ve.wait_ge(*act.at(("column", n)))
                        ve.wait_ge(*poo.at("pad right"))
                        TT(upad[:, c, HALF:HALF + S], gs[:, c % 2, :], bank[6][:, 0:S], ALU.mult)\
                            .then_inc(*vec.mark(("glu", c)))
                    if T_RW <= n < T_VD and ((n - T_RW) % 4 == 3 or n == T_VD - 1):
                        shift_mix((n - T_RW) // 4)
                    yield

            def branch_tiles(order, b, bank0, nb):
                t0 = T_BR + order * (RC + KC)
                for c in range(0, KC, 2):
                    n = t0 + 3 * (c // 2)
                    lo(L, 0, n + HL)
                    yield
                    for e in range(2):
                        ve.wait_ge(*act.at(("gate", b, c + e)))
                        y = bank[bank0 + (c + e) % nb][:, 0:S]
                        if order == 0:
                            if c + e == 0:
                                ve.wait_ge(*vec.at(("mixed", 3)))
                            TT(merged[:, c + e, :], gs[:, e, :], y, ALU.mult).then_inc(*vec.mark(("merge", b, c + e)))
                        else:
                            TT(gs[:, e, :], gs[:, e, :], y, ALU.mult).then_inc(*vec.mark(("gated", b, c + e)))
                            ve.wait_ge(*vec.at(("gated", b, c + e)))
                            TT(merged[:, c + e, :], merged[:, c + e, :], gs[:, e, :], ALU.add)\
                                .then_inc(*vec.mark(("merge", b, c + e)))
                        lo(L, 0, n + 1 + e + HL)
                        yield

            def fill_r():
                yield from branch_tiles(0, 2, 6, 2)
                yield from branch_tiles(1, 1, 6, 2)

            fa = Filling(FILL_A, fill_a(), PIECES)
            fr = Filling(FILL_R, fill_r(), PIECES)

            fa.at("latent squares")
            ve.wait_ge(*act.at("latent rms"))
            V.reciprocal(nrm[:, :, :], nrm[:, :, :]).then_inc(*vec.mark("latent inverse"))
            ve.wait_ge(*vec.at("latent inverse"))
            for c in range(QC + KVC):
                q = c < QC
                m = STT(lat[:, c, :], lat[:, c, :], vv("q_norm", c) if q else vv("kv_norm", c - QC),
                        nrm[:, 0 if q else 1, :], ALU.mult, ALU.mult)
            m.then_inc(*vec.mark("latents normed"))
            fa.at("latents normed")
            ve.wait_ge(*act.at(("column", T_CV - 1)))
            V.tensor_copy(kf[NOPE:QK], rope_in[NOPE:QK].unsqueeze(1).broadcast_to([ROPE, H, S]))\
                .then_inc(*vec.mark("rope keys"))
            for w, x_ in (("k", kf), ("q", qf)):
                fa.at("k squares" if w == "k" else "k turned")
                ve.wait_ge(*act.at(f"{w} rms"))
                V.reciprocal(rn8[0:H, 0, :], rn8[0:H, 0, :]).then_inc(*vec.mark(f"{w} inverse"))
                fa.at(f"{w} inverse")
                ve.wait_ge(*ten.at(f"{w} spread"))
                for g in range(4):
                    xg = x_[0:QK, 2 * g:2 * g + 2, :]
                    m = STT(xg, xg, vv(f"qk_{w}_g", 0, 0, QK),
                            bank[1 + g][0:QK, :].rearrange("p (h t) -> p h t", h=2), ALU.mult, ALU.mult)
                m.then_inc(*vec.mark(f"{w} normed"))
                fa.at(f"{w} normed")
                ve.wait_ge(*ten.at(f"{w} rotated"))
                for g in range(4):
                    m = TT(hs[0:QK, 2 * g:2 * g + 2, :], bank[1 + g][0:QK, :].rearrange("p (h t) -> p h t", h=2),
                           sinT[0:QK].unsqueeze(1).broadcast_to([QK, 2, S]), ALU.mult)
                m.then_inc(*vec.mark(f"{w} sine part"))
                TT(x_[0:QK], x_[0:QK], cosT[0:QK].unsqueeze(1).broadcast_to([QK, H, S]), ALU.mult)\
                    .then_inc(*vec.mark(f"{w} cosine part"))
                ve.wait_ge(*vec.at(f"{w} cosine part"))
                TT(x_[0:QK], x_[0:QK], hs[0:QK], ALU.add).then_inc(*vec.mark(f"{w} turned"))

            taps = [(c, t) for t in range(TAPS) for c in range(2)]

            def conv(n):
                for c, t in [taps.pop(0) for _ in range(min(n, len(taps)))]:
                    src = upad[:, c, t:t + S]
                    if t == 0:
                        ve.wait_ge(*vec.at(("glu", 3)))
                        m = TS(cvo[:, c, :], src, vv("cv_w", c * TAPS), vv("cv_b", c), ALU.mult, ALU.add)
                    else:
                        ve.wait_ge(*vec.at(("conv", c, t - 1)))
                        m = STT(cvo[:, c, :], src, vv("cv_w", c * TAPS + t), cvo[:, c, :], ALU.mult, ALU.add)
                    m.then_inc(*vec.mark(("conv", c, t)))

            fa.at("q turned")

            def head_max(h):
                ve.wait_ge(*ten.at(("scores", h)))
                if h >= 2:
                    ve.wait_ge(*vec.at(("prob", h - 2, 1)))
                V.reduce_max(mx[:, h % 2, 0:2], bank[5 * (h % 2)][:, :].rearrange("p (t k) -> p t k", t=NT), AX.X)\
                    .then_inc(*vec.mark(("rawmax", h)))
                ve.wait_ge(*vec.at(("rawmax", h)))
                TS(mx[:, h % 2, 0:2], mx[:, h % 2, 0:2], -SCALE, None, ALU.mult).then_inc(*vec.mark(("max", h)))

            head_max(0)
            for h in range(H):
                if h + 1 < H:
                    head_max(h + 1)
                fa.at(("head", h))
                ve.wait_ge(*act.at(("exp", h, 1)))
                V.reciprocal(mx[:, h % 2, 2:4], mx[:, h % 2, 2:4]).then_inc(*vec.mark(("invsum", h)))
                ve.wait_ge(*vec.at(("invsum", h)))
                for t in range(NT):
                    TS(prob[:, h % 2, t, :], prob[:, h % 2, t, :], mx[:, h % 2, 2 + t:3 + t], None, ALU.mult)\
                        .then_inc(*vec.mark(("prob", h, t)))
                conv(6)
                if h % 2:
                    j = h // 2
                    ve.wait_ge(*act.at(("u hi", 2, j)))
                    TT(u_lo[:, j, :], bank[3 + j % 2][:, 0:S], u_hi[:, j, :].bitcast(F), ALU.subtract)\
                        .then_inc(*vec.mark(("u", 2, j)))

            for c in range(RC):
                m = TS(kk[:, c, :], k_[:, c, :], vv("k_k", c), None, ALU.mult)
            m.then_inc(*vec.mark("key scaled"))
            conv(len(taps))
            fr.at("key sums")
            ve.wait_ge(*act.at("key rms"))
            TS(rn_rw[0:H, 0, :], rn_rw[0:H, 0, :], 1e-12, None, ALU.max).then_inc(*vec.mark("key floor"))
            ve.wait_ge(*vec.at("key floor"))
            V.reciprocal(rn_rw[0:H, 0, :], rn_rw[0:H, 0, :]).then_inc(*vec.mark("key inverse"))
            fr.at("key inverse")
            ve.wait_ge(*poo.at(("conv", 3, TAPS - 1)))
            TT(tC_, vfirst[:, :, :], v_, ALU.subtract).then_inc(*vec.mark("v difference"))
            ve.wait_ge(*ten.at("key spread"))
            ve.wait_ge(*vec.at("key scaled"))
            for b in range(2):
                m = TT(kk[:, 2 * b:2 * b + 2, :], kk[:, 2 * b:2 * b + 2, :],
                       bank[2 + b][:, :].rearrange("p (c t) -> p c t", c=2), ALU.mult)
            m.then_inc(*vec.mark("kk"))
            fr.at("values")
            ve.wait_ge(*act.at("cv mean"))
            for c in range(RC):
                TT(cvo[:, c, :], cvo[:, c, :], cv_st[:, 0, :], ALU.subtract).then_inc(*vec.mark(("cv centred", c)))
            ve.wait_ge(*act.at("nu"))
            ve.wait_ge(*vec.at("v difference"))
            TT(tC_, tC_, tB, ALU.mult).then_inc(*vec.mark("v share"))
            ve.wait_ge(*vec.at("v share"))
            STT(v_, tC_, vv("keep"), v_, ALU.mult, ALU.add).then_inc(*vec.mark("values"))
            ve.wait_ge(*vec.at("values"))
            TT(tD, v_, vfirst[:, :, :], ALU.subtract).then_inc(*vec.mark("first difference"))
            ve.wait_ge(*vec.at("first difference"))
            STT(vfirst[:, :, :], tD, vv("first"), vfirst[:, :, :], ALU.mult, ALU.add)\
                .then_inc(*vec.mark("first values"))
            fr.at("cv mean")
            ve.wait_ge(*act.at("cv rms"))
            V.reciprocal(cv_st[:, 2, :], cv_st[:, 1, :]).then_inc(*vec.mark("cv inverse"))
            ve.wait_ge(*vec.at("cv inverse"))
            fr.at("cv var")
            for c in range(RC):
                STT(cvo[:, c, :], cvo[:, c, :], vv("ln_g", c), cv_st[:, 2, :], ALU.mult, ALU.mult)\
                    .then_inc(*vec.mark(("cv normed", c)))
            for c in range(RC):
                ve.wait_ge(*act.at(("cv sigmoid", c)))
                STT(cvo[:, c, :], cvo[:, c, :], vv("ln_b", c), cv_sq[:, c, :], ALU.add, ALU.mult)\
                    .then_inc(*vec.mark(("cv act", c)))
            for c in range(RC):
                ve.wait_ge(*act.at(("u hi", 1, c)))
                TT(c_lo[:, c, :], cvo[:, c, :], c_hi[:, c, :].bitcast(F), ALU.subtract).then_inc(*vec.mark(("u", 1, c)))

            kr_kk = kr[:, :, :, 0, :]
            kr_r = kr[:, :, :, 1, :]
            by_tile = lambda a: a.rearrange("p c (t q) -> p c t q", t=NT)
            for d in range(2):
                ve.wait_ge(*act.at(("sw", d)))
                if d == 0:
                    ve.wait_ge(*vec.at("first values"))
                for c in range(RC):
                    m_, s_, o_ = cc("scan", S, d * S), tA[:, c, :], tC_[:, c, :]
                    if d:
                        m_, s_, o_ = (a[:, ::-1] for a in (m_, s_, o_))
                    m = V.tensor_tensor_scan(o_, m_, s_, 0.0, ALU.mult, ALU.add)
                m.then_inc(*vec.mark(("scan", d)))
                ve.wait_ge(*vec.at(("scan", d)))
                TT(tD, tC_, tA, ALU.subtract).then_inc(*vec.mark(("before", d)))
                fr.at(("lora", d))
                ve.wait_ge(*act.at(("w", d)))
                TT(kr_r, by_tile(r_), by_tile(tA), ALU.mult)
                edge = C - 1 if d == 0 else 0
                V.tensor_copy(wch, tA.rearrange("p c (n e) -> p c n e", e=C)[:, :, :, edge]).then_inc(*vec.mark(("wch", d)))
                ve.wait_ge(*act.at(("wx", d)))
                TT(kr_kk, by_tile(kk), by_tile(tD), ALU.mult).then_inc(*vec.mark(("kr", d)))
                ve.wait_ge(*act.at(("icl", d)))
                TT(bt, kk, tB, ALU.mult).then_inc(*vec.mark(("b", d)))
                ve.wait_ge(*act.at(("winv", d)))
                ve.wait_ge(*vec.at(("b", d)))
                ve.wait_ge(*vec.at(("kr", d)))
                TT(bt, bt, tC_, ALU.mult).then_inc(*vec.mark(("bt", d)))
                for c in range(RC):
                    m = TS(tD[:, c, :], tB[:, c, :], -1.0, vv("k_a", c), ALU.add, ALU.mult)
                m.then_inc(*vec.mark(("ka", d)))
                ve.wait_ge(*vec.at(("ka", d)))
                STT(tD, tD, 1.0, k_, ALU.add, ALU.mult).then_inc(*vec.mark(("kdir", d)))
                ve.wait_ge(*vec.at(("kdir", d)))
                if d == 0:
                    V.tensor_copy(kds, tD).then_inc(*vec.mark("kds 0"))
                else:
                    TT(kds, kds, tD, ALU.add).then_inc(*vec.mark("kds 1"))
                TT(kt, tD, tC_, ALU.mult).then_inc(*vec.mark(("kt", d)))
                fr.at(("kr", d))
                ve.wait_ge(*vec.at(("kt", d)))

                tm = msk[:, d * 2 * P:(d + 1) * 2 * P].rearrange("p (i t) -> p i t", i=2)
                tm = tm.unsqueeze(1).broadcast_to([P, NT, 2, P])
                m1 = msk[:, M1 + d * 2 * P:M1 + (d + 1) * 2 * P].rearrange("p (i t) -> p i t", i=2)
                flat = lambda a: a.rearrange("p t n -> p (t n)")
                for h0 in range(0, H, 2):
                    pair = (h0, h0 + 1)
                    for h in pair:
                        s, b = h % 2, 3 * (h % 2)
                        ve.wait_ge(*ten.at(("pairs", d, h)))
                        TT(g1[:, s], bank[b][:, :].rearrange("p (t i n) -> p t i n", t=NT, i=2), tm, ALU.mult)\
                            .then_inc(*vec.mark(("g1", d, h)))
                        TT(mn[:, s, 0], bank[b + 2][:, 0:S].rearrange("p (t n) -> p t n", t=NT),
                           m1[:, 0:1, :].broadcast_to([P, NT, P]), ALU.mult)
                        ve.wait_ge(*vec.at(("g1", d, h)))
                        TT(mn[:, s, 1], g1[:, s, :, 0, :], m1[:, 1:2, :].broadcast_to([P, NT, P]), ALU.mult)\
                            .then_inc(*vec.mark(("m1", d, h)))
                        ve.wait_ge(*vec.at(("m1", d, h)))
                        mn4 = mn[:, s].rearrange("p i t n -> p (i t) n")
                        TT(mn4, mn4, ident.unsqueeze(1).broadcast_to([P, 2 * NT, P]), ALU.add)\
                            .then_inc(*vec.mark(("mn", d, h, 0)))
                    fr.at((d, h0, "pairs"))
                    for lv in range(1, LEVELS):
                        o = LEV + (d * (LEVELS - 1) + lv - 1) * P
                        mask = msk[:, o:o + P].unsqueeze(1).broadcast_to([P, NT, P])
                        fr.at((d, h0, lv, 0))
                        for h in pair:
                            s, b = h % 2, 3 * (h % 2)
                            ve.wait_ge(*ten.at(("z", d, h, lv)))
                            TT(zz[:, s], bank[b + 2][:, 0:S].rearrange("p (t n) -> p t n", t=NT), mask, ALU.mult)\
                                .then_inc(*vec.mark(("z", d, h, lv)))
                        if lv == 1:
                            for h in pair:
                                s, b = h % 2, 3 * (h % 2)
                                TT(g2[:, s], bank[b + 1][:, :].rearrange("p (t i n) -> p t i n", t=NT, i=2), tm,
                                   ALU.mult).then_inc(*vec.mark(("g2", d, h)))
                        fr.at((d, h0, lv, 1))
                        for h in pair:
                            s, b = h % 2, 3 * (h % 2)
                            ve.wait_ge(*ten.at(("mz", d, h, lv)))
                            if lv < LEVELS - 1:
                                mn4 = mn[:, s].rearrange("p i t n -> p (i t) n")
                                TT(mn4, mn4, bank[b][:, :].rearrange("p (i n) -> p i n", n=P), ALU.subtract)\
                                    .then_inc(*vec.mark(("mn", d, h, lv)))
                            else:
                                TT(mn[:, s, 1], mn[:, s, 1], bank[b][:, S:].rearrange("p (i n) -> p i n", n=P),
                                   ALU.subtract).then_inc(*vec.mark(("mn", d, h, lv)))
                    fr.at((d, h0, "x"))
                    for h in pair:
                        s, b, r, j = h % 2, 3 * (h % 2), HD * (h % 2), h // 2
                        ve.wait_ge(*ten.at(("rx", d, h)))
                        w = kr[r:r + HD, j, :, 1, :]
                        TT(w, w, bank[b + 2][r:r + HD, 0:S].rearrange("p (t n) -> p t n", t=NT), ALU.subtract)\
                            .then_inc(*vec.mark(("rx", d, h)))
                    fr.at((d, h0, "o"))
                    for h in pair:
                        s, b, r, j = h % 2, 3 * (h % 2), HD * (h % 2), h // 2
                        ve.wait_ge(*ten.at(("o", d, h)))
                        if d == 0:
                            V.tensor_copy(osum[r:r + HD, j, :], bank[b][r:r + HD, 0:S]).then_inc(*vec.mark(("o", d, h)))
                        else:
                            TT(osum[r:r + HD, j, :], osum[r:r + HD, j, :], bank[b][r:r + HD, 0:S], ALU.add)\
                                .then_inc(*vec.mark(("o", d, h)))
                    for h in pair:
                        s, b, r, j = h % 2, 3 * (h % 2), HD * (h % 2), h // 2
                        ve.wait_ge(*ten.at(("pq", d, h)))
                        for half in range(2):
                            pq = bank[b + 1 + half]
                            by2 = lambda a: a[r:r + HD, j].rearrange("p (t e) n -> p e t n", e=2)[:, half]
                            TT(by2(ptr), cc("ident64", C)[r:r + HD].unsqueeze(1).broadcast_to([HD, NT, C]),
                               pq[r:r + HD, 0:P].rearrange("p (t n) -> p t n", t=NT), ALU.subtract)
                            wb = wch[r:r + HD, j].rearrange("p (t e) -> p e t", e=2)[:, half]
                            m = TT(by2(qw), pq[r:r + HD, P:2 * P].rearrange("p (t n) -> p t n", t=NT),
                                   wb.unsqueeze(2).broadcast_to([HD, NT, HD]), ALU.mult)
                        m.then_inc(*vec.mark(("qw", d, h)))
                chunks = range(NCH) if d == 0 else range(NCH - 1, -1, -1)
                for i in (1, 2):
                    c = chunks[i]
                    ve.wait_ge(*ten.at(("state", d, i)))
                    ve.wait_ge(*vec.at(("qw", d, H - 1)))
                    if i == 2:
                        ve.wait_ge(*vec.at(("state", d, 1, 1)))
                    for e in range(2):
                        r = HD * e
                        dst = tmp_s[r:r + HD]
                        TT(dst, bank[e][r:r + HD, 0:S].rearrange("p (j n) -> p j n", j=RC),
                           wch[r:r + HD, :, c].unsqueeze(2).broadcast_to([HD, RC, HD]), ALU.mult)\
                            .then_inc(*vec.mark(("decayed", d, i, e)))
                    for e in range(2):
                        r = HD * e
                        ve.wait_ge(*vec.at(("decayed", d, i, e)))
                        TT(qw[r:r + HD, :, c, :], qw[r:r + HD, :, c, :], tmp_s[r:r + HD], ALU.add)\
                            .then_inc(*vec.mark(("state", d, i, e)))
                ve.wait_ge(*ten.at(("inter", d)))
                ve.wait_ge(*vec.at(("o", d, H - 1)))
                a, z = (C, S) if d == 0 else (0, S - C)
                for e in range(2):
                    for g in range(2):
                        r = HD * e
                        o = osum[r:r + HD, 2 * g:2 * g + 2, a:z]
                        m = TT(o, o, bank[2 + e + 2 * g][r:r + HD, :].rearrange("p (j t) -> p j t", j=2)[:, :, a:z],
                               ALU.add)
                m.then_inc(*vec.mark(("osum", d)))

            for c in range(RC):
                m = STT(tA[:, c, :], kds[:, c, :], vv("r_k", c), r_[:, c, :], ALU.mult, ALU.mult)
            m.then_inc(*vec.mark("bonus terms"))
            ve.wait_ge(*ten.at("gn mean"))
            ve.wait_ge(*vec.at(("osum", 1)))
            for b in range(2):
                o = osum[:, 2 * b:2 * b + 2, :]
                m = TT(o, o, bank[b][:, :].rearrange("p (c t) -> p c t", c=2), ALU.subtract)
            m.then_inc(*vec.mark("gn centred"))
            ve.wait_ge(*ten.at("bonus"))
            for b in range(2):
                m = STT(tC_[:, 2 * b:2 * b + 2, :], bank[6 + b][:, :].rearrange("p (c t) -> p c t", c=2), 0.5 * HD,
                        v_[:, 2 * b:2 * b + 2, :], ALU.mult, ALU.mult)
            m.then_inc(*vec.mark("bonus"))
            ve.wait_ge(*act.at("gn rms"))
            V.reciprocal(rn_rw[0:H, 1, :], rn_rw[0:H, 1, :]).then_inc(*vec.mark("gn inverse"))
            ve.wait_ge(*ten.at("gn spread"))
            ve.wait_ge(*vec.at("bonus"))
            ve.wait_ge(*vec.at("gn centred"))
            half_bank = lambda b0, c: bank[b0 + c // 2][:, (c % 2) * S:(c % 2 + 1) * S]
            for c in range(RC):
                STT(osum[:, c, :], osum[:, c, :], vv("gn_g", c), half_bank(0, c), ALU.mult, ALU.mult)\
                    .then_inc(*vec.mark(("gn normed", c)))
            for c in range(RC):
                ve.wait_ge(*vec.at(("gn normed", c)))
                STT(osum[:, c, :], osum[:, c, :], vv("gn_b", c), tC_[:, c, :], ALU.add, ALU.add)\
                    .then_inc(*vec.mark(("gn bonus", c)))
            ve.wait_ge(*ten.at("g"))
            for c in range(RC):
                ve.wait_ge(*vec.at(("gn bonus", c)))
                TT(osum[:, c, :], osum[:, c, :], half_bank(2, c), ALU.mult).then_inc(*vec.mark(("rw out", c)))
            for c in range(RC):
                ve.wait_ge(*act.at(("u hi", 0, c)))
                ve.wait_ge(*vec.at(("rw out", c)))
                TT(u_lo[:, c, :], osum[:, c, :], u_hi[:, c, :].bitcast(F), ALU.subtract).then_inc(*vec.mark(("u", 0, c)))
            for _ in branch_tiles(2, 0, 4, 4):
                pass
            for c in range(KC):
                ve.wait_ge(*act.at(("m hi", c)))
                ve.wait_ge(*vec.at(("merge", 0, KC - 1)))
                TT(h_lo[:, c, :], merged[:, c, :], h_hi[:, c, :].bitcast(F), ALU.subtract)\
                    .then_inc(*vec.mark(("m lo", c)))
            for c in range(KC):
                used(T_WO + c)
                TT(xT[:, c, :], xT[:, c, :], bank[4 + c % 4][:, 0:S], ALU.add).then_inc(*vec.mark(("x mixed", c)))
                lo(L, 0, T_WO + c + HL)
            norm(2)
            ffn(1, T_FFN2)
            V.memset(gs[:, 0, 0:1], 0.0).then_inc(x_ready, 1)
            ve.wait_ge(*vec.at(("residual", 1, 3)))
            for n in range(T_END, TILES):
                lo(L, 0, n + HL)
            loop.__exit__(None, None, None)

    return {s.name: s.counted() for s in (vec, act, ten, poo)}


def laid_out(inputs):
    a = {n: np.ascontiguousarray(v) for n, v in inputs.items()}
    f = np.float32

    def col(w, c0):
        return w[:, c0:c0 + P].reshape(-1, P, P).transpose(1, 0, 2).reshape(P, -1)

    stream = np.zeros((DEPTH * TILES + HL, P, D), f)
    vecs = np.zeros((DEPTH + 1, P, NV), f)
    lora = np.zeros((DEPTH + 1, P, 4 * RW), f)
    wuq = np.zeros((DEPTH + 1, P, QC * H * QK), f)
    wukv = np.zeros((DEPTH + 1, P, KVC * H * 128), f)
    for l in range(DEPTH):
        r = max(l - 1, 0)
        T = stream[l * TILES:(l + 1) * TILES]
        for f_, t0 in (("ffn1", T_FFN1), ("ffn2", T_FFN2)):
            w1, w3, w2 = (a[f"{f_}_{w}"][l] for w in ("w1", "w3", "w2"))
            for j in range(NFF):
                up = t0 + (0 if j == 0 else 3 * j - 1)
                T[up], T[up + 1] = col(w1, j * P), col(w3, j * P)
                T[t0 + min(3 * j + 4, 3 * NFF - 2 + (j == NFF - 1))] = w2[j * P:(j + 1) * P]
        w_in = a["w_in"][l]
        for i in range(N_RW):
            T[T_RW + i] = col(w_in, i * P)
        vd = np.zeros((D, P), f)
        vd[:, :32] = a["rw_v_down"][r]
        T[T_VD] = col(vd, 0)
        m0 = RW_COLS + CV_COLS
        for i in range(QC + KVC):
            T[T_MLA + i] = col(w_in, m0 + i * P)
        T[T_MLA + QC + KVC] = col(w_in, m0 + QR + KVR - NOPE)
        for c in range(RC):
            T[T_CV + 2 * c] = col(w_in, RW_COLS + c * P)
            T[T_CV + 2 * c + 1] = col(w_in, RW_COLS + CV + c * P)
        for order, b in enumerate(BRANCH_ORDER):
            t0 = T_BR + order * (RC + KC)
            w = a[("rw_w_branch", "cv_w_branch", "mla_w_branch")[b]][l]
            for c in range(0, KC, 2):
                n = t0 + 3 * (c // 2)
                T[n] = np.concatenate([col(w, c * P), col(w, (c + 1) * P)], 1)
                for e in range(2):
                    T[n + 1 + e] = col(w_in, m0 + MLA_COLS + b * D + (c + e) * P)
        for c in range(KC):
            T[T_WO + c] = col(a["w_o"][l], c * P)

        def put(name, v, at=0):
            v = v.reshape(-1, P).T if v.size % P == 0 else np.pad(v, (0, P - v.size))[:, None]
            vecs[l, :, VEC[name] + at:VEC[name] + at + v.shape[1]] = v

        for name in ("norm_ffn1", "norm_mix", "norm_ffn2"):
            put(name, a[name][l])
        put("mu", a["rw_mu"][l])
        for d in range(2):
            put("w0", a["rw_w0"][l, d], d * RC)
            put("a0", a["rw_a0"][l, d], d * RC)
            lora[l, d * HD:(d + 1) * HD, 0:RW] = a["rw_w_up"][l, d]
            lora[l, d * HD:(d + 1) * HD, RW:2 * RW] = a["rw_a_up"][l, d]
        for name, src in (("k_k", "rw_k_k"), ("k_a", "rw_k_a"), ("gn_g", "rw_gn_g"), ("gn_b", "rw_gn_b"),
                          ("cv_b", "cv_dw_b"), ("ln_g", "cv_ln_g"), ("ln_b", "cv_ln_b"), ("q_norm", "mla_q_norm"),
                          ("kv_norm", "mla_kv_norm"), ("qk_q_g", "mla_qk_q_g"), ("qk_k_g", "mla_qk_k_g")):
            put(name, a[src][l])
        put("r_k", a["rw_r_k"][l].reshape(-1))
        put("v0", a["rw_v0"][r])
        vecs[l, :, VEC["cv_w"]:VEC["cv_w"] + RC * TAPS] = \
            a["cv_dw_w"][l].reshape(TAPS, RC, P).transpose(2, 1, 0).reshape(P, -1)
        vecs[l, :, VEC["keep"]] = float(l > 0)
        vecs[l, :, VEC["first"]] = float(l == 0)
        lora[l, :, 2 * RW:3 * RW] = a["rw_g_up"][l]
        lora[l, :32, 3 * RW:] = a["rw_v_up"][r]
        wuq[l] = a["mla_w_uq"][l].reshape(QC, P, -1).transpose(1, 0, 2).reshape(P, -1)
        wukv[l] = a["mla_w_ukv"][l].reshape(KVC, P, -1).transpose(1, 0, 2).reshape(P, -1)
    x = np.ascontiguousarray(a["x"][0].T.reshape(KC, P, S).transpose(1, 0, 2))
    pos = np.ascontiguousarray(np.broadcast_to(a["positions"][0], (P, S)))
    c, m = constants()
    return {"x": x, "pos": pos, "stream": stream, "vecs": vecs, "cst": c, "msk": m, "lora": lora,
            "wuq": wuq, "wukv": wukv}


def kernel(**inputs):
    import concourse.bacc as bacc
    from concourse.bass_utils import run_bass_kernel_spmd

    arrays = laid_out(inputs)

    def build(known):
        nc = bacc.Bacc("TRN2", target_bir_lowering=False, num_devices=1)
        args = [nc.dram_tensor(f"in_{n}", v.shape, mybir.dt.from_np(v.dtype), kind="ExternalInput").ap()
                for n, v in arrays.items()]
        out = nc.dram_tensor("out", (P, KC, S), F, kind="ExternalOutput").ap()
        return nc, program(nc, *args, out, known)

    _, known = build(None)
    nc, _ = build(known)
    r = run_bass_kernel_spmd(nc, [{f"in_{n}": v for n, v in arrays.items()}], core_ids=[0])
    y = r.results[0]["out"]
    return np.ascontiguousarray(y.transpose(2, 1, 0).reshape(1, S, D))
```

```python
import numpy as np
from contextlib import ExitStack
import concourse.bass as bass
import concourse.mybir as mybir

F = mybir.dt.float32
R = mybir.dt.float32r
BF = mybir.dt.bfloat16
ALU = mybir.AluOpType
ACT = mybir.ActivationFunctionType
AX = mybir.AxisListType

P = 128
D = 1024
S = 256
DEPTH = 2
FF = 2816
KC = D // P
NFF = FF // P
NT = S // P
C = 64
NCH = S // C
H = 8
HD = 64
RW = H * HD
RC = RW // P
CV = 512
TAPS = 31
HALF = TAPS // 2
QR, KVR, ROPE, NOPE = 384, 256, 32, 64
QK = NOPE + ROPE
QC, KVC = QR // P, KVR // P
NORM_EPS, GN_EPS, LN_EPS = 1e-6, 64e-5, 1e-5
DECAY = float(np.exp(-0.5))
SCALE = float(QK) ** -0.5
LEVELS = 6

N_RW, N_VD, N_MLA, N_CV = 15, 1, 6, 8
T_FFN1 = 0
T_MLA = T_FFN1 + 3 * NFF
T_CV = T_MLA + N_MLA
T_RW = T_CV + N_CV
T_VD = T_RW + N_RW
T_BR = T_VD + N_VD
T_WO = T_BR + 3 * (RC + KC)
T_FFN2 = T_WO + KC
T_END = T_FFN2 + 3 * NFF
NORM_BANK = (6, 6, 3)
RAW, HL = 3, 3
LOOP = 6
TILES = -(-T_END // RAW) * RAW
assert RAW == HL and LOOP % RAW == 0
QK_BANKS = ((1, 2), (3, 4), (0, 5))
BRANCH_ORDER = (2, 1, 0)
RW_COLS, CV_COLS, MLA_COLS = 1920, 1024, 672

VEC = {}
NV = 0
for _name, _n in (("norm_ffn1", KC), ("norm_mix", KC), ("norm_ffn2", KC), ("mu", N_RW), ("w0", 2 * RC),
                  ("a0", 2 * RC), ("k_k", RC), ("k_a", RC), ("r_k", RC), ("v0", RC), ("gn_g", RC),
                  ("gn_b", RC), ("cv_b", RC), ("ln_g", RC), ("ln_b", RC), ("q_norm", QC),
                  ("kv_norm", KVC), ("qk_q_g", 1), ("qk_k_g", 1), ("cv_w", RC * TAPS), ("keep", 1),
                  ("first", 1)):
    VEC[_name] = NV
    NV += _n

CST = {}
NC = 0
for _name, _n in (("ident", P), ("ones", P), ("mean64", P), ("ident64", C), ("rot", QK), ("es", RC * H),
                  ("eb", RC * P), ("e96", H * H), ("b96", H * QK), ("scan", 2 * S), ("freq", 1), ("eps", 4)):
    CST[_name] = NC
    NC += _n
M1, LEV = 4 * P, 8 * P
NM = LEV + 2 * (LEVELS - 1) * P
MAGIC = 1.5 * 2.0 ** 23
PI_IN = float(np.nextafter(np.float32(np.pi), np.float32(0)))


def two_pi_parts(n=4, bits=9):
    rest, parts = 2 * np.pi, []
    for _ in range(n):
        q = 2.0 ** (np.floor(np.log2(rest)) - bits + 1)
        parts.append(float(np.floor(rest / q) * q))
        rest -= parts[-1]
    return parts + [float(np.float32(rest))]


TWO_PI = two_pi_parts()
ROPE_STEPS = 4 + 2 * len(TWO_PI) + 3 + 2


def constants():
    c = np.zeros((P, NC), np.float32)

    def put(name, a):
        a = np.asarray(a, np.float32).reshape(a.shape[0], -1)
        c[:a.shape[0], CST[name]:CST[name] + a.shape[1]] = a

    i = np.arange(P)
    put("ident", np.eye(P))
    put("ones", np.ones((P, P)))
    put("mean64", (i[:, None] // HD == i[None] // HD) / HD)
    put("ident64", np.tile(np.eye(C), (2, 1)))
    rot = np.zeros((QK, QK))
    for m in range(ROPE // 2):
        rot[NOPE + ROPE // 2 + m, NOPE + m] = -1.0
        rot[NOPE + m, NOPE + ROPE // 2 + m] = 1.0
    put("rot", rot)
    es = np.zeros((P, RC, H))
    eb = np.zeros((H, RC, P))
    for j in range(RC):
        for p in range(P):
            es[p, j, 2 * j + p // HD] = 1
            eb[2 * j + p // HD, j, p] = 1
    put("es", es)
    put("eb", eb)
    e96 = np.zeros((QK, H, H))
    b96 = np.zeros((H, H, QK))
    for h in range(H):
        e96[:, h, h] = 1
        b96[h, h, :] = 1
    put("e96", e96)
    put("b96", b96)
    same = i[:, None] // C == i[None] // C
    lt = i[:, None] < i[None]
    tm = np.zeros((P, 2, 2, P))
    for d, m in enumerate((lt, lt.T)):
        tm[:, d, 0] = same & m
        tm[:, d, 1] = same & (m | np.eye(P, dtype=bool))
    
    m1 = np.zeros((P, 2, 2, P))
    lev = np.zeros((P, 2, LEVELS - 1, P))
    for n in range(LEVELS):
        h = 2 ** n
        block = (i[:, None] // (2 * h) == i[None] // (2 * h)) & (i[:, None] // h > i[None] // h)
        for d, m in enumerate((block, block.T)):
            if n == 0:
                m1[:, d, 0], m1[:, d, 1] = -1.0 * m, -1.0 * m.T
            else:
                lev[:, d, n - 1] = m
    masks = np.concatenate([v.reshape(P, -1) for v in (tm, m1, lev)], 1).astype(np.float32)
    sc = np.ones((P, 2, S))
    sc[:, 0, ::C] = 0
    sc[:, 1, C - 1::C] = 0
    put("scan", sc)
    freq = 10000.0 ** (-np.arange(0, ROPE, 2) / ROPE)
    f = np.zeros((P, 1))
    f[NOPE:QK, 0] = np.tile(freq, 2)
    put("freq", f)
    put("eps", np.tile(np.array([NORM_EPS, GN_EPS, LN_EPS, 0.0]), (P, 1)))
    return c, masks


PIECES = KC
FILL_A = {"latent squares": 8, "latents normed": 24, "squares": 16, "inverse": 24}
FILL_A.update({("unit", u): 4 for u in range(8)})
FILL_A["turned"] = 24
FILL_A.update({("head", h): 8 for h in range(H)})
FILL_R = {"key sums": 8, "key inverse": 8, "values": 8, "cv mean": 8, "cv var": 8}
for _d in range(2):
    FILL_R.update({("lora", _d): 8, ("kr", _d): 18})
    for _h in range(0, H, 2):
        FILL_R.update({(_d, _h, "start"): 5 if _h else 2, (_d, _h, "pairs"): 5, (_d, _h, "x"): 2})
    FILL_R.update({("state", _d, i): n for i, n in enumerate((3, 1, 1))})
assert sum(FILL_A.values()) == PIECES * (T_BR - T_CV)
assert sum(FILL_R.values()) == PIECES * 2 * (RC + KC)


class Filling:

    def __init__(self, plan, work, unit):
        self.plan, self.work, self.unit, self.points = plan, work, unit, list(plan)
        self.pieces, self.done = 0, 0

    def at(self, point, lag=0):
        assert self.points.pop(0) == point, point
        self.pieces += self.plan[point]
        while self.done < self.pieces // self.unit - lag:
            next(self.work)
            self.done += 1

    def finish(self):
        assert not self.points
        while self.done < self.pieces // self.unit:
            next(self.work)
            self.done += 1


class Steps:

    def __init__(self, sem, name, known):
        self.sem, self.name, self.known = sem, name, known
        self.now, self.n, self.layer = {}, 0, 0

    def mark(self, key):
        self.n += 1
        assert key not in self.now, key
        self.now[key] = self.n
        return self.sem, 1

    def at(self, key):
        if self.known is None:
            return self.sem, 1
        total, values = self.known[self.name]
        return self.sem, self.layer * total + values[key]

    def counted(self):
        return self.n, self.now


def program(nc, x, pos, stream, vecs, cst_in, msk_in, lora, wuq_in, wukv_in, out, known):
    ctx = ExitStack()
    with ctx:
        def sb(name, shape, dt=F):
            return ctx.enter_context(nc.sbuf_tensor(name, shape, dt))

        def sem(name):
            return ctx.enter_context(nc.semaphore(name))

        xT = sb("xT", [P, KC, S])
        h_hi = sb("h_hi", [P, KC, S], R)
        h_lo = sb("h_lo", [P, KC, S], R)
        raw = sb("raw", [P, RAW, D])
        whi = sb("whi", [P, HL, D], R)
        wlo = sb("wlo", [P, HL, D], R)
        u_hi = sb("u_hi", [P, RC, S], R)
        u_lo = sb("u_lo", [P, RC, S], R)
        c_hi = sb("c_hi", [P, RC, S], R)
        c_lo = sb("c_lo", [P, RC, S], R)
        g_hi, g_lo = u_hi[:, 0:2, :], u_lo[:, 0:2, :]
        gs = sb("gs", [P, 2, S])
        msk = sb("masks", [P, NM], BF)
        cst = sb("consts", [P, NC])
        vec_t = sb("vec_t", [P, NV])
        lo_w = sb("lo_w", [P, 4, RW])
        zero_b = sb("zero_b", [1, 512], BF)
        vfirst = sb("vfirst", [P, RC, S])
        cosT = sb("cosT", [P, S])
        sinT = sb("sinT", [P, S])
        ARENA = 24420 + RC * S
        arena = sb("arena", [P, ARENA])
        bank = [ctx.enter_context(nc.psum_tensor(f"bank{i}", [P, 512], F)) for i in range(8)]

        def view(at, *shape):
            n = int(np.prod(shape))
            assert at + n <= ARENA, (at, shape)
            v = arena[:, at:at + n]
            if len(shape) == 2:
                v = v.rearrange("p (a b) -> p a b", b=shape[1])
            elif len(shape) == 3:
                v = v.rearrange("p (a b c) -> p a b c", b=shape[1], c=shape[2])
            elif len(shape) == 4:
                v = v.rearrange("p (a b c d) -> p a b c d", b=shape[1], c=shape[2], d=shape[3])
            return v

        Q1 = RC * S
        r_, k_, v_ = view(0, RC, S), view(Q1, RC, S), view(2 * Q1, RC, S)
        wag = view(3 * Q1, 4, S)
        merged = view(4 * Q1, KC, S)
        pp = view(4 * Q1, 4, S + 2)
        pt = view(4 * Q1 + 4 * (S + 2), 4, S)
        M0 = 6 * Q1 + 16
        pos_i = view(M0 + 3 * Q1, S)
        ang = view(M0 + 3 * Q1 + S, 4, S)
        g_s, g_f = view(0, 2, S), view(2 * S, 2, S)
        sq = view(M0, KC, S)
        lat = view(M0, QC + KVC, S)
        rope_in = view(M0 + 5 * S, S)
        UP0 = M0 + 6 * S
        upad = view(UP0, RC, S + TAPS - 1)
        CVO = UP0 + RC * (S + TAPS - 1)
        cvo = view(CVO, RC, S)
        MB = CVO + Q1
        nrm = view(MB + 4 * Q1, 2, S)
        sq_lat = view(MB + 5 * Q1, QC + KVC, S)
        qf = view(MB, H, S)
        kf = view(MB + 2 * Q1, H, S)
        hs = view(MB + 4 * Q1, H, S)
        hs_q = view(ARENA - H * S, H, S)
        vm = view(MB + 6 * Q1, NT, RW)
        prob = view(MB + 4 * Q1, 2, 2, S)
        probT = view(MB + 5 * Q1, 2, 2, S)
        rn8 = view(MB + 7 * Q1, 2, S)
        wuq = view(MB + 7 * Q1 + 2 * S, QC, H * QK)
        W2 = MB + 7 * Q1 + 2 * S + QC * H * QK
        wukv = view(W2, KVC, H * (NOPE + 64))
        mx = view(W2 + 2048, 2, 4)
        cv_tmp = view(W2 + 2048 + 8, 2, S)
        cv_sq = view(MB, RC, S)
        cv_st = view(MB + Q1, 3, S)
        kk = view(M0, RC, S)
        kds = view(M0 + Q1, RC, S)
        osum = view(M0 + 2 * Q1, RC, S)
        vt = view(ARENA - RC * S, NT, RW)
        kr = view(M0 + 4 * Q1, RC, NT, 2, P)
        bt = view(M0 + 6 * Q1, RC, S)
        kt = view(M0 + 7 * Q1, RC, S)
        tk = view(M0 + 8 * Q1, 3, NT, RW)
        ptr = view(M0 + 11 * Q1, RC, NCH, C)
        qw = view(M0 + 12 * Q1, RC, NCH, HD)
        G0 = M0 + 13 * Q1
        wch = view(G0, RC, NCH)
        G1 = G0 + RC * NCH
        tA, tB, tC_, tD = (view(G1 + i * Q1, RC, S) for i in range(4))
        g1 = view(G1, 2, NT, 2, P)
        g2 = view(G1 + Q1, 2, NT, 2, P)
        mn = view(G1 + 2 * Q1, 2, 2, NT, P)
        zz = view(G1 + 3 * Q1, 2, NT, P)
        xs = view(G1 + 3 * Q1 + 512, 2, NT, HD)
        ys = view(G1 + 3 * Q1 + 768, 2, NT, HD)
        gv = view(G1 + 4 * Q1, 2, NT, HD)
        rn_rw = view(G1 + 4 * Q1 + 256, 2, S)
        tmp_s = view(G1, RC, HD)

        def cc(name, n, at=0, rows=P):
            o = CST[name] + at
            return cst[0:rows, o:o + n]

        def vv(name, i=0, a=0, b=P):
            o = VEC[name] + i
            return vec_t[a:b, o:o + 1]

        ident = cc("ident", P)

        raw_in = [sem(f"raw_in{i}") for i in range(RAW)]
        hi_ready = sem("hi_ready")
        lo_ready = sem("lo_ready")
        tile_used = sem("tile_used")
        consts_in = sem("consts_in")
        masks_in = sem("masks_in")
        x_in = sem("x_in")
        pos_in = sem("pos_in")
        x_ready = sem("x_ready")
        vec_in = sem("vec_in")
        lora_in = sem("lora_in")
        uk_in = sem("uk_in")
        zeros_set = sem("zeros_set")
        rope_v, rope_a = sem("rope_v"), sem("rope_a")
        sig_ready = sem("sig_ready")
        as_ready = sem("as_ready")
        g_ready = sem("g_ready")
        ghi_ready = sem("ghi_ready")
        glo_ready = sem("glo_ready")
        vec = Steps(sem("vector_step"), "vec", known)
        act = Steps(sem("scalar_step"), "act", known)
        ten = Steps(sem("tensor_step"), "ten", known)
        poo = Steps(sem("pool_step"), "poo", known)
        out_done = sem("out_done")

        settles = sem("settles")

        def settled(eng):
            eng.sem_inc(settles, 1)

        def layers(eng):
            loop = eng.Fori(0, DEPTH)
            L = loop.__enter__()
            for steps in (vec, act, ten, poo):
                steps.layer = L
            return loop, L

        block = ctx.enter_context(nc.Block())

        @block.sync
        def _(sp):
            def load(tile, s, n):
                sp.wait_ge(lo_ready, n + 1)
                sp.dma_start(raw[:, s, :], tile).then_inc(raw_in[s], 16)

            sp.dma_start(xT[:, :, :], x).then_inc(x_in, 16)
            sp.dma_start(cst[:, :], cst_in).then_inc(consts_in, 16)
            with sp.Fori(0, DEPTH * TILES // RAW) as g:
                for s in range(RAW):
                    load(stream[g * RAW + s], s, g * RAW + s)
            for s in range(HL):
                load(stream[DEPTH * TILES + s], s, DEPTH * TILES + s)
            sp.wait_ge(*((vec.sem, 1) if known is None else (vec.sem, DEPTH * known["vec"][0])))
            sp.dma_start(out, xT[:, :, :]).then_inc(out_done, 16)
            sp.wait_ge(out_done, 16)

        @block.gpsimd
        def _(pool):
            pool.dma_start(vec_t[:, :], vecs[0]).then_inc(vec_in, 16)
            pool.dma_start(pos_i.bitcast(mybir.dt.int32), pos).then_inc(pos_in, 16)
            pool.dma_start(arena[:, 2048:2048 + NM], msk_in).then_inc(masks_in, 16)
            pool.dma_start(lo_w[:, :, :], lora[0]).then_inc(lora_in, 16)
            pool.dma_start(wuq, wuq_in[0]).then_inc(uk_in, 16)
            pool.dma_start(wukv, wukv_in[0]).then_inc(uk_in, 16)
            nc.gpsimd.memset(vfirst[:, :, :], 0.0).then_inc(zeros_set, 1)
            nc.gpsimd.memset(zero_b[:, :], 0.0).then_inc(zeros_set, 1)
            loop, L = layers(pool)
            pool.wait_ge(*vec.at(("h lo", 1, KC - 1)))
            settled(pool)
            nc.gpsimd.memset(upad[:, :, 0:HALF], 0.0).then_inc(*poo.mark("pad left"))
            nc.gpsimd.memset(upad[:, :, HALF + S:], 0.0).then_inc(*poo.mark("pad right"))
            for c in range(2, 4):
                pool.wait_ge(*vec.at(("glu", c)))
                if c == 2:
                    pool.wait_ge(vec_in, L * 16 + 16)
                settled(pool)
                for t in range(TAPS):
                    w = vv("cv_w", c * TAPS + t)
                    src = upad[:, c, t:t + S]
                    if t == 0:
                        if c == 2:
                            pool.wait_ge(*poo.at("pad left"))
                            pool.wait_ge(*poo.at("pad right"))
                            settled(pool)
                        nc.gpsimd.tensor_scalar(cvo[:, c, :], src, w, vv("cv_b", c), ALU.mult, ALU.add)\
                            .then_inc(*poo.mark(("conv", c, 0)))
                    else:
                        nc.gpsimd.tensor_scalar(cv_tmp[:, t % 2, :], src, w, None, ALU.mult)\
                            .then_inc(*poo.mark(("tap", c, t)))
                        pool.wait_ge(*poo.at(("tap", c, t)))
                        nc.gpsimd.tensor_tensor(cvo[:, c, :], cvo[:, c, :], cv_tmp[:, t % 2, :], ALU.add)\
                            .then_inc(*poo.mark(("conv", c, t)))
            pool.wait_ge(*ten.at("norm 2"))
            pool.wait_ge(*vec.at(("h", 2, KC - 1)))
            pool.dma_start(vec_t[:, :], vecs[L + 1]).then_inc(vec_in, 16)
            pool.dma_start(lo_w[:, :, :], lora[L + 1]).then_inc(lora_in, 16)
            pool.dma_start(wuq, wuq_in[L + 1]).then_inc(uk_in, 16)
            pool.dma_start(wukv, wukv_in[L + 1]).then_inc(uk_in, 16)
            loop.__exit__(None, None, None)
            pool.wait_ge(vec_in, (DEPTH + 1) * 16)
            pool.wait_ge(lora_in, (DEPTH + 1) * 16)
            pool.wait_ge(uk_in, (DEPTH + 1) * 32)

        @block.tensor
        def _(pe):
            TE = nc.tensor

            def products(o, wh, wl, hi, lo, first, last, **kw):
                TE.matmul(o, wh, hi, start=first, stop=False, **kw)
                TE.matmul(o, wh, lo, start=False, stop=False, **kw)
                return TE.matmul(o, wl, hi, start=False, stop=last, **kw)

            def col_tile(n, slot, o, hi, lo):
                pe.wait_ge(lo_ready, n + 1 + RAW)
                for k in range(KC):
                    last = products(o, whi[:, slot, k * P:(k + 1) * P], wlo[:, slot, k * P:(k + 1) * P],
                                    hi[:, k, :], lo[:, k, :], k == 0, k == KC - 1)
                last.then_inc(tile_used, 1)

            def first_tiles(part, tiles):
                for n, _, _, _ in tiles:
                    pe.wait_ge(lo_ready, n + 1 + RAW)
                for k in range(KC):
                    pe.wait_ge(*vec.at(part(k)))
                    for n, slot, o, clear in tiles:
                        last = products(o, whi[:, slot, k * P:(k + 1) * P], wlo[:, slot, k * P:(k + 1) * P],
                                        h_hi[:, k, :], h_lo[:, k, :], k == 0 and clear, k == KC - 1,
                                        skip_group_check=True)
                        if k == KC - 1:
                            last.then_inc(tile_used, 1)

            def row_tile(n, slot, hi, lo, first):
                pe.wait_ge(lo_ready, n + 1 + RAW)
                for m in range(KC):
                    last = products(bank[m // 2][:, (m % 2) * S:(m % 2 + 1) * S],
                                    whi[:, slot, m * P:(m + 1) * P], wlo[:, slot, m * P:(m + 1) * P],
                                    hi, lo, first and m % 2 == 0, False, skip_group_check=True)
                last.then_inc(tile_used, 1)

            pe.wait_ge(consts_in, 16)
            pe.wait_ge(zeros_set, 2)
            for _ in range(HL):
                TE.matmul(bank[7][:, 0:P], zero_b[0:1, 0:P], zero_b[0:1, 0:P], start=True, stop=True)\
                    .then_inc(tile_used, 1)
            loop, L = layers(pe)

            def norm(i):
                for k in range(KC):
                    if k % 2 == 0:
                        pe.wait_ge(*act.at(("squares", i, k // 2)))
                    m = TE.matmul(bank[NORM_BANK[i]][:, 0:S], cc("ones", P), sq[:, k, :],
                                  start=k == 0, stop=k == KC - 1)
                m.then_inc(*ten.mark(f"norm {i}"))

            def ffn(f, tile0):
                base = (2 * L + f) * NFF
                t0 = L * TILES + tile0

                def up(j, s, n, slot):
                    pe.wait_ge(g_ready, base + j + 1)
                    for half in range(2):
                        col_tile(t0 + n + half, (slot + half) % HL, bank[4 + s][:, half * S:(half + 1) * S],
                                 h_hi, h_lo)

                def down(j, s, n, slot):
                    pe.wait_ge(glo_ready, base + j + 1)
                    row_tile(t0 + n, slot % HL, g_hi[:, s, :], g_lo[:, s, :], False)

                pe.wait_ge(*vec.at(("rstd", 2 * f)))
                for b in range(4):
                    TE.matmul(bank[b][:, :], zero_b[0:1, 0:P], zero_b[0:1, :], start=True, stop=True)
                pe.wait_ge(g_ready, base + 1)
                first_tiles(lambda k: ("h lo", 2 * f, k),
                            [(t0 + e, (tile0 + e) % HL, bank[4][:, e * S:(e + 1) * S], e == 0) for e in range(2)])
                with pe.Fori(0, (NFF - 2) // 2) as it:
                    for q in range(2):
                        n = it * LOOP + (2 + 3 * q)
                        up(it * 2 + (q + 1), (q + 1) % 2, n, tile0 + 2 + 3 * q)
                        down(it * 2 + q, q, n + 2, tile0 + 4 + 3 * q)
                up(NFF - 1, 1, 3 * NFF - 4, tile0 + 3 * NFF - 4)
                down(NFF - 2, 0, 3 * NFF - 2, tile0 + 3 * NFF - 2)
                down(NFF - 1, 1, 3 * NFF - 1, tile0 + 3 * NFF - 1)

            norm(0)
            ffn(0, T_FFN1)
            norm(1)

            first_tiles(lambda k: ("h lo", 1, k),
                        [(L * TILES + T_MLA + e, (T_MLA + e) % HL, bank[e][:, 0:S], True) for e in range(2)])
            for i in range(2, N_MLA):
                n = T_MLA + i
                col_tile(L * TILES + n, n % HL, bank[i][:, 0:S], h_hi, h_lo)

            def tile_pieces(n, o):
                pe.wait_ge(lo_ready, L * TILES + n + 1 + RAW)
                for k in range(KC):
                    last = products(o, whi[:, n % HL, k * P:(k + 1) * P], wlo[:, n % HL, k * P:(k + 1) * P],
                                    h_hi[:, k, :], h_lo[:, k, :], k == 0, k == KC - 1)
                    if k == KC - 1:
                        last.then_inc(tile_used, 1)
                    yield

            def fill_a():
                for n in range(T_CV, T_BR):
                    if n < T_RW:
                        c, e = (n - T_CV) // 2, (n - T_CV) % 2
                        if c >= 2 and e == 0:
                            pe.wait_ge(*vec.at(("glu", c - 2)))
                        yield from tile_pieces(n, bank[6 + c % 2][:, e * S:(e + 1) * S])
                    else:
                        i = n - T_RW
                        if i < 2:
                            pe.wait_ge(*vec.at(("glu", RC - 2 + i)))
                        else:
                            pe.wait_ge(*act.at(("column", n - 2)))
                        yield from tile_pieces(n, bank[6 + i % 2][:, 0:S])

            def branch_pieces(order, b, bank0, nb, hi, lo):
                t0 = T_BR + order * (RC + KC)
                late = order == 2
                for c in range(0, KC, 2):
                    n = t0 + 3 * (c // 2)
                    y, gates = (n + 2, n) if late else (n, n + 1)
                    for e in range(2):
                        back = KC * order + c + e - nb
                        if late:
                            pe.wait_ge(*vec.at(("merge", BRANCH_ORDER[back // KC], back % KC)))
                            yield from tile_pieces(gates + e, bank[bank0 + (c + e) % nb][:, S:2 * S])
                    pe.wait_ge(lo_ready, L * TILES + y + 1 + RAW)
                    for e in range(2):
                        back = KC * order + c + e - nb
                        if back >= 0 and not late:
                            pe.wait_ge(*vec.at(("merge", BRANCH_ORDER[back // KC], back % KC)))
                        for k in range(RC):
                            if late and c + e == 0:
                                pe.wait_ge(*vec.at(("u", b, k)))
                            w = slice((RC * e + k) * P, (RC * e + k + 1) * P)
                            last = products(bank[bank0 + (c + e) % nb][:, 0:S], whi[:, y % HL, w], wlo[:, y % HL, w],
                                            hi[:, k, :], lo[:, k, :], k == 0, k == RC - 1)
                            if e == 1 and k == RC - 1:
                                last.then_inc(tile_used, 1)
                            yield
                    if not late:
                        for e in range(2):
                            yield from tile_pieces(gates + e, bank[bank0 + (c + e) % nb][:, S:2 * S])

            def fill_r():
                pe.wait_ge(*act.at(("column", T_VD - 1)))
                pe.wait_ge(*act.at(("column", T_VD)))
                pe.wait_ge(*vec.at(("u", 2, RC - 1)))
                yield from branch_pieces(0, 2, 6, 2, u_hi, u_lo)
                pe.wait_ge(*vec.at(("u", 1, RC - 1)))
                yield from branch_pieces(1, 1, 6, 2, c_hi, c_lo)

            fa = Filling(FILL_A, fill_a(), 1)
            fr = Filling(FILL_R, fill_r(), 1)

            fa.at("latent squares")
            pe.wait_ge(*act.at("latent squares"))
            for a, b, o in ((0, QC, 0), (QC, QC + KVC, S)):
                for c in range(a, b):
                    m = TE.matmul(bank[0][:, o:o + S], cc("ones", P), sq_lat[:, c, :], start=c == a, stop=c == b - 1)
            m.then_inc(*ten.mark("latent norms"))
            fa.at("latents normed")
            pe.wait_ge(*vec.at("latents normed"))
            pe.wait_ge(uk_in, L * 32 + 32)
            for h in range(H):
                for c in range(KVC):
                    m = TE.matmul(bank[2 + h // 2][0:NOPE, (h % 2) * S:(h % 2 + 1) * S],
                                  wukv[:, c, h * 128:h * 128 + NOPE], lat[:, QC + c, :],
                                  start=c == 0, stop=c == KVC - 1)
                if h % 2:
                    m.then_inc(*ten.mark(("k", h // 2)))
            for h in range(H):
                if h % 2 == 0:
                    pe.wait_ge(*act.at(("k", h // 2)))
                for c in range(QC):
                    m = TE.matmul(bank[2 + h // 2][0:QK, (h % 2) * S:(h % 2 + 1) * S],
                                  wuq[:, c, h * QK:(h + 1) * QK], lat[:, c, :],
                                  start=c == 0, stop=c == QC - 1)
                if h % 2:
                    m.then_inc(*ten.mark(("q", h // 2)))
            wv = wukv.rearrange("p c (h n) -> p c h n", n=128)
            for t in range(NT):
                for c in range(KVC):
                    m = TE.matmul(bank[t][:, :], lat[:, QC + c, t * P:(t + 1) * P],
                                  wv[:, c, :, NOPE:], start=c == 0, stop=c == KVC - 1)
                m.then_inc(*ten.mark(("v", t)))
            fa.at("squares")
            pe.wait_ge(*act.at(("v", NT - 1)))
            pe.wait_ge(*act.at(("q", 3)))
            for w, sq_w, b in (("k", hs, 0), ("q", hs_q, 5)):
                pe.wait_ge(*act.at(f"{w} squares"))
                for h in range(H):
                    m = TE.matmul(bank[b][0:H, 0:S], cc("e96", H, h * H, QK), sq_w[0:QK, h, :],
                                  start=h == 0, stop=h == H - 1)
                m.then_inc(*ten.mark(f"{w} sums"))
            fa.at("inverse")
            for u in range(8):
                w, x_ = ("k", kf) if u % 4 < 2 else ("q", qf)
                if u in (0, 2):
                    pe.wait_ge(*vec.at(f"{w} inverse"))
                if u >= 3:
                    pe.wait_ge(*vec.at(("unit", u - 3)))
                for g in range(2):
                    b, h = QK_BANKS[u % 3][g], 4 * (u % 2) + 2 * g
                    if u < 4:
                        for e in range(2):
                            m = TE.matmul(bank[b][0:QK, e * S:(e + 1) * S], cc("b96", QK, (h + e) * QK, H),
                                          rn8[0:H, u // 2, :], start=True, stop=True)
                    else:
                        m = TE.matmul(bank[b][0:QK, :], cc("rot", QK, 0, QK), x_[0:QK, h:h + 2, :],
                                      start=True, stop=True)
                m.then_inc(*ten.mark(("unit", u)))
                fa.at(("unit", u))
            fa.at("turned")
            pe.wait_ge(*vec.at("q turned"))

            def scores(h):
                if h >= 2:
                    pe.wait_ge(*act.at(("exp", h - 2, 1)))
                for t in range(NT):
                    m = TE.matmul(bank[5 * (h % 2)][:, t * S:(t + 1) * S], qf[0:QK, h, t * P:(t + 1) * P],
                                  kf[0:QK, h, :], start=True, stop=True)
                m.then_inc(*ten.mark(("scores", h)))

            def turn(h):
                pe.wait_ge(*vec.at(("prob", h, 1)))
                if h >= 2:
                    pe.wait_ge(*act.at(("probT", h - 2)))
                for t in range(NT):
                    for b in range(NT):
                        m = TE.transpose(bank[1 + h % 2][:, b * S + t * P:b * S + (t + 1) * P],
                                         prob[:, h % 2, t, b * P:(b + 1) * P], ident)
                m.then_inc(*ten.mark(("probT", h)))

            def mix(h):
                pe.wait_ge(*act.at(("probT", h)))
                if h >= 4 and h % 2 == 0:
                    pe.wait_ge(*vec.at(("u", 2, h // 2 - 2)))
                r = HD * (h % 2)
                for b in range(NT):
                    m = TE.matmul(bank[3 + (h // 2) % 2][r:r + HD, 0:S], vm[:, b, h * HD:(h + 1) * HD],
                                  probT[:, h % 2, b, :], start=b == 0, stop=b == NT - 1)
                m.then_inc(*ten.mark(("attended", h)))

            scores(0)
            for h in range(H):
                if h + 1 < H:
                    scores(h + 1)
                turn(h)
                fa.at(("head", h))
                mix(h)

            pe.wait_ge(*vec.at(("u", 2, RC - 1)))
            fr.at("key sums")
            pe.wait_ge(*act.at("key squares"))
            for j in range(RC):
                m = TE.matmul(bank[4][0:H, 0:S], cc("es", H, j * H), tA[:, j, :], start=j == 0, stop=j == RC - 1)
            m.then_inc(*ten.mark("key sums"))
            fr.at("key inverse")
            pe.wait_ge(*act.at(("column", T_VD)))
            for c in range(RC):
                m = TE.matmul(bank[c // 2][:, (c % 2) * S:(c % 2 + 1) * S], lo_w[0:32, 3, c * P:(c + 1) * P],
                              wag[0:32, 3, :], start=True, stop=True)
            m.then_inc(*ten.mark("nu"))
            pe.wait_ge(*vec.at("key inverse"))
            for j in range(RC):
                m = TE.matmul(bank[2 + j // 2][:, (j % 2) * S:(j % 2 + 1) * S], cc("eb", P, j * P, H),
                              rn_rw[0:H, 0, :], start=True, stop=True)
            m.then_inc(*ten.mark("key spread"))
            fr.at("values")
            pe.wait_ge(*vec.at(("conv", 1, TAPS - 1)))
            pe.wait_ge(*poo.at(("conv", 3, TAPS - 1)))
            pe.wait_ge(*act.at("key rms"))
            for c in range(RC):
                m = TE.matmul(bank[4][:, 0:S], cc("ones", P), cvo[:, c, :], start=c == 0, stop=c == RC - 1)
            m.then_inc(*ten.mark("cv mean"))
            fr.at("cv mean")
            pe.wait_ge(*act.at("cv squares"))
            for c in range(RC):
                m = TE.matmul(bank[5][:, 0:S], cc("ones", P), cv_sq[:, c, :], start=c == 0, stop=c == RC - 1)
            m.then_inc(*ten.mark("cv var"))
            fr.at("cv var")
            pe.wait_ge(*vec.at("values"))
            pe.wait_ge(*act.at("cv rms"))
            for t in range(NT):
                for c in range(RC):
                    m = TE.transpose(bank[4 + t][:, c * P:(c + 1) * P], v_[:, c, t * P:(t + 1) * P], ident)
            m.then_inc(*ten.mark("vt"))

            for d in range(2):
                pe.wait_ge(*act.at("wag"))
                if d == 0:
                    pe.wait_ge(*vec.at("kk"))
                    pe.wait_ge(*act.at("vt"))
                    pe.wait_ge(*act.at("nu"))
                else:
                    pe.wait_ge(*vec.at(("osum", 0)))
                for b0, col in ((0, 0), (2, 1)):
                    for c in range(RC):
                        m = TE.matmul(bank[b0 + c // 2][:, (c % 2) * S:(c % 2 + 1) * S],
                                      lo_w[HD * d:HD * d + HD, col, c * P:(c + 1) * P],
                                      wag[HD * d:HD * d + HD, col, :], start=True, stop=True)
                    m.then_inc(*ten.mark(("lora", d, col)))
                fr.at(("lora", d))
                fr.at(("kr", d))
                pe.wait_ge(*vec.at(("kr", d)))
                pe.wait_ge(*vec.at(("bt", d)))
                pe.wait_ge(*vec.at(("kt", d)))
                if d == 0:
                    pe.wait_ge(*vec.at("kk"))
                pe.wait_ge(*act.at(("icl", d)))
                pe.wait_ge(*act.at(("sw", d)))
                for i in range(3):
                    for t in range(NT):
                        q = i * NT + t
                        for c in range(RC):
                            src = (kr[:, c, t, 0, :], bt[:, c, t * P:(t + 1) * P], kt[:, c, t * P:(t + 1) * P])[i]
                            m = TE.transpose(bank[q][:, c * P:(c + 1) * P], src, ident)
                        m.then_inc(*ten.mark(("tk", d, q)))
                pe.wait_ge(*act.at(("tk", d, 5)))
                for h0 in range(0, H, 2):
                    pair = (h0, h0 + 1)
                    bk = {h: [bank[3 * (h % 2) + i] for i in (0, 1, 2, 0)] for h in pair}
                    fr.at((d, h0, "start"))
                    if h0:
                        for h in pair:
                            pe.wait_ge(*vec.at(("qw", d, h - 2)))
                            pe.wait_ge(*vec.at(("o", d, h - 2)))
                    for h in pair:
                        r, j = HD * (h % 2), h // 2
                        for t in range(NT):
                            TE.matmul(bk[h][0][:, t * S:(t + 1) * S], bt[r:r + HD, j, t * P:(t + 1) * P],
                                      kr[r:r + HD, j, t, :, :], start=True, stop=True)
                        for t in range(NT):
                            TE.matmul(bk[h][1][:, t * S:(t + 1) * S], kt[r:r + HD, j, t * P:(t + 1) * P],
                                      kr[r:r + HD, j, t, :, :], start=True, stop=True)
                        for t in range(NT):
                            m = TE.matmul(bk[h][2][:, t * P:(t + 1) * P], kr[r:r + HD, j, t, 0, :],
                                          bt[r:r + HD, j, t * P:(t + 1) * P], start=True, stop=True)
                        m.then_inc(*ten.mark(("pairs", d, h)))
                    fr.at((d, h0, "pairs"))
                    for lv in range(1, LEVELS):
                        for h in pair:
                            s = h % 2
                            pe.wait_ge(*vec.at(("mn", d, h, lv - 1)))
                            for t in range(NT):
                                m = TE.matmul(bk[h][2][:, t * P:(t + 1) * P], g1[:, s, t, 0, :], mn[:, s, 0, t, :],
                                              start=True, stop=True)
                            m.then_inc(*ten.mark(("z", d, h, lv)))
                        for h in pair:
                            s = h % 2
                            pe.wait_ge(*vec.at(("z", d, h, lv)))
                            for t in range(NT):
                                if lv < LEVELS - 1:
                                    TE.matmul(bk[h][3][:, t * P:(t + 1) * P], mn[:, s, 1, t, :], zz[:, s, t, :],
                                              start=True, stop=True)
                                m = TE.matmul(bk[h][3][:, S + t * P:S + (t + 1) * P], zz[:, s, t, :],
                                              mn[:, s, 1, t, :], start=True, stop=True)
                            m.then_inc(*ten.mark(("mz", d, h, lv)))
                    for h in pair:
                        s = h % 2
                        for t in range(NT):
                            m = TE.matmul(bk[h][2][:, S + t * HD:S + (t + 1) * HD], g2[:, s, t, 0, :],
                                          vt[:, t, h * HD:(h + 1) * HD], start=True, stop=True)
                        m.then_inc(*ten.mark(("gv", d, h)))
                    for h in pair:
                        s = h % 2
                        pe.wait_ge(*vec.at(("mn", d, h, LEVELS - 1)))
                        pe.wait_ge(*act.at(("gv", d, h)))
                        for t in range(NT):
                            TE.matmul(bk[h][3][:, t * HD:(t + 1) * HD], mn[:, s, 1, t, :],
                                      tk[:, 0, t, h * HD:(h + 1) * HD], start=True, stop=True)
                        for t in range(NT):
                            m = TE.matmul(bk[h][3][:, P + t * HD:P + (t + 1) * HD], mn[:, s, 1, t, :],
                                          gv[:, s, t, :], start=True, stop=True)
                        m.then_inc(*ten.mark(("xy", d, h)))
                    fr.at((d, h0, "x"))
                    for h in pair:
                        pe.wait_ge(*act.at(("x", d, h)))
                    for t in range(NT):
                        for h in pair:
                            s, r = h % 2, HD * (h % 2)
                            m = TE.matmul(bk[h][2][r:r + HD, t * P:(t + 1) * P], xs[:, s, t, :], g1[:, s, t, 1, :],
                                          start=True, stop=True)
                            if t == NT - 1:
                                m.then_inc(*ten.mark(("rx", d, h)))
                    for h in pair:
                        pe.wait_ge(*act.at(("y", d, h)))
                    for t in range(NT):
                        for h in pair:
                            s, r = h % 2, HD * (h % 2)
                            TE.matmul(bk[h][0][r:r + HD, t * P:(t + 1) * P], vt[:, t, h * HD:(h + 1) * HD],
                                      g2[:, s, t, 1, :], start=True, stop=False)
                        for h in pair:
                            s, r = h % 2, HD * (h % 2)
                            m = TE.matmul(bk[h][0][r:r + HD, t * P:(t + 1) * P], ys[:, s, t, :], g1[:, s, t, 1, :],
                                          start=False, stop=True)
                            if t == NT - 1:
                                m.then_inc(*ten.mark(("o", d, h)))
                    for half in range(2):
                        q = HD * half
                        if half:
                            for h in pair:
                                pe.wait_ge(*vec.at(("rx", d, h)))
                            settled(pe)
                        for t in range(NT):
                            for h in pair:
                                s, r = h % 2, HD * (h % 2)
                                TE.matmul(bk[h][1 + half][r:r + HD, t * C:(t + 1) * C], xs[q:q + HD, s, t, :],
                                          tk[q:q + HD, 1, t, h * HD:(h + 1) * HD], start=True, stop=True)
                        for t in range(NT):
                            for h in pair:
                                s, r = h % 2, HD * (h % 2)
                                TE.matmul(bk[h][1 + half][r:r + HD, P + t * HD:P + (t + 1) * HD],
                                          tk[q:q + HD, 2, t, h * HD:(h + 1) * HD],
                                          vt[q:q + HD, t, h * HD:(h + 1) * HD], start=True, stop=False)
                            for h in pair:
                                s, r = h % 2, HD * (h % 2)
                                m = TE.matmul(bk[h][1 + half][r:r + HD, P + t * HD:P + (t + 1) * HD],
                                              tk[q:q + HD, 1, t, h * HD:(h + 1) * HD], ys[q:q + HD, s, t, :],
                                              start=False, stop=True)
                                if half and t == NT - 1:
                                    m.then_inc(*ten.mark(("pq", d, h)))
                chunks = range(NCH) if d == 0 else range(NCH - 1, -1, -1)
                fr.at(("state", d, 0))
                pe.wait_ge(*vec.at(("qw", d, H - 1)))
                pe.wait_ge(*vec.at(("o", d, H - 1)))
                pe.wait_ge(*vec.at(("qw", d, H - 2)))
                pe.wait_ge(*vec.at(("o", d, H - 2)))
                for i in (1, 2):
                    c, before = chunks[i], chunks[i - 1]
                    if i == 2:
                        fr.at(("state", d, 1))
                        pe.wait_ge(*vec.at(("state", d, 1, 1)))
                    settled(pe)
                    for h in range(H):
                        r, j = HD * (h % 2), h // 2
                        m = TE.matmul(bank[h % 2][r:r + HD, j * HD:(j + 1) * HD], ptr[r:r + HD, j, c, :],
                                      qw[r:r + HD, j, before, :], start=True, stop=True)
                    m.then_inc(*ten.mark(("state", d, i)))
                fr.at(("state", d, 2))
                pe.wait_ge(*vec.at(("state", d, 2, 1)))
                settled(pe)
                for i in (1, 2, 3):
                    c, before = chunks[i], chunks[i - 1]
                    for h in range(H):
                        r, j = HD * (h % 2), h // 2
                        m = TE.matmul(bank[2 + h % 2 + 2 * (j // 2)][r:r + HD, (j % 2) * S + c * C:(j % 2) * S + (c + 1) * C],
                                      qw[r:r + HD, j, before, :], kr[r:r + HD, j, c // 2, 1, (c % 2) * C:(c % 2 + 1) * C],
                                      start=True, stop=True)
                m.then_inc(*ten.mark(("inter", d)))

            pe.wait_ge(*vec.at(("osum", 1)))
            pe.wait_ge(*vec.at("bonus terms"))
            for b in range(2):
                m = TE.matmul(bank[b][:, :], cc("mean64", P), osum[:, 2 * b:2 * b + 2, :], start=True, stop=True)
            m.then_inc(*ten.mark("gn mean"))
            for b in range(2):
                m = TE.matmul(bank[6 + b][:, :], cc("mean64", P), tA[:, 2 * b:2 * b + 2, :], start=True, stop=True)
            m.then_inc(*ten.mark("bonus"))
            for c in range(RC):
                m = TE.matmul(bank[2 + c // 2][:, (c % 2) * S:(c % 2 + 1) * S], lo_w[:, 2, c * P:(c + 1) * P],
                              wag[:, 2, :], start=True, stop=True)
            m.then_inc(*ten.mark("g"))
            pe.wait_ge(*act.at("gn squares"))
            for j in range(RC):
                m = TE.matmul(bank[4][0:H, 0:S], cc("es", H, j * H), tB[:, j, :], start=j == 0, stop=j == RC - 1)
            m.then_inc(*ten.mark("gn sums"))
            pe.wait_ge(*vec.at("gn inverse"))
            for j in range(RC):
                m = TE.matmul(bank[j // 2][:, (j % 2) * S:(j % 2 + 1) * S], cc("eb", P, j * P, H),
                              rn_rw[0:H, 1, :], start=True, stop=True)
            m.then_inc(*ten.mark("gn spread"))
            for _ in branch_pieces(2, 0, 4, 4, u_hi, u_lo):
                pass

            pe.wait_ge(*act.at(("gate", 0, KC - 1)))
            first_tiles(lambda k: ("m lo", k),
                        [(L * TILES + T_WO + e, (T_WO + e) % HL, bank[4 + e][:, 0:S], True) for e in range(2)])
            for c in range(2, KC):
                if c >= 4:
                    pe.wait_ge(*vec.at(("x mixed", c - 4)))
                n = T_WO + c
                col_tile(L * TILES + n, n % HL, bank[4 + c % 4][:, 0:S], h_hi, h_lo)
            norm(2)
            ffn(1, T_FFN2)
            for n in range(T_END, TILES):
                pe.wait_ge(lo_ready, L * TILES + n + 1 + RAW)
                TE.matmul(bank[7][:, 0:P], zero_b[0:1, 0:P], zero_b[0:1, 0:P], start=True, stop=True)\
                    .then_inc(tile_used, 1)
            loop.__exit__(None, None, None)

        @block.scalar
        def _(sc):
            SE = nc.scalar

            def hi(L, it, m):
                sc.wait_ge(raw_in[m % RAW], (L * (TILES // RAW) + it * (LOOP // RAW) + (m // RAW + 1)) * 16)
                sc.wait_ge(tile_used, L * TILES + it * LOOP + (m + 1))
                SE.copy(whi[:, m % HL, :], raw[:, m % RAW, :]).then_inc(hi_ready, 1)

            for m in range(HL):
                hi(0, 0, m)
            sc.wait_ge(rope_v, ROPE_STEPS)
            SE.activation(sinT[:, :], ang[:, 0, :], ACT.Sin).then_inc(rope_a, 1)
            SE.activation(cosT[:, :], ang[:, 1, :], ACT.Sin).then_inc(rope_a, 1)
            SE.preload_act_table(ACT.Sigmoid)
            loop, L = layers(sc)

            def used(n):
                sc.wait_ge(tile_used, L * TILES + n + 1 + HL)

            def norm(i):
                SE.preload_act_table(ACT.Sqrt)
                for b in range(KC // 2):
                    if i == 0:
                        sc.wait_ge(x_ready, L * 4 + b + 1)
                    elif i == 1:
                        sc.wait_ge(*vec.at(("residual", 0, b)))
                    else:
                        sc.wait_ge(*vec.at(("x mixed", 2 * b + 1)))
                    SE.activation(sq[:, 2 * b:2 * b + 2, :], xT[:, 2 * b:2 * b + 2, :], ACT.Square)\
                        .then_inc(*act.mark(("squares", i, b)))
                sc.wait_ge(*ten.at(f"norm {i}"))
                SE.activation(nrm[:, 0, :], bank[NORM_BANK[i]][:, 0:S], ACT.Sqrt, bias=cc("eps", 1, 0), scale=1.0 / D)\
                    .then_inc(*act.mark(("rms", i)))
                SE.preload_act_table(ACT.Sigmoid)
                for c in range(KC):
                    sc.wait_ge(*vec.at(("h", i, c)))
                    SE.copy(h_hi[:, c, :], sq[:, c, :]).then_inc(*act.mark(("h hi", i, c)))

            def ffn(f, tile0):
                def chunk(it, j, s, m, down):
                    base = (2 * L + f) * NFF
                    hi(L, it, m + HL)
                    sc.wait_ge(tile_used, L * TILES + it * LOOP + (m + 2 + HL))
                    SE.activation(g_s[:, s, :], bank[4 + s][:, 0:S], ACT.Sigmoid).then_inc(sig_ready, 1)
                    hi(L, it, m + 1 + HL)
                    sc.wait_ge(g_ready, base + j + 3)
                    SE.copy(g_hi[:, s, :], g_f[:, s, :]).then_inc(ghi_ready, 1)
                    if down:
                        hi(L, it, m + 2 + HL)

                chunk(0, 0, 0, tile0, False)
                with sc.Fori(0, (NFF - 2) // 2) as it:
                    for q in range(2):
                        chunk(it, it * 2 + (q + 1), (q + 1) % 2, tile0 + 2 + 3 * q, True)
                chunk(0, NFF - 1, 1, tile0 + 3 * NFF - 4, True)
                hi(L, 0, tile0 + 3 * NFF - 1 + HL)

            norm(0)
            ffn(0, T_FFN1)
            norm(1)
            for i in range(N_MLA):
                n = T_MLA + i
                used(n)
                if i < QC + KVC:
                    SE.copy(lat[:, i, :], bank[i][:, 0:S]).then_inc(*act.mark(("column", n)))
                else:
                    SE.copy(rope_in[NOPE:QK, :], bank[i][NOPE:QK, 0:S]).then_inc(*act.mark(("column", n)))
                hi(L, 0, n + HL)

            def fill_a():
                for n in range(T_CV, T_BR):
                    src = bank[6 + (n - T_RW) % 2]
                    used(n)
                    if n < T_RW:
                        if (n - T_CV) % 2:
                            c = (n - T_CV) // 2
                            if c >= 2:
                                sc.wait_ge(*vec.at(("glu", c - 2)))
                            SE.activation(gs[:, c % 2, :], bank[6 + c % 2][:, S:2 * S], ACT.Sigmoid)\
                                .then_inc(*act.mark(("column", n)))
                    elif n < T_VD:
                        i = n - T_RW
                        sc.wait_ge(*(vec.at(("mixed", i // 4 - 1) if i >= 4 else "pp edges")))
                        SE.copy(pp[:, i % 4, 1:S + 1], src[:, 0:S]).then_inc(*act.mark(("column", n)))
                    else:
                        sc.wait_ge(*vec.at(("mixed", 3)))
                        SE.copy(wag[0:32, 3, :], src[0:32, 0:S]).then_inc(*act.mark(("column", n)))
                    hi(L, 0, n + HL)
                    yield

            def branch_tiles(order, b, bank0, nb):
                t0 = T_BR + order * (RC + KC)
                for c in range(0, KC, 2):
                    n = t0 + 3 * (c // 2)
                    hi(L, 0, n + HL)
                    if order == 2:
                        hi(L, 0, n + 1 + HL)
                    yield
                    for e in range(2):
                        back = KC * order + c + e - 2
                        if back >= 0:
                            sc.wait_ge(*vec.at(("merge", BRANCH_ORDER[back // KC], back % KC)))
                        else:
                            sc.wait_ge(*vec.at(("glu", RC + back)))
                        used(n + 2 if order == 2 else n + 1 + e)
                        SE.activation(gs[:, e, :], bank[bank0 + (c + e) % nb][:, S:2 * S], ACT.Sigmoid)\
                            .then_inc(*act.mark(("gate", b, c + e)))
                        if order < 2 or e == 1:
                            hi(L, 0, n + 1 + e + HL)
                        yield

            def fill_r():
                yield from branch_tiles(0, 2, 6, 2)
                yield from branch_tiles(1, 1, 6, 2)

            fa = Filling(FILL_A, fill_a(), PIECES)
            fr = Filling(FILL_R, fill_r(), PIECES)

            sc.wait_ge(*act.at(("column", T_MLA + QC + KVC - 1)))
            SE.activation(sq_lat, lat, ACT.Square).then_inc(*act.mark("latent squares"))
            fa.at("latent squares")
            sc.wait_ge(*ten.at("latent norms"))
            SE.activation(nrm[:, 0, :], bank[0][:, 0:S], ACT.Sqrt, bias=cc("eps", 1, 0), scale=1.0 / QR)
            SE.activation(nrm[:, 1, :], bank[0][:, S:2 * S], ACT.Sqrt, bias=cc("eps", 1, 0), scale=1.0 / KVR)\
                .then_inc(*act.mark("latent rms"))
            fa.at("latents normed")
            for g in range(4):
                sc.wait_ge(*ten.at(("k", g)))
                SE.copy(kf[0:NOPE, 2 * g:2 * g + 2, :], bank[2 + g][0:NOPE, :].rearrange("p (h t) -> p h t", h=2))\
                    .then_inc(*act.mark(("k", g)))
            for g in range(4):
                sc.wait_ge(*ten.at(("q", g)))
                SE.copy(qf[0:QK, 2 * g:2 * g + 2, :], bank[2 + g][0:QK, :].rearrange("p (h t) -> p h t", h=2))\
                    .then_inc(*act.mark(("q", g)))
            for t in range(NT):
                sc.wait_ge(*ten.at(("v", t)))
                SE.copy(vm[:, t, :], bank[t][:, :]).then_inc(*act.mark(("v", t)))
            sc.wait_ge(*vec.at("rope keys"))
            sc.wait_ge(*act.at(("q", 3)))
            SE.activation(hs[0:QK], kf[0:QK], ACT.Square).then_inc(*act.mark("k squares"))
            SE.activation(hs_q[0:QK], qf[0:QK], ACT.Square).then_inc(*act.mark("q squares"))
            fa.at("squares")
            for i, w, b in ((0, "k", 0), (1, "q", 5)):
                sc.wait_ge(*ten.at(f"{w} sums"))
                SE.activation(rn8[0:H, i, :], bank[b][0:H, 0:S], ACT.Sqrt, bias=cc("eps", 1, 0, H), scale=1.0 / QK)\
                    .then_inc(*act.mark(f"{w} rms"))
            fa.at("inverse")
            for u in range(8):
                fa.at(("unit", u))
            fa.at("turned")

            def exps(h):
                sc.wait_ge(*ten.at(("scores", h)))
                sc.wait_ge(*vec.at(("max", h)))
                if h >= 2:
                    sc.wait_ge(*ten.at(("probT", h - 2)))
                for t in range(NT):
                    SE.activation(prob[:, h % 2, t, :], bank[5 * (h % 2)][:, t * S:(t + 1) * S], ACT.Exp,
                                  bias=mx[:, h % 2, t:t + 1], scale=SCALE, accum_out=mx[:, h % 2, 2 + t:3 + t])\
                        .then_inc(*act.mark(("exp", h, t)))

            def u_round(j):
                sc.wait_ge(*ten.at(("attended", 2 * j + 1)))
                SE.copy(u_hi[:, j, :], bank[3 + j % 2][:, 0:S]).then_inc(*act.mark(("u hi", 2, j)))

            exps(0)
            for h in range(H):
                if h >= 2:
                    sc.wait_ge(*ten.at(("attended", h - 2)))
                sc.wait_ge(*ten.at(("probT", h)))
                SE.copy(probT[:, h % 2, :, :], bank[1 + h % 2][:, :].rearrange("p (b t) -> p b t", b=2))\
                    .then_inc(*act.mark(("probT", h)))
                if h + 1 < H:
                    exps(h + 1)
                fa.at(("head", h), 1)
                if h >= 2 and h % 2 == 0:
                    u_round(h // 2 - 1)
            u_round(RC - 1)
            fa.finish()

            sc.wait_ge(*vec.at("key scaled"))
            SE.activation(tA, kk, ACT.Square).then_inc(*act.mark("key squares"))
            SE.preload_act_table(ACT.Sigmoid)
            sc.wait_ge(*vec.at(("mixed", 3)))
            SE.activation(wag[:, 0, :], wag[:, 0, :], ACT.Tanh).then_inc(*act.mark("wag tanh"))
            SE.activation(wag[:, 2, :], wag[:, 2, :], ACT.Sigmoid).then_inc(*act.mark("wag"))
            fr.at("key sums")
            sc.wait_ge(*ten.at("key sums"))
            SE.activation(rn_rw[0:H, 0, :], bank[4][0:H, 0:S], ACT.Sqrt).then_inc(*act.mark("key rms"))
            SE.preload_act_table(ACT.Sigmoid)
            fr.at("key inverse")
            sc.wait_ge(*ten.at("nu"))
            for c in range(RC):
                m = SE.activation(tB[:, c, :], bank[c // 2][:, (c % 2) * S:(c % 2 + 1) * S], ACT.Sigmoid,
                                  bias=vv("v0", c))
            m.then_inc(*act.mark("nu"))
            fr.at("values")
            sc.wait_ge(*ten.at("cv mean"))
            SE.mul(cv_st[:, 0, :], bank[4][:, 0:S], 1.0 / CV).then_inc(*act.mark("cv mean"))
            sc.wait_ge(*vec.at(("cv centred", RC - 1)))
            SE.activation(cv_sq, cvo, ACT.Square).then_inc(*act.mark("cv squares"))
            fr.at("cv mean")
            sc.wait_ge(*ten.at("cv var"))
            SE.activation(cv_st[:, 1, :], bank[5][:, 0:S], ACT.Sqrt, bias=cc("eps", 1, 2), scale=1.0 / CV)\
                .then_inc(*act.mark("cv rms"))
            SE.preload_act_table(ACT.Sigmoid)
            fr.at("cv var")
            sc.wait_ge(*ten.at("vt"))
            for t in range(NT):
                m = SE.copy(vt[:, t, :], bank[4 + t][:, :])
            m.then_inc(*act.mark("vt"))
            for c in range(RC):
                sc.wait_ge(*vec.at(("cv normed", c)))
                SE.activation(cv_sq[:, c, :], cvo[:, c, :], ACT.Sigmoid, bias=vv("ln_b", c))\
                    .then_inc(*act.mark(("cv sigmoid", c)))
            for c in range(RC):
                sc.wait_ge(*vec.at(("cv act", c)))
                SE.copy(c_hi[:, c, :], cvo[:, c, :]).then_inc(*act.mark(("u hi", 1, c)))

            for d in range(2):
                if d:
                    sc.wait_ge(*vec.at(("o", 0, H - 1)))
                    sc.wait_ge(*vec.at(("qw", 0, H - 1)))
                    sc.wait_ge(*ten.at(("pq", 0, H - 1)))
                else:
                    sc.wait_ge(*vec.at("values"))
                    sc.wait_ge(*vec.at("kk"))
                sc.wait_ge(*ten.at(("lora", d, 0)))
                for c in range(RC):
                    m = SE.activation(tA[:, c, :], bank[c // 2][:, (c % 2) * S:(c % 2 + 1) * S], ACT.Sigmoid,
                                      bias=vv("w0", d * RC + c))
                m.then_inc(*act.mark(("sw", d)))
                sc.wait_ge(*ten.at(("lora", d, 1)))
                for c in range(RC):
                    m = SE.activation(tB[:, c, :], bank[2 + c // 2][:, (c % 2) * S:(c % 2 + 1) * S], ACT.Sigmoid,
                                      bias=vv("a0", d * RC + c))
                m.then_inc(*act.mark(("icl", d)))
                SE.preload_act_table(ACT.Exp)
                sc.wait_ge(*vec.at(("before", d)))
                SE.activation(tA, tC_, ACT.Exp, scale=-DECAY).then_inc(*act.mark(("w", d)))
                SE.activation(tD, tD, ACT.Exp, scale=-DECAY).then_inc(*act.mark(("wx", d)))
                sc.wait_ge(*act.at(("w", d)))
                SE.activation(tC_, tC_, ACT.Exp, scale=DECAY).then_inc(*act.mark(("winv", d)))
                SE.preload_act_table(ACT.Sigmoid)
                fr.at(("lora", d))
                fr.at(("kr", d))
                for q in range(6):
                    sc.wait_ge(*ten.at(("tk", d, q)))
                    SE.copy(tk[:, q // NT, q % NT, :], bank[q][:, :]).then_inc(*act.mark(("tk", d, q)))
                for h0 in range(0, H, 2):
                    fr.at((d, h0, "start"))
                    fr.at((d, h0, "pairs"))
                    for h in (h0, h0 + 1):
                        sc.wait_ge(*ten.at(("gv", d, h)))
                        SE.copy(gv[:, h % 2, :, :], bank[3 * (h % 2) + 2][:, S:S + P].rearrange("p (t c) -> p t c", t=NT))\
                            .then_inc(*act.mark(("gv", d, h)))
                    for h in (h0, h0 + 1):
                        b = bank[3 * (h % 2)]
                        sc.wait_ge(*ten.at(("xy", d, h)))
                        SE.copy(xs[:, h % 2, :, :], b[:, 0:P].rearrange("p (t c) -> p t c", t=NT))\
                            .then_inc(*act.mark(("x", d, h)))
                        SE.mul(ys[:, h % 2, :, :], b[:, P:2 * P].rearrange("p (t c) -> p t c", t=NT), -1.0)\
                            .then_inc(*act.mark(("y", d, h)))
                    fr.at((d, h0, "x"))
                for i in range(3):
                    fr.at(("state", d, i))
            sc.wait_ge(*vec.at("gn centred"))
            SE.activation(tB, osum, ACT.Square).then_inc(*act.mark("gn squares"))
            sc.wait_ge(*ten.at("gn sums"))
            SE.activation(rn_rw[0:H, 1, :], bank[4][0:H, 0:S], ACT.Sqrt, bias=cc("eps", 1, 1, H), scale=1.0 / HD)\
                .then_inc(*act.mark("gn rms"))
            used(T_BR + RC + KC - 1)
            for c in range(RC):
                sc.wait_ge(*vec.at(("rw out", c)))
                SE.copy(u_hi[:, c, :], osum[:, c, :]).then_inc(*act.mark(("u hi", 0, c)))
            SE.preload_act_table(ACT.Sigmoid)
            for _ in branch_tiles(2, 0, 4, 4):
                pass
            for c in range(KC):
                sc.wait_ge(*vec.at(("merge", 0, KC - 1)))
                used(T_WO - 1)
                SE.copy(h_hi[:, c, :], merged[:, c, :]).then_inc(*act.mark(("m hi", c)))
            for c in range(KC):
                hi(L, 0, T_WO + c + HL)
            norm(2)
            ffn(1, T_FFN2)
            for n in range(T_END, TILES):
                hi(L, 0, n + HL)
            loop.__exit__(None, None, None)

        @block.vector
        def _(ve):
            V = nc.vector
            TT, TS, STT = V.tensor_tensor, V.tensor_scalar, V.scalar_tensor_tensor

            def lo(L, it, m):
                ve.wait_ge(hi_ready, L * TILES + it * LOOP + (m + 1))
                TT(wlo[:, m % HL, :], raw[:, m % RAW, :], whi[:, m % HL, :].bitcast(F), ALU.subtract)\
                    .then_inc(lo_ready, 1)

            for i in range(RAW):
                V.memset(gs[:, 0, i:i + 1], 0.0).then_inc(lo_ready, 1)
            for i in range(RAW, RAW + 2):
                V.memset(gs[:, 0, i:i + 1], 0.0).then_inc(g_ready, 1)
            ve.wait_ge(pos_in, 16)
            ve.wait_ge(consts_in, 16)
            steps = [0]

            def chain(ins):
                steps[0] += 1
                ins.then_inc(rope_v, 1)
                ve.wait_ge(rope_v, steps[0])

            chain(V.tensor_copy(ang[:, 2, :], pos_i.bitcast(mybir.dt.int32)))
            chain(V.tensor_scalar(ang[:, 0, :], ang[:, 2, :], cc("freq", 1), None, ALU.mult))
            chain(V.tensor_scalar(ang[:, 3, :], ang[:, 0, :], 1.0 / (2 * np.pi), MAGIC, ALU.mult, ALU.add))
            chain(V.tensor_scalar(ang[:, 3, :], ang[:, 3, :], MAGIC, None, ALU.subtract))
            for part in TWO_PI:
                chain(V.tensor_scalar(ang[:, 2, :], ang[:, 3, :], -part, None, ALU.mult))
                chain(V.tensor_tensor(ang[:, 0, :], ang[:, 0, :], ang[:, 2, :], ALU.add))
            chain(V.tensor_scalar(ang[:, 1, :], ang[:, 0, :], float(np.pi / 2), None, ALU.add))
            chain(V.tensor_scalar(ang[:, 3, :], ang[:, 1, :], float(np.pi), float(-2 * np.pi), ALU.is_gt, ALU.mult))
            chain(V.tensor_tensor(ang[:, 1, :], ang[:, 1, :], ang[:, 3, :], ALU.add))
            for i in range(2):
                chain(V.tensor_scalar(ang[:, i, :], ang[:, i, :], PI_IN, -PI_IN, ALU.min, ALU.max))
            assert steps[0] == ROPE_STEPS
            ve.wait_ge(x_in, 16)
            V.memset(gs[:, 0, RAW + 2:RAW + 3], 0.0).then_inc(x_ready, 4)
            ve.wait_ge(masks_in, 16)
            V.tensor_copy(msk[:, :], arena[:, 2048:2048 + NM])
            for m in range(HL):
                lo(0, 0, m)
            loop, L = layers(ve)
            ve.wait_ge(vec_in, L * 16 + 16)
            ve.wait_ge(lora_in, L * 16 + 16)

            def used(n):
                ve.wait_ge(tile_used, L * TILES + n + 1 + HL)

            def h_rest(i, c):
                ve.wait_ge(*act.at(("h hi", i, c)))
                TT(h_lo[:, c, :], sq[:, c, :], h_hi[:, c, :].bitcast(F), ALU.subtract)\
                    .then_inc(*vec.mark(("h lo", i, c)))

            def norm(i):
                gain = ("norm_ffn1", "norm_mix", "norm_ffn2")[i]
                ve.wait_ge(*act.at(("rms", i)))
                V.reciprocal(nrm[:, 1, :], nrm[:, 0, :]).then_inc(*vec.mark(("rstd", i)))
                ve.wait_ge(*vec.at(("rstd", i)))
                for c in range(KC):
                    STT(sq[:, c, :], xT[:, c, :], vv(gain, c), nrm[:, 1, :], ALU.mult, ALU.mult)\
                        .then_inc(*vec.mark(("h", i, c)))
                    if c:
                        h_rest(i, c - 1)
                h_rest(i, KC - 1)

            def ffn(f, tile0):
                def chunk(it, j, s, m, down):
                    base = (2 * L + f) * NFF
                    lo(L, it, m + HL)
                    ve.wait_ge(sig_ready, base + j + 1)
                    TT(g_s[:, s, :], g_s[:, s, :], bank[4 + s][:, 0:S], ALU.mult).then_inc(as_ready, 1)
                    ve.wait_ge(as_ready, base + j + 1)
                    TT(g_f[:, s, :], g_s[:, s, :], bank[4 + s][:, S:2 * S], ALU.mult).then_inc(g_ready, 1)
                    lo(L, it, m + 1 + HL)
                    ve.wait_ge(ghi_ready, base + j + 1)
                    TT(g_lo[:, s, :], g_f[:, s, :], g_hi[:, s, :].bitcast(F), ALU.subtract).then_inc(glo_ready, 1)
                    if down:
                        lo(L, it, m + 2 + HL)

                chunk(0, 0, 0, tile0, False)
                with ve.Fori(0, (NFF - 2) // 2) as it:
                    for q in range(2):
                        chunk(it, it * 2 + (q + 1), (q + 1) % 2, tile0 + 2 + 3 * q, True)
                chunk(0, NFF - 1, 1, tile0 + 3 * NFF - 4, True)
                lo(L, 0, tile0 + 3 * NFF - 1 + HL)
                used(tile0 + 3 * NFF - 1)
                for b in range(4):
                    x2 = xT[:, 2 * b:2 * b + 2, :]
                    m = STT(x2, bank[b][:, :].rearrange("p (c t) -> p c t", c=2), 0.5, x2, ALU.mult, ALU.add)
                    m.then_inc(*vec.mark(("residual", f, b)))
                    if f:
                        V.memset(gs[:, 0, b:b + 1], 0.0).then_inc(x_ready, 1)

            norm(0)
            ffn(0, T_FFN1)
            norm(1)
            for i in range(N_MLA):
                lo(L, 0, T_MLA + i + HL)
            V.memset(pp[:, :, 0:1], 0.0)
            V.memset(pp[:, :, S + 1:S + 2], 0.0).then_inc(*vec.mark("pp edges"))

            def shift_mix(g):
                n = 4 if g < 3 else 3
                dst = (r_, k_, v_, wag)[g]
                ve.wait_ge(*act.at(("column", T_RW + 4 * g + n - 1)))
                ve.wait_ge(*vec.at("pp edges"))
                if g:
                    ve.wait_ge(*vec.at(("mixed", g - 1)))
                TT(pt[:, 0:n, :], pp[:, 0:n, 0:S], pp[:, 0:n, 2:S + 2], ALU.add).then_inc(*vec.mark(("sum", g)))
                ve.wait_ge(*vec.at(("sum", g)))
                STT(pt[:, 0:n, :], pt[:, 0:n, :], 0.5, pp[:, 0:n, 1:S + 1], ALU.mult, ALU.subtract)\
                    .then_inc(*vec.mark(("shift", g)))
                ve.wait_ge(*vec.at(("shift", g)))
                for c in range(n):
                    m = STT(dst[:, c, :], pt[:, c, :], vv("mu", 4 * g + c), pp[:, c, 1:S + 1], ALU.mult, ALU.add)
                m.then_inc(*vec.mark(("mixed", g)))

            def fill_a():
                for n in range(T_CV, T_BR):
                    lo(L, 0, n + HL)
                    if n < T_RW and (n - T_CV) % 2:
                        c = (n - T_CV) // 2
                        ve.wait_ge(*act.at(("column", n)))
                        ve.wait_ge(*poo.at("pad right"))
                        TT(upad[:, c, HALF:HALF + S], gs[:, c % 2, :], bank[6 + c % 2][:, 0:S], ALU.mult)\
                            .then_inc(*vec.mark(("glu", c)))
                    if T_RW <= n < T_VD and ((n - T_RW) % 4 == 3 or n == T_VD - 1):
                        shift_mix((n - T_RW) // 4)
                    yield

            def branch_tiles(order, b, bank0, nb):
                t0 = T_BR + order * (RC + KC)
                for c in range(0, KC, 2):
                    n = t0 + 3 * (c // 2)
                    lo(L, 0, n + HL)
                    if order == 2:
                        lo(L, 0, n + 1 + HL)
                    yield
                    for e in range(2):
                        ve.wait_ge(*act.at(("gate", b, c + e)))
                        y = bank[bank0 + (c + e) % nb][:, 0:S]
                        if order == 0:
                            if c + e == 0:
                                ve.wait_ge(*vec.at(("mixed", 3)))
                            TT(merged[:, c + e, :], gs[:, e, :], y, ALU.mult).then_inc(*vec.mark(("merge", b, c + e)))
                        else:
                            TT(gs[:, e, :], gs[:, e, :], y, ALU.mult).then_inc(*vec.mark(("gated", b, c + e)))
                            ve.wait_ge(*vec.at(("gated", b, c + e)))
                            TT(merged[:, c + e, :], merged[:, c + e, :], gs[:, e, :], ALU.add)\
                                .then_inc(*vec.mark(("merge", b, c + e)))
                        if order < 2 or e == 1:
                            lo(L, 0, n + 1 + e + HL)
                        yield

            def fill_r():
                yield from branch_tiles(0, 2, 6, 2)
                yield from branch_tiles(1, 1, 6, 2)

            fa = Filling(FILL_A, fill_a(), PIECES)
            fr = Filling(FILL_R, fill_r(), PIECES)

            fa.at("latent squares")
            ve.wait_ge(*act.at("latent rms"))
            V.reciprocal(nrm[:, :, :], nrm[:, :, :]).then_inc(*vec.mark("latent inverse"))
            ve.wait_ge(*vec.at("latent inverse"))
            for c in range(QC + KVC):
                q = c < QC
                m = STT(lat[:, c, :], lat[:, c, :], vv("q_norm", c) if q else vv("kv_norm", c - QC),
                        nrm[:, 0 if q else 1, :], ALU.mult, ALU.mult)
            m.then_inc(*vec.mark("latents normed"))
            fa.at("latents normed")
            ve.wait_ge(*act.at(("column", T_CV - 1)))
            V.tensor_copy(kf[NOPE:QK], rope_in[NOPE:QK].unsqueeze(1).broadcast_to([ROPE, H, S]))\
                .then_inc(*vec.mark("rope keys"))
            fa.at("squares")
            for i, w in enumerate("kq"):
                ve.wait_ge(*act.at(f"{w} rms"))
                V.reciprocal(rn8[0:H, i, :], rn8[0:H, i, :]).then_inc(*vec.mark(f"{w} inverse"))
            fa.at("inverse")
            for u in range(8):
                w, x_, part = ("k", kf, hs) if u % 4 < 2 else ("q", qf, hs_q)
                ve.wait_ge(*ten.at(("unit", u)))
                for g in range(2):
                    h = 4 * (u % 2) + 2 * g
                    src = bank[QK_BANKS[u % 3][g]][0:QK, :].rearrange("p (h t) -> p h t", h=2)
                    if u < 4:
                        xg = x_[0:QK, h:h + 2, :]
                        m = STT(xg, xg, vv(f"qk_{w}_g", 0, 0, QK), src, ALU.mult, ALU.mult)
                    else:
                        m = TT(part[0:QK, h:h + 2, :], src, sinT[0:QK].unsqueeze(1).broadcast_to([QK, 2, S]), ALU.mult)
                m.then_inc(*vec.mark(("unit", u)))
                fa.at(("unit", u))
                if u in (5, 7):
                    ve.wait_ge(*vec.at(("unit", u - 2 if u == 7 else 3)))
                    TT(x_[0:QK], x_[0:QK], cosT[0:QK].unsqueeze(1).broadcast_to([QK, H, S]), ALU.mult)\
                        .then_inc(*vec.mark(f"{w} cosine part"))
                    ve.wait_ge(*vec.at(f"{w} cosine part"))
                    TT(x_[0:QK], x_[0:QK], part[0:QK], ALU.add).then_inc(*vec.mark(f"{w} turned"))

            taps = [(c, t) for t in range(TAPS) for c in range(2)]

            def conv(n):
                for c, t in [taps.pop(0) for _ in range(min(n, len(taps)))]:
                    src = upad[:, c, t:t + S]
                    if t == 0:
                        ve.wait_ge(*vec.at(("glu", 3)))
                        m = TS(cvo[:, c, :], src, vv("cv_w", c * TAPS), vv("cv_b", c), ALU.mult, ALU.add)
                    else:
                        ve.wait_ge(*vec.at(("conv", c, t - 1)))
                        m = STT(cvo[:, c, :], src, vv("cv_w", c * TAPS + t), cvo[:, c, :], ALU.mult, ALU.add)
                    m.then_inc(*vec.mark(("conv", c, t)))

            fa.at("turned")

            def head_max(h):
                ve.wait_ge(*ten.at(("scores", h)))
                if h >= 2:
                    ve.wait_ge(*vec.at(("prob", h - 2, 1)))
                V.reduce_max(mx[:, h % 2, 0:2], bank[5 * (h % 2)][:, :].rearrange("p (t k) -> p t k", t=NT), AX.X)\
                    .then_inc(*vec.mark(("rawmax", h)))
                ve.wait_ge(*vec.at(("rawmax", h)))
                TS(mx[:, h % 2, 0:2], mx[:, h % 2, 0:2], -SCALE, None, ALU.mult).then_inc(*vec.mark(("max", h)))

            def u_rest(j):
                ve.wait_ge(*act.at(("u hi", 2, j)))
                TT(u_lo[:, j, :], bank[3 + j % 2][:, 0:S], u_hi[:, j, :].bitcast(F), ALU.subtract)\
                    .then_inc(*vec.mark(("u", 2, j)))

            head_max(0)
            for h in range(H):
                ve.wait_ge(*act.at(("exp", h, 1)))
                V.reciprocal(mx[:, h % 2, 2:4], mx[:, h % 2, 2:4]).then_inc(*vec.mark(("invsum", h)))
                ve.wait_ge(*vec.at(("invsum", h)))
                for t in range(NT):
                    TS(prob[:, h % 2, t, :], prob[:, h % 2, t, :], mx[:, h % 2, 2 + t:3 + t], None, ALU.mult)\
                        .then_inc(*vec.mark(("prob", h, t)))
                if h + 1 < H:
                    head_max(h + 1)
                conv(3)
                fa.at(("head", h), 1)
                if h >= 2 and h % 2 == 0:
                    u_rest(h // 2 - 1)
                conv(3)
            u_rest(RC - 1)
            fa.finish()

            for c in range(RC):
                m = TS(kk[:, c, :], k_[:, c, :], vv("k_k", c), None, ALU.mult)
            m.then_inc(*vec.mark("key scaled"))
            conv(len(taps))
            fr.at("key sums")
            ve.wait_ge(*act.at("key rms"))
            TS(rn_rw[0:H, 0, :], rn_rw[0:H, 0, :], 1e-12, None, ALU.max).then_inc(*vec.mark("key floor"))
            ve.wait_ge(*vec.at("key floor"))
            V.reciprocal(rn_rw[0:H, 0, :], rn_rw[0:H, 0, :]).then_inc(*vec.mark("key inverse"))
            fr.at("key inverse")
            ve.wait_ge(*poo.at(("conv", 3, TAPS - 1)))
            TT(tC_, vfirst[:, :, :], v_, ALU.subtract).then_inc(*vec.mark("v difference"))
            ve.wait_ge(*ten.at("key spread"))
            ve.wait_ge(*vec.at("key scaled"))
            for b in range(2):
                m = TT(kk[:, 2 * b:2 * b + 2, :], kk[:, 2 * b:2 * b + 2, :],
                       bank[2 + b][:, :].rearrange("p (c t) -> p c t", c=2), ALU.mult)
            m.then_inc(*vec.mark("kk"))
            fr.at("values")
            ve.wait_ge(*act.at("cv mean"))
            for c in range(RC):
                TT(cvo[:, c, :], cvo[:, c, :], cv_st[:, 0, :], ALU.subtract).then_inc(*vec.mark(("cv centred", c)))
            ve.wait_ge(*act.at("nu"))
            ve.wait_ge(*vec.at("v difference"))
            TT(tC_, tC_, tB, ALU.mult).then_inc(*vec.mark("v share"))
            ve.wait_ge(*vec.at("v share"))
            STT(v_, tC_, vv("keep"), v_, ALU.mult, ALU.add).then_inc(*vec.mark("values"))
            ve.wait_ge(*vec.at("values"))
            TT(tD, v_, vfirst[:, :, :], ALU.subtract).then_inc(*vec.mark("first difference"))
            ve.wait_ge(*vec.at("first difference"))
            STT(vfirst[:, :, :], tD, vv("first"), vfirst[:, :, :], ALU.mult, ALU.add)\
                .then_inc(*vec.mark("first values"))
            fr.at("cv mean")
            ve.wait_ge(*act.at("cv rms"))
            V.reciprocal(cv_st[:, 2, :], cv_st[:, 1, :]).then_inc(*vec.mark("cv inverse"))
            ve.wait_ge(*vec.at("cv inverse"))
            fr.at("cv var")
            for c in range(RC):
                STT(cvo[:, c, :], cvo[:, c, :], vv("ln_g", c), cv_st[:, 2, :], ALU.mult, ALU.mult)\
                    .then_inc(*vec.mark(("cv normed", c)))
            for c in range(RC):
                ve.wait_ge(*act.at(("cv sigmoid", c)))
                STT(cvo[:, c, :], cvo[:, c, :], vv("ln_b", c), cv_sq[:, c, :], ALU.add, ALU.mult)\
                    .then_inc(*vec.mark(("cv act", c)))
            for c in range(RC):
                ve.wait_ge(*act.at(("u hi", 1, c)))
                TT(c_lo[:, c, :], cvo[:, c, :], c_hi[:, c, :].bitcast(F), ALU.subtract).then_inc(*vec.mark(("u", 1, c)))

            kr_kk = kr[:, :, :, 0, :]
            kr_r = kr[:, :, :, 1, :]
            by_tile = lambda a: a.rearrange("p c (t q) -> p c t q", t=NT)
            for d in range(2):
                ve.wait_ge(*act.at(("sw", d)))
                if d == 0:
                    ve.wait_ge(*vec.at("first values"))
                for c in range(RC):
                    m_, s_, o_ = cc("scan", S, d * S), tA[:, c, :], tC_[:, c, :]
                    if d:
                        m_, s_, o_ = (a[:, ::-1] for a in (m_, s_, o_))
                    m = V.tensor_tensor_scan(o_, m_, s_, 0.0, ALU.mult, ALU.add)
                m.then_inc(*vec.mark(("scan", d)))
                ve.wait_ge(*vec.at(("scan", d)))
                TT(tD, tC_, tA, ALU.subtract).then_inc(*vec.mark(("before", d)))
                ve.wait_ge(*act.at(("w", d)))
                TT(kr_r, by_tile(r_), by_tile(tA), ALU.mult)
                edge = C - 1 if d == 0 else 0
                V.tensor_copy(wch, tA.rearrange("p c (n e) -> p c n e", e=C)[:, :, :, edge]).then_inc(*vec.mark(("wch", d)))
                ve.wait_ge(*act.at(("wx", d)))
                TT(kr_kk, by_tile(kk), by_tile(tD), ALU.mult).then_inc(*vec.mark(("kr", d)))
                fr.at(("lora", d))
                ve.wait_ge(*act.at(("icl", d)))
                TT(bt, kk, tB, ALU.mult).then_inc(*vec.mark(("b", d)))
                ve.wait_ge(*act.at(("winv", d)))
                ve.wait_ge(*vec.at(("b", d)))
                ve.wait_ge(*vec.at(("kr", d)))
                TT(bt, bt, tC_, ALU.mult).then_inc(*vec.mark(("bt", d)))
                for c in range(RC):
                    m = TS(tD[:, c, :], tB[:, c, :], -1.0, vv("k_a", c), ALU.add, ALU.mult)
                m.then_inc(*vec.mark(("ka", d)))
                ve.wait_ge(*vec.at(("ka", d)))
                STT(tD, tD, 1.0, k_, ALU.add, ALU.mult).then_inc(*vec.mark(("kdir", d)))
                ve.wait_ge(*vec.at(("kdir", d)))
                if d == 0:
                    V.tensor_copy(kds, tD).then_inc(*vec.mark("kds 0"))
                else:
                    TT(kds, kds, tD, ALU.add).then_inc(*vec.mark("kds 1"))
                TT(kt, tD, tC_, ALU.mult).then_inc(*vec.mark(("kt", d)))
                fr.at(("kr", d))
                ve.wait_ge(*vec.at(("kt", d)))

                tm = msk[:, d * 2 * P:(d + 1) * 2 * P].rearrange("p (i t) -> p i t", i=2)
                tm = tm.unsqueeze(1).broadcast_to([P, NT, 2, P])
                m1 = msk[:, M1 + d * 2 * P:M1 + (d + 1) * 2 * P].rearrange("p (i t) -> p i t", i=2)
                flat = lambda a: a.rearrange("p t n -> p (t n)")
                for h0 in range(0, H, 2):
                    pair = (h0, h0 + 1)
                    fr.at((d, h0, "start"))
                    for h in pair:
                        s, b = h % 2, 3 * (h % 2)
                        ve.wait_ge(*ten.at(("pairs", d, h)))
                        TT(g1[:, s], bank[b][:, :].rearrange("p (t i n) -> p t i n", t=NT, i=2), tm, ALU.mult)\
                            .then_inc(*vec.mark(("g1", d, h)))
                        TT(mn[:, s, 0], bank[b + 2][:, 0:S].rearrange("p (t n) -> p t n", t=NT),
                           m1[:, 0:1, :].broadcast_to([P, NT, P]), ALU.mult)
                        ve.wait_ge(*vec.at(("g1", d, h)))
                        TT(mn[:, s, 1], g1[:, s, :, 0, :], m1[:, 1:2, :].broadcast_to([P, NT, P]), ALU.mult)\
                            .then_inc(*vec.mark(("m1", d, h)))
                        ve.wait_ge(*vec.at(("m1", d, h)))
                        mn4 = mn[:, s].rearrange("p i t n -> p (i t) n")
                        TT(mn4, mn4, ident.unsqueeze(1).broadcast_to([P, 2 * NT, P]), ALU.add)\
                            .then_inc(*vec.mark(("mn", d, h, 0)))
                    fr.at((d, h0, "pairs"))
                    for lv in range(1, LEVELS):
                        o = LEV + (d * (LEVELS - 1) + lv - 1) * P
                        mask = msk[:, o:o + P].unsqueeze(1).broadcast_to([P, NT, P])
                        for h in pair:
                            s, b = h % 2, 3 * (h % 2)
                            ve.wait_ge(*ten.at(("z", d, h, lv)))
                            TT(zz[:, s], bank[b + 2][:, 0:S].rearrange("p (t n) -> p t n", t=NT), mask, ALU.mult)\
                                .then_inc(*vec.mark(("z", d, h, lv)))
                        if lv == 1:
                            for h in pair:
                                s, b = h % 2, 3 * (h % 2)
                                TT(g2[:, s], bank[b + 1][:, :].rearrange("p (t i n) -> p t i n", t=NT, i=2), tm,
                                   ALU.mult).then_inc(*vec.mark(("g2", d, h)))
                        for h in pair:
                            s, b = h % 2, 3 * (h % 2)
                            ve.wait_ge(*ten.at(("mz", d, h, lv)))
                            if lv < LEVELS - 1:
                                mn4 = mn[:, s].rearrange("p i t n -> p (i t) n")
                                TT(mn4, mn4, bank[b][:, :].rearrange("p (i n) -> p i n", n=P), ALU.subtract)\
                                    .then_inc(*vec.mark(("mn", d, h, lv)))
                            else:
                                TT(mn[:, s, 1], mn[:, s, 1], bank[b][:, S:].rearrange("p (i n) -> p i n", n=P),
                                   ALU.subtract).then_inc(*vec.mark(("mn", d, h, lv)))
                    fr.at((d, h0, "x"))
                    for h in pair:
                        s, b, r, j = h % 2, 3 * (h % 2), HD * (h % 2), h // 2
                        ve.wait_ge(*ten.at(("rx", d, h)))
                        w = kr[r:r + HD, j, :, 1, :]
                        TT(w, w, bank[b + 2][r:r + HD, 0:S].rearrange("p (t n) -> p t n", t=NT), ALU.subtract)\
                            .then_inc(*vec.mark(("rx", d, h)))
                    for h in pair:
                        s, b, r, j = h % 2, 3 * (h % 2), HD * (h % 2), h // 2
                        ve.wait_ge(*ten.at(("o", d, h)))
                        if d == 0:
                            V.tensor_copy(osum[r:r + HD, j, :], bank[b][r:r + HD, 0:S]).then_inc(*vec.mark(("o", d, h)))
                        else:
                            TT(osum[r:r + HD, j, :], osum[r:r + HD, j, :], bank[b][r:r + HD, 0:S], ALU.add)\
                                .then_inc(*vec.mark(("o", d, h)))
                    for h in pair:
                        s, b, r, j = h % 2, 3 * (h % 2), HD * (h % 2), h // 2
                        ve.wait_ge(*ten.at(("pq", d, h)))
                        for half in range(2):
                            pq = bank[b + 1 + half]
                            by2 = lambda a: a[r:r + HD, j].rearrange("p (t e) n -> p e t n", e=2)[:, half]
                            TT(by2(ptr), cc("ident64", C)[r:r + HD].unsqueeze(1).broadcast_to([HD, NT, C]),
                               pq[r:r + HD, 0:P].rearrange("p (t n) -> p t n", t=NT), ALU.subtract)
                            wb = wch[r:r + HD, j].rearrange("p (t e) -> p e t", e=2)[:, half]
                            m = TT(by2(qw), pq[r:r + HD, P:2 * P].rearrange("p (t n) -> p t n", t=NT),
                                   wb.unsqueeze(2).broadcast_to([HD, NT, HD]), ALU.mult)
                        m.then_inc(*vec.mark(("qw", d, h)))
                fr.at(("state", d, 0))
                chunks = range(NCH) if d == 0 else range(NCH - 1, -1, -1)
                for i in (1, 2):
                    c = chunks[i]
                    ve.wait_ge(*ten.at(("state", d, i)))
                    ve.wait_ge(*vec.at(("qw", d, H - 1)))
                    if i == 2:
                        ve.wait_ge(*vec.at(("state", d, 1, 1)))
                    for e in range(2):
                        r = HD * e
                        dst = tmp_s[r:r + HD]
                        TT(dst, bank[e][r:r + HD, 0:S].rearrange("p (j n) -> p j n", j=RC),
                           wch[r:r + HD, :, c].unsqueeze(2).broadcast_to([HD, RC, HD]), ALU.mult)\
                            .then_inc(*vec.mark(("decayed", d, i, e)))
                    for e in range(2):
                        r = HD * e
                        ve.wait_ge(*vec.at(("decayed", d, i, e)))
                        TT(qw[r:r + HD, :, c, :], qw[r:r + HD, :, c, :], tmp_s[r:r + HD], ALU.add)\
                            .then_inc(*vec.mark(("state", d, i, e)))
                    fr.at(("state", d, i))
                ve.wait_ge(*ten.at(("inter", d)))
                ve.wait_ge(*vec.at(("o", d, H - 1)))
                a, z = (C, S) if d == 0 else (0, S - C)
                for e in range(2):
                    for g in range(2):
                        r = HD * e
                        o = osum[r:r + HD, 2 * g:2 * g + 2, a:z]
                        m = TT(o, o, bank[2 + e + 2 * g][r:r + HD, :].rearrange("p (j t) -> p j t", j=2)[:, :, a:z],
                               ALU.add)
                m.then_inc(*vec.mark(("osum", d)))

            for c in range(RC):
                m = STT(tA[:, c, :], kds[:, c, :], vv("r_k", c), r_[:, c, :], ALU.mult, ALU.mult)
            m.then_inc(*vec.mark("bonus terms"))
            ve.wait_ge(*ten.at("gn mean"))
            ve.wait_ge(*vec.at(("osum", 1)))
            for b in range(2):
                o = osum[:, 2 * b:2 * b + 2, :]
                m = TT(o, o, bank[b][:, :].rearrange("p (c t) -> p c t", c=2), ALU.subtract)
            m.then_inc(*vec.mark("gn centred"))
            ve.wait_ge(*ten.at("bonus"))
            for b in range(2):
                m = STT(tC_[:, 2 * b:2 * b + 2, :], bank[6 + b][:, :].rearrange("p (c t) -> p c t", c=2), 0.5 * HD,
                        v_[:, 2 * b:2 * b + 2, :], ALU.mult, ALU.mult)
            m.then_inc(*vec.mark("bonus"))
            ve.wait_ge(*act.at("gn rms"))
            V.reciprocal(rn_rw[0:H, 1, :], rn_rw[0:H, 1, :]).then_inc(*vec.mark("gn inverse"))
            ve.wait_ge(*ten.at("gn spread"))
            ve.wait_ge(*vec.at("bonus"))
            ve.wait_ge(*vec.at("gn centred"))
            half_bank = lambda b0, c: bank[b0 + c // 2][:, (c % 2) * S:(c % 2 + 1) * S]
            for i in range(RC + 3):
                if i < RC:
                    c = i
                    STT(osum[:, c, :], osum[:, c, :], vv("gn_g", c), half_bank(0, c), ALU.mult, ALU.mult)\
                        .then_inc(*vec.mark(("gn normed", c)))
                if 0 <= i - 1 < RC:
                    c = i - 1
                    ve.wait_ge(*vec.at(("gn normed", c)))
                    STT(osum[:, c, :], osum[:, c, :], vv("gn_b", c), tC_[:, c, :], ALU.add, ALU.add)\
                        .then_inc(*vec.mark(("gn bonus", c)))
                if 0 <= i - 2 < RC:
                    c = i - 2
                    if c == 0:
                        ve.wait_ge(*ten.at("g"))
                    ve.wait_ge(*vec.at(("gn bonus", c)))
                    TT(osum[:, c, :], osum[:, c, :], half_bank(2, c), ALU.mult).then_inc(*vec.mark(("rw out", c)))
                if i >= 3:
                    c = i - 3
                    ve.wait_ge(*act.at(("u hi", 0, c)))
                    ve.wait_ge(*vec.at(("rw out", c)))
                    TT(u_lo[:, c, :], osum[:, c, :], u_hi[:, c, :].bitcast(F), ALU.subtract)\
                        .then_inc(*vec.mark(("u", 0, c)))
            for _ in branch_tiles(2, 0, 4, 4):
                pass
            for c in range(KC):
                ve.wait_ge(*act.at(("m hi", c)))
                ve.wait_ge(*vec.at(("merge", 0, KC - 1)))
                TT(h_lo[:, c, :], merged[:, c, :], h_hi[:, c, :].bitcast(F), ALU.subtract)\
                    .then_inc(*vec.mark(("m lo", c)))
            for c in range(KC):
                used(T_WO + c)
                TT(xT[:, c, :], xT[:, c, :], bank[4 + c % 4][:, 0:S], ALU.add).then_inc(*vec.mark(("x mixed", c)))
                lo(L, 0, T_WO + c + HL)
            norm(2)
            ffn(1, T_FFN2)
            ve.wait_ge(*vec.at(("residual", 1, 3)))
            for n in range(T_END, TILES):
                lo(L, 0, n + HL)
            loop.__exit__(None, None, None)

    return {s.name: s.counted() for s in (vec, act, ten, poo)}


def laid_out(inputs):
    a = {n: np.ascontiguousarray(v) for n, v in inputs.items()}
    f = np.float32

    def col(w, c0):
        return w[:, c0:c0 + P].reshape(-1, P, P).transpose(1, 0, 2).reshape(P, -1)

    stream = np.zeros((DEPTH * TILES + HL, P, D), f)
    vecs = np.zeros((DEPTH + 1, P, NV), f)
    lora = np.zeros((DEPTH + 1, P, 4 * RW), f)
    wuq = np.zeros((DEPTH + 1, P, QC * H * QK), f)
    wukv = np.zeros((DEPTH + 1, P, KVC * H * 128), f)
    for l in range(DEPTH):
        r = max(l - 1, 0)
        T = stream[l * TILES:(l + 1) * TILES]
        for f_, t0 in (("ffn1", T_FFN1), ("ffn2", T_FFN2)):
            w1, w3, w2 = (a[f"{f_}_{w}"][l] for w in ("w1", "w3", "w2"))
            for j in range(NFF):
                up = t0 + (0 if j == 0 else 3 * j - 1)
                T[up], T[up + 1] = col(w1, j * P), col(w3, j * P)
                T[t0 + min(3 * j + 4, 3 * NFF - 2 + (j == NFF - 1))] = w2[j * P:(j + 1) * P]
        w_in = a["w_in"][l]
        for i in range(N_RW):
            T[T_RW + i] = col(w_in, i * P)
        vd = np.zeros((D, P), f)
        vd[:, :32] = a["rw_v_down"][r]
        T[T_VD] = col(vd, 0)
        m0 = RW_COLS + CV_COLS
        for i in range(QC + KVC):
            T[T_MLA + i] = col(w_in, m0 + i * P)
        T[T_MLA + QC + KVC] = col(w_in, m0 + QR + KVR - NOPE)
        for c in range(RC):
            T[T_CV + 2 * c] = col(w_in, RW_COLS + c * P)
            T[T_CV + 2 * c + 1] = col(w_in, RW_COLS + CV + c * P)
        for order, b in enumerate(BRANCH_ORDER):
            t0 = T_BR + order * (RC + KC)
            w = a[("rw_w_branch", "cv_w_branch", "mla_w_branch")[b]][l]
            for c in range(0, KC, 2):
                n = t0 + 3 * (c // 2)
                y, gates = (n + 2, n) if order == 2 else (n, n + 1)
                T[y] = np.concatenate([col(w, c * P), col(w, (c + 1) * P)], 1)
                for e in range(2):
                    T[gates + e] = col(w_in, m0 + MLA_COLS + b * D + (c + e) * P)
        for c in range(KC):
            T[T_WO + c] = col(a["w_o"][l], c * P)

        def put(name, v, at=0):
            v = v.reshape(-1, P).T if v.size % P == 0 else np.pad(v, (0, P - v.size))[:, None]
            vecs[l, :, VEC[name] + at:VEC[name] + at + v.shape[1]] = v

        for name in ("norm_ffn1", "norm_mix", "norm_ffn2"):
            put(name, a[name][l])
        put("mu", a["rw_mu"][l])
        for d in range(2):
            put("w0", a["rw_w0"][l, d], d * RC)
            put("a0", a["rw_a0"][l, d], d * RC)
            lora[l, d * HD:(d + 1) * HD, 0:RW] = a["rw_w_up"][l, d]
            lora[l, d * HD:(d + 1) * HD, RW:2 * RW] = a["rw_a_up"][l, d]
        for name, src in (("k_k", "rw_k_k"), ("k_a", "rw_k_a"), ("gn_g", "rw_gn_g"), ("gn_b", "rw_gn_b"),
                          ("cv_b", "cv_dw_b"), ("ln_g", "cv_ln_g"), ("ln_b", "cv_ln_b"), ("q_norm", "mla_q_norm"),
                          ("kv_norm", "mla_kv_norm"), ("qk_q_g", "mla_qk_q_g"), ("qk_k_g", "mla_qk_k_g")):
            put(name, a[src][l])
        put("r_k", a["rw_r_k"][l].reshape(-1))
        put("v0", a["rw_v0"][r])
        vecs[l, :, VEC["cv_w"]:VEC["cv_w"] + RC * TAPS] = \
            a["cv_dw_w"][l].reshape(TAPS, RC, P).transpose(2, 1, 0).reshape(P, -1)
        vecs[l, :, VEC["keep"]] = float(l > 0)
        vecs[l, :, VEC["first"]] = float(l == 0)
        lora[l, :, 2 * RW:3 * RW] = a["rw_g_up"][l]
        lora[l, :32, 3 * RW:] = a["rw_v_up"][r]
        wuq[l] = a["mla_w_uq"][l].reshape(QC, P, -1).transpose(1, 0, 2).reshape(P, -1)
        wukv[l] = a["mla_w_ukv"][l].reshape(KVC, P, -1).transpose(1, 0, 2).reshape(P, -1)
    x = np.ascontiguousarray(a["x"][0].T.reshape(KC, P, S).transpose(1, 0, 2))
    pos = np.ascontiguousarray(np.broadcast_to(a["positions"][0], (P, S)))
    c, m = constants()
    return {"x": x, "pos": pos, "stream": stream, "vecs": vecs, "cst": c, "msk": m, "lora": lora,
            "wuq": wuq, "wukv": wukv}


def kernel(**inputs):
    import concourse.bacc as bacc
    from concourse.bass_utils import run_bass_kernel_spmd

    arrays = laid_out(inputs)

    def build(known):
        nc = bacc.Bacc("TRN2", target_bir_lowering=False, num_devices=1)
        args = [nc.dram_tensor(f"in_{n}", v.shape, mybir.dt.from_np(v.dtype), kind="ExternalInput").ap()
                for n, v in arrays.items()]
        out = nc.dram_tensor("out", (P, KC, S), F, kind="ExternalOutput").ap()
        return nc, program(nc, *args, out, known)

    _, known = build(None)
    nc, _ = build(known)
    r = run_bass_kernel_spmd(nc, [{f"in_{n}": v for n, v in arrays.items()}], core_ids=[0])
    y = r.results[0]["out"]
    return np.ascontiguousarray(y.transpose(2, 1, 0).reshape(1, S, D))
```
